# Optimizing a Trainium2 kernel written in Bass

```python
import math
import jax, jax.numpy as jnp
from jax import lax
import numpy as np

D_MODEL = 1024
BATCH = 1
SEQ = 512
DEPTH = 1
DEC_BATCH = 1
DEC_SEQ = 64
PAST_LEN = 512

CHUNK = 64
HEAD_DIM = 64
A_HEADS = 8
A_BAND = 8
A_WIDTH = A_HEADS * HEAD_DIM
REL_CLIP = 128
B_HEADS = D_MODEL // (2 * HEAD_DIM)
B_QK_WIDTH = B_HEADS * 2 * HEAD_DIM
B_V_WIDTH = B_HEADS * 2 * HEAD_DIM
IN_WIDTH = 3 * A_WIDTH + 2 * B_QK_WIDTH + B_V_WIDTH
IN_SPLITS = (A_WIDTH, 2 * A_WIDTH, 3 * A_WIDTH, 3 * A_WIDTH + B_QK_WIDTH, 3 * A_WIDTH + 2 * B_QK_WIDTH)
D_FF = 4 * D_MODEL
PLE_DIM = 256
Q_BLOCK = 128
NORM_EPS = 1e-6
MASK_VALUE = -1e30

kernel_name = "streaming_hybrid_chunkband_diffattn"

def rms_norm(x, g):
    x32 = x.astype(jnp.float32)
    y = x32 * lax.rsqrt(jnp.mean(x32 * x32, axis=-1, keepdims=True) + NORM_EPS)
    return (y * g.astype(jnp.float32)).astype(x.dtype)

def alibi_slopes(n):
    return jnp.asarray(2.0 ** (-8.0 * np.arange(1, n + 1) / n), dtype=jnp.float32)

def lambda_init(layer):
    return 0.8 - 0.6 * math.exp(-0.3 * layer)

def band_mask(q_pos, k_pos):
    qc = q_pos[:, :, None] // CHUNK
    kc = k_pos[:, None, :] // CHUNK
    return (k_pos[:, None, :] >= 0) & (kc <= qc) & (kc >= qc - A_BAND)

def band_attention(q, k, v, q_pos, k_pos, rel_table):
    s = jnp.einsum('bnqhd,bnkhd->bnhqk', q, k).astype(jnp.float32) * (HEAD_DIM ** -0.5)
    rel = jnp.clip(q_pos[:, :, None] - k_pos[:, None, :], -REL_CLIP, REL_CLIP) + REL_CLIP
    bias = jnp.moveaxis(rel_table.astype(jnp.float32)[:, rel], 0, 1)
    s = jnp.where(band_mask(q_pos, k_pos)[None, :, None], s + bias[None], MASK_VALUE)
    p = jax.nn.softmax(s, axis=-1).astype(v.dtype)
    return jnp.einsum('bnhqk,bnkhd->bnqhd', p, v)

def mixer_a_prompt(qa, ka, va, rel_table):
    b, s = qa.shape[:2]
    n = s // CHUNK

    def chunks(t):
        return t.reshape(b, n, CHUNK, A_HEADS, HEAD_DIM)

    def band(t):
        tp = jnp.pad(chunks(t), ((0, 0), (A_BAND, 0), (0, 0), (0, 0), (0, 0)))
        return jnp.concatenate([tp[:, j:j + n] for j in range(A_BAND + 1)], axis=2)

    c = jnp.arange(n)[:, None]
    i = jnp.arange(CHUNK)[None, :]
    q_pos = c * CHUNK + i
    k_pos = jnp.concatenate([(c - A_BAND + j) * CHUNK + i for j in range(A_BAND + 1)], axis=1)
    o = band_attention(chunks(qa), band(ka), band(va), q_pos, k_pos, rel_table)
    return o.reshape(b, s, A_WIDTH)

def mixer_a_sample(qa, ka, va, cache_k, cache_v, past, rel_table):
    b, t = qa.shape[:2]
    w = cache_k.shape[1]
    k = jnp.concatenate([cache_k, ka], axis=1)[:, None]
    v = jnp.concatenate([cache_v, va], axis=1)[:, None]
    q_pos = (past + jnp.arange(t))[None]
    k_pos = jnp.concatenate([past - w + jnp.arange(w), past + jnp.arange(t)])[None]
    o = band_attention(qa[:, None], k, v, q_pos, k_pos, rel_table)
    return o.reshape(b, t, A_WIDTH)

def diff_attention(q, k, v, q_pos, k_pos, lam, lam0, sub_g):
    s = jnp.einsum('bqhcd,bkhcd->bhcqk', q, k).astype(jnp.float32) * (HEAD_DIM ** -0.5)
    dist = jnp.abs(q_pos[:, None] - k_pos[None, :]).astype(jnp.float32)
    s = s - alibi_slopes(B_HEADS)[:, None, None, None] * dist
    valid = (k_pos[None, :] // CHUNK) <= (q_pos[:, None] // CHUNK)
    p = jax.nn.softmax(jnp.where(valid, s, MASK_VALUE), axis=-1)
    a = (p[:, :, 0] - lam * p[:, :, 1]).astype(v.dtype)
    o = jnp.einsum('bhqk,bkhe->bqhe', a, v)
    o = rms_norm(o, sub_g) * (1.0 - lam0)
    return o.reshape(o.shape[0], o.shape[1], B_V_WIDTH)

def mixer_b_prompt(qb, kb, vb, lam, lam0, sub_g):
    b, s = qb.shape[:2]
    nb = s // Q_BLOCK
    pos = jnp.arange(s)
    q_blocks = jnp.moveaxis(qb.reshape(b, nb, Q_BLOCK, B_HEADS, 2, HEAD_DIM), 1, 0)
    p_blocks = pos.reshape(nb, Q_BLOCK)
    out = lax.map(lambda a: diff_attention(a[0], kb, vb, a[1], pos, lam, lam0, sub_g), (q_blocks, p_blocks))
    return jnp.moveaxis(out, 0, 1).reshape(b, s, B_V_WIDTH)

def split_projection(u, w):
    b, t = u.shape[:2]
    qa, ka, va, qb, kb, vb = jnp.split(u @ w, IN_SPLITS, axis=-1)
    head_a = (b, t, A_HEADS, HEAD_DIM)
    head_b = (b, t, B_HEADS, 2, HEAD_DIM)
    return (qa.reshape(head_a), ka.reshape(head_a), va.reshape(head_a),
            qb.reshape(head_b), kb.reshape(head_b), vb.reshape(b, t, B_HEADS, 2 * HEAD_DIM))

def setup_inputs(seed: int = 0) -> dict:
    key = jax.random.key(seed)
    ks = jax.random.split(key, 32)
    a_win = min(A_BAND * CHUNK, PAST_LEN)
    nrm = lambda k, shape, scale: jax.random.normal(k, shape, jnp.float32) * scale
    gain = lambda k, shape: 1.0 + 0.01 * jax.random.normal(k, shape, jnp.float32)
    return {
        "x_prompt": nrm(ks[0], (BATCH, SEQ, D_MODEL), 1.0),
        "x_sample": nrm(ks[1], (DEC_BATCH, DEC_SEQ, D_MODEL), 1.0),
        "cache_a_k": nrm(ks[2], (DEPTH, DEC_BATCH, a_win, A_HEADS, HEAD_DIM), 1.0),
        "cache_a_v": nrm(ks[3], (DEPTH, DEC_BATCH, a_win, A_HEADS, HEAD_DIM), 1.0),
        "cache_b_k": nrm(ks[4], (DEPTH, DEC_BATCH, PAST_LEN, B_HEADS, 2, HEAD_DIM), 1.0),
        "cache_b_v": nrm(ks[5], (DEPTH, DEC_BATCH, PAST_LEN, B_HEADS, 2 * HEAD_DIM), 1.0),
        "p_prompt": nrm(ks[6], (DEPTH, BATCH, SEQ, PLE_DIM), 1.0),
        "p_sample": nrm(ks[7], (DEPTH, DEC_BATCH, DEC_SEQ, PLE_DIM), 1.0),
        "w_in": nrm(ks[8], (DEPTH, D_MODEL, IN_WIDTH), D_MODEL ** -0.5),
        "rel_bias": nrm(ks[9], (DEPTH, A_HEADS, 2 * REL_CLIP + 1), 0.1),
        "diff_lambda": nrm(ks[10], (DEPTH, 4, HEAD_DIM), 0.1),
        "diff_subln": gain(ks[11], (DEPTH, 2 * HEAD_DIM)),
        "w_gate": nrm(ks[12], (DEPTH, D_MODEL, 2 * D_MODEL), D_MODEL ** -0.5),
        "w_branch_a": nrm(ks[13], (DEPTH, A_WIDTH, D_MODEL), A_WIDTH ** -0.5),
        "w_branch_b": nrm(ks[14], (DEPTH, B_V_WIDTH, D_MODEL), B_V_WIDTH ** -0.5),
        "w_out": nrm(ks[15], (DEPTH, D_MODEL, D_MODEL), D_MODEL ** -0.5),
        "g_mix_pre": gain(ks[16], (DEPTH, D_MODEL)),
        "g_mix_post": gain(ks[17], (DEPTH, D_MODEL)),
        "g_ffn_pre": gain(ks[18], (DEPTH, D_MODEL)),
        "g_ffn_post": gain(ks[19], (DEPTH, D_MODEL)),
        "w_up": nrm(ks[20], (DEPTH, D_MODEL, D_FF), D_MODEL ** -0.5),
        "w_down": nrm(ks[21], (DEPTH, D_FF, D_MODEL), D_FF ** -0.5),
        "w_ple": nrm(ks[22], (DEPTH, PLE_DIM, D_MODEL), PLE_DIM ** -0.5),
        "g_ple": gain(ks[23], (DEPTH, D_MODEL)),
        "w_ple_gate": nrm(ks[24], (DEPTH, D_MODEL, D_MODEL), D_MODEL ** -0.5),
    }

def reference(x_prompt, x_sample, cache_a_k, cache_a_v, cache_b_k, cache_b_v, p_prompt, p_sample,
              w_in, rel_bias, diff_lambda, diff_subln, w_gate, w_branch_a, w_branch_b, w_out,
              g_mix_pre, g_mix_post, g_ffn_pre, g_ffn_post, w_up, w_down, w_ple, g_ple, w_ple_gate):
    past = cache_b_k.shape[2]

    def layer(i, h, ple, cache):
        u = rms_norm(h, g_mix_pre[i])
        qa, ka, va, qb, kb, vb = split_projection(u, w_in[i])
        lq = diff_lambda[i].astype(jnp.float32)
        lam0 = lambda_init(i)
        lam = jnp.exp(jnp.sum(lq[0] * lq[1])) - jnp.exp(jnp.sum(lq[2] * lq[3])) + lam0
        if cache is None:
            oa = mixer_a_prompt(qa, ka, va, rel_bias[i])
            ob = mixer_b_prompt(qb, kb, vb, lam, lam0, diff_subln[i])
            keep = min(A_BAND * CHUNK, h.shape[1])
            new = (ka[:, h.shape[1] - keep:], va[:, h.shape[1] - keep:], kb, vb)
        else:
            ca_k, ca_v, cb_k, cb_v = cache
            oa = mixer_a_sample(qa, ka, va, ca_k, ca_v, past, rel_bias[i])
            t = h.shape[1]
            ob = diff_attention(qb, jnp.concatenate([cb_k, kb], axis=1), jnp.concatenate([cb_v, vb], axis=1),
                                past + jnp.arange(t), jnp.arange(past + t), lam, lam0, diff_subln[i])
            new = (ka, va, kb, vb)
        g_a, g_b = jnp.split(jax.nn.sigmoid(u @ w_gate[i]), 2, axis=-1)
        mix = (g_a * (oa @ w_branch_a[i]) + g_b * (ob @ w_branch_b[i])) @ w_out[i]
        h = h + rms_norm(mix, g_mix_post[i])
        f = jnp.square(jax.nn.relu(rms_norm(h, g_ffn_pre[i]) @ w_up[i])) @ w_down[i]
        h = h + rms_norm(f, g_ffn_post[i])
        h = h + jax.nn.sigmoid(h @ w_ple_gate[i]) * rms_norm(ple @ w_ple[i], g_ple[i])
        return h, new

    hp, hs = x_prompt, x_sample
    ak_p, av_p, bk_p, bv_p = [], [], [], []
    ak_s, av_s, bk_s, bv_s = [], [], [], []
    for i in range(DEPTH):
        hp, (a1, a2, a3, a4) = layer(i, hp, p_prompt[i], None)
        hs, (s1, s2, s3, s4) = layer(i, hs, p_sample[i], (cache_a_k[i], cache_a_v[i], cache_b_k[i], cache_b_v[i]))
        ak_p.append(a1); av_p.append(a2); bk_p.append(a3); bv_p.append(a4)
        ak_s.append(s1); av_s.append(s2); bk_s.append(s3); bv_s.append(s4)
    return (hp, hs, jnp.stack(ak_p), jnp.stack(av_p), jnp.stack(bk_p), jnp.stack(bv_p),
            jnp.stack(ak_s), jnp.stack(av_s), jnp.stack(bk_s), jnp.stack(bv_s))


_drawn_inputs = setup_inputs


def setup_inputs(seed=0):
    import zlib

    import numpy as np

    out = dict(_drawn_inputs(seed))
    spreads = {}
    factors = {'rel_bias': 5.884,
     'diff_subln': 41.666,
     'g_mix_pre': 4.543,
     'g_mix_post': 114.045,
     'g_ffn_pre': 176.754,
     'g_ffn_post': 200.0,
     'g_ple': 200.0,
     'cache_a_k': 8.0,
     'cache_a_v': 8.0,
     'cache_b_k': 8.0,
     'cache_b_v': 8.0}
    for name, (base, spread) in spreads.items():
        noise = np.random.default_rng([zlib.crc32(name.encode()), seed]).standard_normal(out[name].shape)
        drawn = base * np.exp(spread * noise) if base else spread * noise
        out[name] = __import__('jax').numpy.asarray(drawn.astype(out[name].dtype))
    for name, factor in factors.items():
        out[name] = (out[name] * factor).astype(out[name].dtype)
    return out
```

```python
from contextlib import ExitStack

import concourse.bass as bass
from concourse import mybir

F32, F32R, I32 = mybir.dt.float32, mybir.dt.float32r, mybir.dt.int32
ALU, ACT, AX = mybir.AluOpType, mybir.ActivationFunctionType, mybir.AxisListType

P = 128
EPS = 1e-6
LAM0 = 0.2
MASK = -1e30
RING = 4
PIECE = 512

A_STEPS = [("S", 0, 1), ("V4", 0, 1), ("S", 1, 1), ("K4", 0, 1), ("T", (0, 0), 1), ("T", (0, 1), 1),
           ("OT", 0, 1), ("AV", 0, 1), ("S", 2, 0), ("Tail", 0, 1), ("T", (1, 0), 1), ("T", (1, 1), 1),
           ("CK", 0, 1), ("AV", 1, 1), ("S", 3, 0), ("T", (2, 0), 1), ("T", (2, 1), 1), ("AV", 2, 1),
           ("Sa", 4, 1), ("T", (3, 0), 1), ("Sb", 4, 1), ("T", (3, 1), 1), ("AV", 3, 1),
           ("T", (4, 0), 1), ("T", (4, 1), 1), ("AV", 4, 1)]
B_STEPS = [("S", 0, 1), ("V4", 0, 1), ("K4", 0, 1), ("C", 0, 0), ("S", 1, 2), ("OT", 0, 1),
           ("T", (0, 0), 1), ("AV", 0, 1), ("C", 1, 0), ("S", 2, 1), ("Tail", 0, 1), ("T", (1, 0), 1),
           ("AV", 1, 1), ("C", 2, 0), ("CK", 0, 1), ("S", 3, 1), ("T", (2, 0), 1), ("AV", 2, 1),
           ("C", 3, 0), ("Sa", 4, 1), ("T", (3, 0), 1), ("Sb", 4, 1), ("AV", 3, 1), ("C", 4, 0),
           ("T", (4, 0), 3), ("AV", 4, 1)]


def walk(steps, with_projections, with_outputs):
    k, turn = 0, 0
    for name, arg, before in steps:
        for _ in range(before if with_projections else 0):
            yield "k", k, None
            k += 1
        if name == "OT" and not with_outputs:
            continue
        if name in ("V4", "K4", "T", "OT", "Tail", "CK"):
            yield name, arg, turn
            turn += 1
        else:
            yield name, arg, None


class Count:

    def __init__(self, const, terms=()):
        self.const, self.terms = const, tuple(terms)

    def __add__(self, n):
        if isinstance(n, Count):
            return Count(self.const + n.const, self.terms + n.terms)
        return Count(self.const + n, self.terms)

    def __mul__(self, n):
        return Count(self.const * n, [(r, f * n) for r, f in self.terms])

    def over(self, n):
        assert all(f % n == 0 for _, f in self.terms)
        return Count(self.const // n, [(r, f // n) for r, f in self.terms])

    def mod(self, n):
        assert all(f % n == 0 for _, f in self.terms)
        return self.const % n

    def value(self):
        v = self.const
        for register, factor in self.terms:
            v = register * factor + v
        return v


def at_least(eng, sem, count):
    v = count.value()
    if not isinstance(v, int) or v > 0:
        eng.wait_ge(sem, v)


def at_least_alone(eng, sem, count):
    at_least(eng, sem, count)
    if count.terms:
        eng.nop(nofuse=True)


def encoder_layer(nc, x_prompt, x_sample, cache_a_k, cache_a_v, cache_b_k, cache_b_v, p_prompt, p_sample,
                  w_in, rel_bias_reversed, diff_lambda, diff_subln, w_gate, w_branch_a, w_branch_b, w_out,
                  g_mix_pre, g_mix_post, g_ffn_pre, g_ffn_post, w_up, w_down, w_ple, g_ple, w_ple_gate,
                  y_prompt, y_sample, ak_p, av_p, bk_p, bv_p, ak_s, av_s, bk_s, bv_s):
    SEQ, D = x_prompt.shape[1:]
    SMP = x_sample.shape[1]
    T = SEQ + SMP
    HALF = T // 2
    QB = SEQ // P + 1
    KB = D // P
    AW = cache_a_k.shape[3] * cache_a_k.shape[4]
    NA = AW // P
    NB = cache_b_k.shape[3]
    NU = NA + NB
    FF = w_up.shape[2]
    FG = FF // D
    REL = rel_bias_reversed.shape[2] // 2
    TW = SEQ + P
    assert T == 576 and NA == 4 and NB == 8 and REL == P and cache_a_k.shape[2] == SEQ

    xp, xs_d = x_prompt[0], x_sample[0]
    cak, cav = [c[0, 0].rearrange("t h d -> t (h d)") for c in (cache_a_k, cache_a_v)]
    cbk, cbv = cache_b_k[0, 0].rearrange("t h c d -> t (h c d)"), cache_b_v[0, 0].rearrange("t h d -> t (h d)")
    out_a = [o[0, 0].rearrange("t h d -> t (h d)") for o in (ak_p, av_p, ak_s, av_s)]
    out_b = [bk_p[0, 0].rearrange("t h c d -> t (h c d)"), bv_p[0, 0].rearrange("t h d -> t (h d)"),
             bk_s[0, 0].rearrange("t h c d -> t (h c d)"), bv_s[0, 0].rearrange("t h d -> t (h d)")]
    rev = rel_bias_reversed[0]
    BW = P + 2 * REL
    band = nc.dram_tensor("band_bias", [2 * NA, P, BW], F32, kind="Internal").ap()

    PC_GATE = 6 * NU
    PC_BRA = PC_GATE + 2 * 2 * KB
    PC_BRB = PC_BRA + KB
    PC_PLE = PC_BRB + 2 * KB
    PC_OUT = PC_PLE + KB // 2
    PC_FF = PC_OUT + 2 * KB
    PC_PG = PC_FF + FG * 4 * KB
    PC_END = PC_PG + 2 * KB
    PJ_IN = KB
    PJ_GATE = PJ_IN + 3 * NU
    PJ_BRA = PJ_GATE + 2 * KB
    PJ_BRB = PJ_BRA + KB
    PJ_PLE = PJ_BRB + KB
    PJ_OUT = PJ_PLE + KB
    PJ_FF = PJ_OUT + KB
    PJ_PG = PJ_FF + FG * 2 * KB
    A_TURNS, B_TURNS = 15, 10
    TURN_B = A_TURNS * NA - 1
    TURN_END = TURN_B + B_TURNS * NB

    with ExitStack() as ctx:
        def sb(name, shape, dt=F32, stack=ctx):
            return stack.enter_context(nc.sbuf_tensor(name, shape, dt))

        def sem(name):
            return ctx.enter_context(nc.semaphore(name))

        ident, ones = sb("ident", [P, P]), sb("ones", [P, P])
        gcol = sb("gcol", [P, 48])
        G_PRE, G_POST, G_FPRE, G_FPOST, G_PLE, G_SUB, G_SUBL = 0, 8, 16, 24, 32, 40, 41
        eps_t, neg_half, neg_lam = sb("eps", [P, 1]), sb("neg_half", [P, QB]), sb("neg_lam", [P, 1])
        act_hi, act_lo = sb("act_hi", [P, KB, T], F32R), sb("act_lo", [P, KB, T], F32R)
        w_raw = sb("w_raw", [P, RING, PIECE])
        w_hi, w_lo = sb("w_hi", [P, RING, PIECE], F32R), sb("w_lo", [P, RING, PIECE], F32R)
        hT = sb("hT", [P, KB, T])
        small = sb("small", [P, 64])
        ss_x, sq_x, r_x = small[:, 0:5], small[:, 8:13], small[:, 16:21]
        with ExitStack() as start:
            x_tm = sb("x_tm", [P, QB, D], F32, start)
            x_scaled = sb("x_scaled", [P, QB, D], F32, start)
            gain_rows = sb("gain_rows", [41, P], F32, start)
            lam_in = sb("lam_in", [P, 4, 64], F32, start)
            lam_pr = sb("lam_pr", [P, 2, 64], F32, start)
            lam_s = sb("lam_s", [P, 4], F32, start)
            dist_i = sb("dist_i", [P, TW], I32, start)
            dist = sb("dist", [P, TW], F32, start)
            band_sb = sb("band_sb", [2 * NA, BW], F32, start)
        mid_hi, mid_lo = sb("mid_hi", [P, NB, T], F32R), sb("mid_lo", [P, NB, T], F32R)
        with ExitStack() as branch_a:
            oa_hi, oa_lo = sb("oa_hi", [P, NA, T], F32R, branch_a), sb("oa_lo", [P, NA, T], F32R, branch_a)
            with ExitStack() as att:
                qT = [sb(f"qT{b}", [P, T], F32, att) for b in range(2)]
                kT = [sb(f"kT{b}", [P, T], F32, att) for b in range(2)]
                vT = [sb(f"vT{b}", [P, T], F32, att) for b in range(2)]
                k_tm, v_tm = sb("k_tm", [P, QB, P], F32, att), sb("v_tm", [P, QB, P], F32, att)
                ck, cv, ckT = (sb(n, [P, SEQ], F32, att) for n in ("ck", "cv", "ckT"))
                tab_a = [sb(f"tab_a{b}", [P, 2, TW], F32, att) for b in range(2)]
                tab_b = [sb(f"tab_b{b}", [P, TW], F32, att) for b in range(2)]
                prob = [[sb(f"prob{b}{m}", [P, T], F32, att) for m in range(2)] for b in range(2)]
                probT = [sb(f"probT{m}", [P, SEQ], F32, att) for m in range(2)]
                neg_max = sb("neg_max", [P, 2, 2], F32, att)
                sums, r_sum = sb("sums", [P, 2, 2], F32, att), sb("r_sum", [P, 2, 2], F32, att)
                c_map = sb("c_map", [P, 2], F32, att)
                o_tm = [sb(f"o_tm{b}", [P, QB, P], F32, att) for b in range(2)]
                o_sq = sb("o_sq", [P, QB, P], F32, att)
                o_ms = sb("o_ms", [P, 2, QB], F32, att)
                o_r = sb("o_r", [P, QB], F32, att)
            wide = sb("wide", [P, 2 * KB, T], F32, branch_a)
            down_sum, mixed = wide[:, 0:KB], wide[:, KB:2 * KB]
            sq = [sb(f"sq{b}", [P, T], F32, branch_a) for b in range(2)]
            sq_sum = sb("sq_sum", [P, QB * P], F32, branch_a)
            diag = sb("diag", [P, QB, P], F32, branch_a)
            ms_t, r_t = sb("ms_t", [P, QB], F32, branch_a), sb("r_t", [P, QB], F32, branch_a)
            with ExitStack() as ple_in:
                p_tm = sb("p_tm", [P, QB, 2 * P], F32, ple_in)
                pT_hi, pT_lo = sb("pT_hi", [P, 2, T], F32R, ple_in), sb("pT_lo", [P, 2, T], F32R, ple_in)
            r_row = sb("r_row", [P, T], F32, branch_a)
            up_t, up_a = sb("up_t", [P, T], F32, branch_a), sb("up_a", [P, T], F32, branch_a)
            y_f = [sb(f"y_f{b}", [P, T], F32, branch_a) for b in range(2)]
            y_tm = [sb(f"y_tm{b}", [P, QB, P], F32, branch_a) for b in range(2)]
        ple = sb("ple", [P, KB, T])
        assert KB == 2 * NA

        proj = [ctx.enter_context(nc.psum_tensor(f"proj{b}", [P, 1024], F32)) for b in range(2)]
        score = ctx.enter_context(nc.psum_tensor("score", [P, 1024], F32))
        turn_out = ctx.enter_context(nc.psum_tensor("turn_out", [P, 1024], F32))
        turn, outp = turn_out[:, 0:512], turn_out[:, 512:1024]
        pair = [score, turn_out]
        acc = [p[:, :].rearrange("p (h n) -> p h n", h=2)[:, :, 0:HALF] for p in proj]

        def halves(ap):
            return ap.rearrange("p (h n) -> p h n", h=2)

        w_loaded = [sem(f"w_loaded{s}") for s in range(RING)]
        hi_done, lo_done = sem("hi_done"), sem("lo_done")
        w_used = sem("w_used")
        proj_free = [sem(f"proj_free{b}") for b in range(2)]
        x_loaded = [sem(f"x_loaded{t}") for t in range(QB)]
        rows_loaded, lam_loaded, rel_loaded = sem("rows_loaded"), sem("lam_loaded"), sem("rel_loaded")
        band_made = sem("band_made")
        band_kept = [sem("band_kept_first"), sem("band_kept_others")]
        consts, dist_made = sem("consts"), sem("dist_made")
        vec = sem("vec")
        act_own, pool_own = sem("act_own"), sem("pool_own")
        rows_turned, gains_ready = sem("rows_turned"), sem("gains_ready")
        lam_ready, lam_exped = sem("lam_ready"), sem("lam_exped")
        x_squared, x_rooted, x_ready = sem("x_squared"), sem("x_rooted"), sem("x_ready")
        u_turned, u_hi = sem("u_turned"), sem("u_hi")
        x_turned, x_kept = sem("x_turned"), sem("x_kept")
        tab_loaded = [sem(f"tab_loaded{b}") for b in range(2)]
        tab_ready = sem("tab_ready")
        ck_loaded, cv_loaded, kv_stored = sem("ck_loaded"), sem("cv_loaded"), sem("kv_stored")
        scored, biased, exped, combined = sem("scored"), sem("biased"), sem("exped"), sem("combined")
        turned, turn_free = sem("turned"), sem("turn_free")
        tail_copied, o_hi = sem("tail_copied"), sem("o_hi")
        av_done, out_free = sem("av_done"), sem("out_free")
        o_summed, o_rooted, o_normed = sem("o_summed"), sem("o_rooted"), sem("o_normed")
        br_mixed, m_hi, m_split = sem("br_mixed"), sem("m_hi"), sem("m_split")
        sq_cleared, squared, sq_added = sem("sq_cleared"), sem("squared"), sem("sq_added")
        sum_turned, ms_ready, r_ready = sem("sum_turned"), sem("ms_ready"), sem("r_ready")
        diag_ready, row_ready, row_read = sem("diag_ready"), sem("row_ready"), sem("row_read")
        h_updated, h_hi, h_split = sem("h_updated"), sem("h_hi"), sem("h_split")
        down_cleared, up_ready, up_hi, up_split = (sem(n) for n in ("down_cleared", "up_ready", "up_hi", "up_split"))
        p_loaded, p_turned, p_hi, p_split = sem("p_loaded"), sem("p_turned"), sem("p_hi"), sem("p_split")
        ple_first = sem("ple_first")
        y_ready, y_turned, y_copied = sem("y_ready"), sem("y_turned"), sem("y_copied")
        y_stored = [sem(f"y_stored{b}") for b in range(2)]

        block = ctx.enter_context(nc.Block())

        def rows(i):
            return P if i < QB - 1 else SMP

        def keys(i):
            return P * (i + 1) if i < QB - 1 else T

        def n_key_blocks(i):
            return min(i + 1, QB)

        def out_block(x, u, kind, cols):
            n = u if kind == "A" else u + (-NA)
            return x[:, bass.ds(n.value(), 1), cols].rearrange("p a n -> p (a n)")

        def block_of(x, n):
            return x[:, bass.ds(n.value(), 1)].rearrange("p a n -> p (a n)")

        def turn_base(u, kind):
            if kind == "A":
                return u * A_TURNS + (-1) if u.const else u
            return (u + (-NA)) * B_TURNS + TURN_B

        @block.sync
        def _(sp):
            def piece(p, src, shaped=None):
                slot = p.mod(RING)
                at_least(sp, lo_done, p + (1 - RING))
                dst = w_raw[:, slot].rearrange("p (k n) -> p k n", n=shaped or P)
                sp.dma_start(dst, src).then_inc(w_loaded[slot], 16)

            def k_half(w, kh, col, n=P, kblocks=4, row0=0):
                return w[bass.ds(row0 + kh * 512, P * kblocks), bass.ds(col, n)].rearrange(
                    "(k p) n -> p k n", p=P)

            for t in range(QB - 1):
                sp.dma_start(x_tm[:, t], xp[P * t:P * t + P]).then_inc(x_loaded[t], 16)
            sp.dma_start(x_tm[0:SMP, QB - 1], xs_d).then_inc(x_loaded[QB - 1], 16)
            for g, at in ((g_mix_pre, 0), (g_mix_post, 8), (g_ffn_pre, 16), (g_ffn_post, 24), (g_ple, 32)):
                sp.dma_start(gain_rows[at:at + 8], g[0].rearrange("(k p) -> k p", p=P)).then_inc(rows_loaded, 16)
            sp.dma_start(gain_rows[40:41], diff_subln).then_inc(rows_loaded, 16)
            sp.dma_start(band_sb[:, P:BW], rev[:, 0:2 * REL]).then_inc(rel_loaded, 16)

            def unit_pieces(u0, u, cols):
                for n, base in enumerate(cols):
                    for kh in range(2):
                        piece(u * 6 + (2 * n + kh), k_half(w_in[0], kh, ((u + (-u0)) * P + base).value()))

            a_cols = (2 * AW, AW, 0)
            b_cols = (3 * AW + 2 * NB * P, 3 * AW + NB * P, 3 * AW)
            unit_pieces(0, Count(0), a_cols)
            sp.dma_start(lam_in[:, :, :], bass.AP(diff_lambda.tensor, 0, [[0, P], [64, 4], [1, 64]])).then_inc(lam_loaded, 16)
            sp.wait_ge(band_made, 1)
            for u in range(NA):
                sp.dma_start(band[2 * u:2 * u + 2], band_sb[2 * u:2 * u + 2].unsqueeze(1).broadcast_to([2, P, BW])
                             ).then_inc(band_kept[min(u, 1)], 16)
            with sp.Fori(0, (NA - 2) // 2) as it:
                for v in range(2):
                    unit_pieces(0, Count(1 + v, [(it, 2)]), a_cols)
            unit_pieces(0, Count(NA - 1), a_cols)
            with sp.Fori(0, NB // 2) as it:
                for v in range(2):
                    unit_pieces(NA, Count(NA + v, [(it, 2)]), b_cols)

            def stage(p0, w, n, kblocks=4, halves_=2):
                per = RING // halves_
                with sp.Fori(0, n // per) as it:
                    for j in range(per):
                        for kh in range(halves_):
                            piece(Count(p0 + j * halves_ + kh, [(it, RING)]),
                                  k_half(w, kh, Count(P * j, [(it, P * per)]).value()))

            stage(PC_GATE, w_gate[0], 2 * KB)
            sp.wait_ge(av_done, NU * QB)
            sp.dma_start(p_tm[:, 0:QB - 1], p_prompt[0, 0].rearrange("(j p) n -> p j n", p=P)).then_inc(p_loaded, 16)
            sp.dma_start(p_tm[0:SMP, QB - 1], p_sample[0, 0]).then_inc(p_loaded, 16)
            stage(PC_BRA, w_branch_a[0], KB, halves_=1)
            stage(PC_BRB, w_branch_b[0], KB)
            for n in range(KB // 2):
                piece(Count(PC_PLE + n), k_half(w_ple[0], 0, 2 * P * n, n=2 * P, kblocks=2), shaped=2 * P)
            stage(PC_OUT, w_out[0], KB)
            with sp.Fori(0, FG) as g:
                with sp.Fori(0, KB // 2) as it:
                    for j in range(2):
                        for kh in range(2):
                            piece(Count(PC_FF + 2 * j + kh, [(g, 4 * KB), (it, RING)]),
                                  k_half(w_up[0], kh, Count(P * j, [(g, D), (it, 2 * P)]).value()))
                with sp.Fori(0, KB // 2) as it:
                    for j in range(2):
                        for kh in range(2):
                            piece(Count(PC_FF + 2 * KB + 2 * j + kh, [(g, 4 * KB), (it, RING)]),
                                  k_half(w_down[0], kh, Count(P * j, [(it, 2 * P)]).value(),
                                         row0=Count(0, [(g, D)]).value()))
            stage(PC_PG, w_ple_gate[0], KB)
            for m in range(KB):
                sp.wait_ge(y_copied, m + 1)
                yt, cols = y_tm[m % 2], slice(P * m, P * m + P)
                sp.dma_start(y_prompt[0, :, cols].rearrange("(j p) n -> p j n", p=P),
                             yt[:, 0:QB - 1]).then_inc(y_stored[m % 2], 16)
                sp.dma_start(y_sample[0, :, cols], yt[0:SMP, QB - 1]).then_inc(y_stored[m % 2], 16)
            for b in range(2):
                sp.wait_ge(y_stored[b], 32 * KB // 2)
            sp.wait_ge(kv_stored, 64 * NU)

        @block.gpsimd
        def _(pool):
            def lo_part(p):
                slot = p.mod(RING)
                at_least(pool, hi_done, p + 1)
                pool.tensor_tensor(w_lo[:, slot], w_raw[:, slot], w_hi[:, slot].bitcast(F32),
                                   ALU.subtract).then_inc(lo_done, 1)

            def load_table(u):
                src = bass.AP(band.tensor, 2 * u * P * BW + P, [[BW - 1, P], [P * BW, 2], [1, 2 * REL]])
                pool.dma_start(tab_a[u % 2][:, :, TW - 2 * REL:TW], src).then_inc(tab_loaded[u % 2], 16)

            def finish_table(u):
                pool.wait_ge(tab_loaded[u % 2], 16 * (u // 2 + 1))
                tab, flat = tab_a[u % 2], TW - 2 * REL
                pool.tensor_copy(tab[:, :, 0:flat], tab[:, :, flat:flat + 1].broadcast_to([P, 2, flat])).then_inc(pool_own, 1)
                pool.wait_ge(pool_own, u + 2)
                pool.memset(tab[0:SMP, :, TW - SMP:TW], MASK).then_inc(tab_ready, 1)

            pool.memset(ident[:, :], 0.0).then_inc(pool_own, 1)
            pool.memset(ones[:, :], 1.0)
            pool.memset(eps_t[:, :], EPS)
            pool.memset(neg_half[:, :], -0.5)
            pool.iota(dist_i[:, :], [[-1, TW]], base=SEQ, channel_multiplier=1).then_inc(dist_made, 1)
            pool.wait_ge(pool_own, 1)
            pool.affine_select(out=ident[:, :], in_=ident[:, :], compare_op=ALU.not_equal, fill=1.0,
                               base=0, pattern=[[-1, P]], channel_multiplier=1).then_inc(consts, 1)
            for p in range(RING):
                lo_part(Count(p))
            pool.dma_start(ck[:, :].rearrange("p (j n) -> p j n", n=P), cak[:, 0:P].rearrange("(j p) n -> p j n", p=P)).then_inc(ck_loaded, 16)
            pool.dma_start(cv[:, :].rearrange("p (j n) -> p j n", n=P), cav[:, 0:P].rearrange("(j p) n -> p j n", p=P)).then_inc(cv_loaded, 16)
            for u in range(2):
                pool.wait_ge(band_kept[u], (1, NA - 1)[u] * 16)
                load_table(u)
            for u in range(2):
                finish_table(u)
            for n in range(6):
                lo_part(Count(RING + n))

            def unit(u, kind, next_kind, par, projections, prev):
                steps = A_STEPS if kind == "A" else B_STEPS
                turns = turn_base(u, kind)
                cols = ((u + (0 if kind == "A" else -NA)) * P).value()
                outs = out_a if kind == "A" else out_b
                for name, arg, t in walk(steps, projections, prev is not None):
                    if name == "k" and arg % 4 == 3:
                        lo_part((u + 1) * 6 + (arg // 4 + RING))
                    elif name == "V4" and prev == "B":
                        at_least(pool, o_summed, u + (-NA))
                        pool.tensor_tensor(o_r[:, :], o_ms[:, 1 - par], neg_half[:, :], ALU.pow).then_inc(o_rooted, 1)
                    elif name == "Tail":
                        at_least_alone(pool, turn_free, turns + (t + 1))
                        for src, dst_p, dst_s in ((k_tm, outs[0], outs[2]), (v_tm, outs[1], outs[3])):
                            pool.dma_start(dst_p[:, bass.ds(cols, P)].rearrange("(j p) n -> p j n", p=P),
                                           src[:, 0:QB - 1]).then_inc(kv_stored, 16)
                            pool.dma_start(dst_s[:, bass.ds(cols, P)], src[0:SMP, QB - 1]).then_inc(kv_stored, 16)
                    elif name == "CK" and next_kind:
                        at_least_alone(pool, turned, turns + (t + 1))
                        c = cak if next_kind == "A" else cbk
                        col = ((u + (1 if next_kind == "A" else 1 - NA)) * P).value()
                        pool.dma_start(ck[:, :].rearrange("p (j n) -> p j n", n=P),
                                       c[:, bass.ds(col, P)].rearrange("(j p) n -> p j n", p=P)).then_inc(ck_loaded, 16)
                if next_kind:
                    at_least_alone(pool, av_done, (u + 1) * QB)
                    c = cav if next_kind == "A" else cbv
                    col = ((u + (1 if next_kind == "A" else 1 - NA)) * P).value()
                    pool.dma_start(cv[:, :].rearrange("p (j n) -> p j n", n=P),
                                   c[:, bass.ds(col, P)].rearrange("(j p) n -> p j n", p=P)).then_inc(cv_loaded, 16)

            for u in range(NA):
                if u >= 1 and u + 1 < NA:
                    finish_table(u + 1)
                unit(Count(u), "A", "A" if u + 1 < NA else "B", u % 2, True, "A" if u else None)
                if u + 2 < NA:
                    pool.wait_ge(biased, 10 * (u + 1))
                    load_table(u + 2)

            def b_unit(u, par, next_kind="B", projections=True, prev="B"):
                if next_kind:
                    at_least(pool, tab_ready, u)
                    at_least_alone(pool, biased, u * 10)
                    pool.tensor_scalar(tab_b[1 - par][:, :], tab_b[par][:, :], 0.5, None, ALU.mult).then_inc(tab_ready, 1)
                unit(u, "B", next_kind, par, projections, prev)

            b_unit(Count(NA), 0, prev="A")
            b_unit(Count(NA + 1), 1)
            with pool.Fori(0, (NB - 4) // 2) as it:
                for v in range(2):
                    b_unit(Count(NA + 2 + v, [(it, 2)]), v)
            b_unit(Count(NU - 2), 0)
            b_unit(Count(NU - 1), 1, next_kind=None, projections=False)
            pool.wait_ge(o_summed, NB)
            pool.tensor_tensor(o_r[:, :], o_ms[:, 1], neg_half[:, :], ALU.pow).then_inc(o_rooted, 1)

            def root(n):
                pool.wait_ge(ms_ready, n + 1)
                pool.tensor_tensor(r_t[:, :], ms_t[:, :], neg_half[:, :], ALU.pow).then_inc(r_ready, 1)

            def split(p0, end):
                if end - p0 == RING:
                    for j in range(RING):
                        lo_part(Count(p0 + j))
                else:
                    with pool.Fori(0, (end - p0) // RING) as it:
                        for j in range(RING):
                            lo_part(Count(p0 + j, [(it, RING)]))

            split(PC_GATE + RING, PC_OUT)
            split(PC_OUT, PC_OUT + 2 * RING)
            root(0)
            split(PC_OUT + 2 * RING, PC_FF + RING)
            pool.wait_ge(m_hi, KB)
            pool.wait_ge(proj_free[(PJ_PLE + 1) % 2], (PJ_PLE + 1) // 2)
            pool.memset(down_sum, 0.0).then_inc(down_cleared, 1)
            root(1)
            root(2)
            split(PC_FF + RING, PC_PG + RING)
            root(3)
            split(PC_PG + RING, PC_END)

        @block.scalar
        def _(act):
            def hi_part(p):
                slot = p.mod(RING)
                at_least(act, w_loaded[slot], (p.over(RING) + 1) * 16)
                at_least(act, w_used, p + (1 - RING))
                act.activation(w_hi[:, slot], w_raw[:, slot], ACT.Copy).then_inc(hi_done, 1)

            def square(t):
                act.wait_ge(x_loaded[t], 16)
                n = rows(t)
                act.activation(x_scaled[0:n, t], x_tm[0:n, t], ACT.Square, accum_out=ss_x[0:n, t:t + 1]).then_inc(x_squared, 1)

            def root_x(t):
                act.wait_ge(x_squared, t + 1)
                if t == 0:
                    act.wait_ge(consts, 1)
                n = rows(t)
                act.activation(sq_x[0:n, t:t + 1], ss_x[0:n, t:t + 1], ACT.Sqrt, scale=1.0 / D,
                               bias=eps_t[0:n, :]).then_inc(x_rooted, 1)

            square(0)
            for t in range(1, QB):
                square(t)
                root_x(t - 1)
            root_x(QB - 1)
            for p in range(RING):
                hi_part(Count(p))
            for k in range(KB):
                act.wait_ge(u_turned, k + 1)
                if k == 0:
                    act.wait_ge(gains_ready, 1)
                act.activation(act_hi[:, k], proj[k % 2][:, 0:T], ACT.Copy, scale=gcol[:, G_PRE + k:G_PRE + k + 1]).then_inc(u_hi, 1)
            act.wait_ge(lam_ready, 1)
            act.activation(lam_s[:, 2:4], lam_s[:, 0:2], ACT.Exp).then_inc(lam_exped, 1)
            for k in range(24):
                if k % 4 == 3:
                    hi_part(Count(RING + k // 4))
                if k % 3 == 2:
                    j = k // 3
                    act.wait_ge(x_turned, j + 1)
                    act.activation(hT[:, j], pair[j % 2][:, 0:T], ACT.Copy).then_inc(x_kept, 1)

            def unit(u, kind, par, projections, prev):
                steps = A_STEPS if kind == "A" else B_STEPS
                turns = turn_base(u, kind)

                def expo(i, m):
                    n, np_, b = keys(i), rows(i), i % 2
                    at_least(act, biased, u * 10 + (2 * i + m + 1))
                    act.activation(prob[b][m][0:np_, 0:n], prob[b][m][0:np_, 0:n], ACT.Exp, scale=-1.0,
                                   bias=neg_max[0:np_, b, m:m + 1],
                                   accum_out=sums[0:np_, b, m:m + 1]).then_inc(exped, 1)

                for name, arg, t in walk(steps, projections, prev is not None):
                    if name == "k" and arg % 4 == 3:
                        hi_part((u + 1) * 6 + (arg // 4 + RING))
                    elif name == "S":
                        expo(arg, 0)
                        expo(arg, 1)
                    elif name in ("Sa", "Sb"):
                        expo(arg, int(name == "Sb"))
                    elif name == "T":
                        i, m = arg
                        at_least(act, turned, turns + (t + 1))
                        if i < QB - 1:
                            act.activation(probT[m][:, 0:P * (i + 1)], turn[:, 0:P * (i + 1)], ACT.Copy).then_inc(turn_free, 1)
                        else:
                            act.activation(probT[m][:, 0:4 * SMP], turn[:, 0:4 * SMP], ACT.Copy)
                            act.activation(probT[m][0:SMP, 4 * SMP:5 * SMP], turn[0:SMP, 4 * SMP:5 * SMP],
                                           ACT.Copy).then_inc(turn_free, 1)
                    elif name == "OT":
                        at_least(act, turned, turns + (t + 1))
                        out_hi(u + (-1), prev, turn[:, 0:SEQ], slice(0, SEQ))
                    elif name == "Tail" and prev is not None:
                        at_least(act, tail_copied, u)
                        out_hi(u + (-1), prev, turn[:, 2 * P:2 * P + SMP], slice(SEQ, T))

            def out_hi(u, kind, src, cols):
                dst = out_block(oa_hi if kind == "A" else mid_hi, u, kind, cols)
                if kind == "A":
                    act.activation(dst, src, ACT.Copy).then_inc(o_hi, 1)
                else:
                    act.activation(dst, src, ACT.Copy, scale=gcol[:, G_SUBL:G_SUBL + 1]).then_inc(o_hi, 1)

            for u in range(NA):
                unit(Count(u), "A", u % 2, True, "A" if u else None)
            unit(Count(NA), "B", 0, True, "A")
            unit(Count(NA + 1), "B", 1, True, "B")
            with act.Fori(0, (NB - 4) // 2) as it:
                for v in range(2):
                    unit(Count(NA + 2 + v, [(it, 2)]), "B", v, True, "B")
            unit(Count(NU - 2), "B", 0, True, "B")
            unit(Count(NU - 1), "B", 1, False, "B")

            def gate(n, p):
                for kh in range(2):
                    hi_part(p + (kh + RING))
                at_least(act, w_used, p + 2)
                b = (n + PJ_GATE).mod(2)
                act.activation(halves(block_of(wide, n)), acc[b], ACT.Sigmoid).then_inc(proj_free[b], 1)

            act.wait_ge(av_done, NU * QB)
            act.wait_ge(out_free, NU * QB)
            act.wait_ge(o_summed, NB)
            for n in range(2):
                gate(Count(n), Count(PC_GATE + 2 * n))
            act.wait_ge(turned, TURN_END + 1)
            out_hi(Count(NU - 1), "B", turn[:, 0:SEQ], slice(0, SEQ))
            act.wait_ge(turned, TURN_END + 2)
            out_hi(Count(NU - 1), "B", turn[:, 2 * P:2 * P + SMP], slice(SEQ, T))
            act.wait_ge(kv_stored, 64 * NU)
            with act.Fori(0, KB - 1) as it:
                for j in range(2):
                    gate(Count(2 + j, [(it, 2)]), Count(PC_GATE + 4 + 2 * j, [(it, 4)]))
            for k in range(2):
                act.wait_ge(p_turned, k + 1)
                act.activation(pT_hi[:, k], pair[k][:, 0:T], ACT.Copy).then_inc(p_hi, 1)
            with act.Fori(0, KB // RING) as it:
                for j in range(RING):
                    hi_part(Count(PC_BRA + RING + j, [(it, RING)]))
            with act.Fori(0, KB // 2) as it:
                for j in range(2):
                    n = Count(j, [(it, 2)])
                    for kh in range(2):
                        hi_part(Count(PC_BRB + RING + 2 * j + kh, [(it, RING)]))
                    at_least(act, br_mixed, n + 1)
                    act.activation(block_of(act_hi, n), block_of(wide, n), ACT.Copy).then_inc(m_hi, 1)

            def square(n, src):
                at_least(act, sq_added, Count(n - 1))
                act.activation(sq[n % 2][:, :], src, ACT.Square).then_inc(squared, 1)

            for m in range(KB):
                if m % 2 == 1:
                    hi_part(Count(PC_PLE + RING + m // 2))
                act.wait_ge(proj_free[(PJ_PLE + m) % 2], (PJ_PLE + m) // 2 + 1)
                square(m, ple[:, m])
            for m in range(KB):
                for kh in range(2):
                    hi_part(Count(PC_OUT + RING + 2 * m + kh))
                act.wait_ge(proj_free[(PJ_OUT + m) % 2], (PJ_OUT + m) // 2 + 1)
                square(KB + m, mixed[:, m])
            for k in range(KB):
                act.wait_ge(h_updated, k + 1)
                act.activation(act_hi[:, k], hT[:, k], ACT.Copy, scale=gcol[:, G_FPRE + k:G_FPRE + k + 1]).then_inc(h_hi, 1)
            for k in range(KB):
                square(2 * KB + k, hT[:, k])
            with act.Fori(0, FG) as g:
                with act.Fori(0, KB // 2) as it:
                    for j in range(2):
                        for kh in range(2):
                            hi_part(Count(PC_FF + RING + 2 * j + kh, [(g, 4 * KB), (it, RING)]))
                        at_least(act, up_ready, Count(j + 1, [(g, KB), (it, 2)]))
                        act.activation(block_of(mid_hi, Count(j, [(it, 2)])), up_a[:, :], ACT.Copy).then_inc(up_hi, 1)
                with act.Fori(0, KB // 2) as it:
                    for j in range(RING):
                        hi_part(Count(PC_FF + 2 * KB + RING + j, [(g, 4 * KB), (it, RING)]))
            for b in range(2):
                act.wait_ge(proj_free[b], PJ_PG // 2)
            for k in range(KB):
                square(3 * KB + k, down_sum[:, k])
            for k in range(KB):
                act.wait_ge(h_updated, KB + k + 1)
                act.activation(act_hi[:, k], hT[:, k], ACT.Copy).then_inc(h_hi, 1)

            def y_rows(m):
                act.wait_ge(y_turned, m + 1)
                if m >= 2:
                    act.wait_ge(y_stored[m % 2], 32 * (m // 2))
                act.activation(y_tm[m % 2][:, 0:QB - 1], pair[m % 2][:, 0:SEQ].rearrange("p (j n) -> p j n", n=P), ACT.Copy)
                act.activation(y_tm[m % 2][0:SMP, QB - 1], pair[m % 2][0:SMP, SEQ:SEQ + P], ACT.Copy).then_inc(y_copied, 1)

            for m in range(KB):
                for kh in range(2):
                    if PC_PG + RING + 2 * m + kh < PC_END:
                        hi_part(Count(PC_PG + RING + 2 * m + kh))
                act.wait_ge(w_used, PC_PG + 2 * m + 2)
                if m >= 2:
                    act.wait_ge(y_turned, m - 1)
                b = (PJ_PG + m) % 2
                act.activation(halves(y_f[m % 2][:, :]), acc[b], ACT.Sigmoid).then_inc(proj_free[b], 1)
                if m:
                    y_rows(m - 1)
            y_rows(KB - 1)

        @block.vector
        def _(dve):
            own = [Count(0)]

            def done(ins):
                ins.then_inc(vec, 1)
                own[0] = own[0] + 1

            def settle():
                at_least(dve, vec, own[0])

            def loop(n, per):
                start = own[0]

                def enter(register):
                    own[0] = start + Count(0, [(register, per)])

                def leave(register):
                    got = own[0].const - start.const
                    assert got == per, got
                    own[0] = start + per * n
                return enter, leave

            for b in range(2):
                dve.memset(o_tm[b][SMP:P, QB - 1], 0.0)
            dve.wait_ge(rows_turned, 1)
            done(dve.tensor_copy(gcol[:, 0:41], turn[:, 0:41]))
            settle()
            dve.tensor_scalar(gcol[:, G_SUBL:G_SUBL + 1], gcol[:, G_SUB:G_SUB + 1], 1.0 - LAM0, None,
                              ALU.mult).then_inc(gains_ready, 1)
            for t in range(QB):
                n = rows(t)
                dve.wait_ge(x_rooted, t + 1)
                done(dve.reciprocal(r_x[0:n, t:t + 1], sq_x[0:n, t:t + 1]))
                settle()
                dve.tensor_scalar(x_scaled[0:n, t], x_tm[0:n, t], r_x[0:n, t:t + 1], None, ALU.mult).then_inc(x_ready, 1)
            dve.wait_ge(rel_loaded, 16)
            dve.tensor_copy(band_sb[:, 0:P], band_sb[:, P:P + 1].broadcast_to([2 * NA, P])).then_inc(band_made, 1)
            for k in range(KB):
                dve.wait_ge(u_hi, k + 1)
                dve.scalar_tensor_tensor(out=act_lo[:, k], in0=proj[k % 2][:, 0:T], scalar=gcol[:, G_PRE + k:G_PRE + k + 1],
                                         in1=act_hi[:, k].bitcast(F32), op0=ALU.mult, op1=ALU.subtract).then_inc(proj_free[k % 2], 1)
            dve.wait_ge(lam_loaded, 16)
            done(dve.tensor_tensor(lam_pr[:, 0], lam_in[:, 0], lam_in[:, 1], ALU.mult))
            done(dve.tensor_tensor(lam_pr[:, 1], lam_in[:, 2], lam_in[:, 3], ALU.mult))
            settle()
            dve.tensor_reduce(lam_s[:, 0:2], lam_pr[:, :, :], AX.X, ALU.add).then_inc(lam_ready, 1)
            dve.wait_ge(dist_made, 1)
            done(dve.tensor_copy(dist[:, :], dist_i[:, :]))
            settle()
            done(dve.scalar_tensor_tensor(out=tab_b[0][:, :], in0=dist[:, :], scalar=-1.0, in1=dist[:, :],
                                          op0=ALU.mult, op1=ALU.max))
            settle()
            done(dve.memset(tab_b[0][0:SMP, TW - SMP:TW], -2e2 * MASK))
            settle()
            done(dve.tensor_scalar(tab_b[0][:, :], tab_b[0][:, :], -0.5, None, ALU.mult))
            dve.wait_ge(lam_exped, 1)
            done(dve.tensor_tensor(lam_s[:, 0:1], lam_s[:, 3:4], lam_s[:, 2:3], ALU.subtract))
            settle()
            done(dve.tensor_scalar(neg_lam[:, :], lam_s[:, 0:1], -LAM0, None, ALU.add))

            def projected(u, n):
                b = (u * 3 + (PJ_IN + n)).mod(2)
                par = u.mod(2)
                at_least(dve, w_used, u * 6 + (2 * n + 2))
                dst = (vT, kT, qT)[n][par][:, :]
                if n < 2:
                    dve.tensor_copy(halves(dst), acc[b]).then_inc(proj_free[b], 1)
                else:
                    dve.tensor_scalar(halves(dst), acc[b], 0.125, None, ALU.mult).then_inc(proj_free[b], 1)

            for n in range(3):
                projected(Count(0), n)

            def unit(u, kind, par, projections, prev):
                steps = A_STEPS if kind == "A" else B_STEPS
                turns = turn_base(u, kind)

                def bias(i, m):
                    n, np_, b = keys(i), rows(i), i % 2
                    at_least_alone(dve, scored, u * 10 + (2 * i + m + 1))
                    tab = tab_a[par][:, m] if kind == "A" else tab_b[par][:, :]
                    tab = tab[:, TW - n:TW] if i < QB - 1 else tab[0:np_, 0:n]
                    src = score[0:np_, 512 * m:512 * m + n] if i < QB - 1 else score[0:np_, 0:n]
                    dve.tensor_tensor_reduce(prob[b][m][0:np_, 0:n], src, tab, -1.0, 3e38, ALU.add, ALU.min,
                                             neg_max[0:np_, b, m:m + 1]).then_inc(biased, 1)

                for name, arg, t in walk(steps, projections, prev is not None):
                    if name == "k" and arg % 8 == 7:
                        projected(u + 1, arg // 8)
                    elif name == "S":
                        if arg == 0:
                            at_least(dve, tab_ready, u + int(kind == "A"))
                        bias(arg, 0)
                        bias(arg, 1)
                    elif name in ("Sa", "Sb"):
                        bias(arg, int(name == "Sb"))
                    elif name in ("V4", "K4"):
                        at_least(dve, turned, turns + (t + 1))
                        at_least(dve, kv_stored, u * 64)
                        dst = v_tm if name == "V4" else k_tm
                        dve.tensor_copy(dst[:, 0:QB - 1].rearrange("p j n -> p (j n)"), turn[:, 0:SEQ]).then_inc(turn_free, 1)
                    elif name == "Tail":
                        at_least(dve, turned, turns + (t + 1))
                        dve.tensor_copy(v_tm[0:SMP, QB - 1], turn[0:SMP, 0:P])
                        if prev is None:
                            dve.tensor_copy(k_tm[0:SMP, QB - 1], turn[0:SMP, P:2 * P]).then_inc(turn_free, 1)
                        else:
                            dve.tensor_copy(k_tm[0:SMP, QB - 1], turn[0:SMP, P:2 * P]).then_inc(tail_copied, 1)
                            at_least(dve, o_hi, u * 2)
                            out_lo(u + (-1), prev, turn[:, 2 * P:2 * P + SMP], slice(SEQ, T))
                    elif name == "OT":
                        if prev == "B":
                            normalise(u + (-1), 1 - par)
                        at_least(dve, o_hi, u * 2 + (-1))
                        out_lo(u + (-1), prev, turn[:, 0:SEQ], slice(0, SEQ))
                    elif name == "CK":
                        at_least(dve, turned, turns + (t + 1))
                        dve.tensor_copy(ckT[:, :], turn[:, 0:SEQ]).then_inc(turn_free, 1)
                    elif name == "C":
                        i, b, np_ = arg, arg % 2, rows(arg)
                        at_least(dve, exped, u * 10 + (2 * i + 2))
                        done(dve.reciprocal(r_sum[0:np_, b], sums[0:np_, b]))
                        settle()
                        done(dve.scalar_tensor_tensor(out=c_map[0:np_, b:b + 1], in0=sums[0:np_, b, 0:1],
                                                      scalar=r_sum[0:np_, b, 1:2], in1=neg_lam[0:np_, :],
                                                      op0=ALU.mult, op1=ALU.mult))
                        settle()
                        n = keys(i)
                        dve.scalar_tensor_tensor(out=prob[b][0][0:np_, 0:n], in0=prob[b][1][0:np_, 0:n],
                                                 scalar=c_map[0:np_, b:b + 1], in1=prob[b][0][0:np_, 0:n],
                                                 op0=ALU.mult, op1=ALU.add).then_inc(combined, 1)
                    elif name == "AV":
                        i, b, np_ = arg, arg % 2, rows(arg)
                        if kind == "A":
                            at_least(dve, exped, u * 10 + (2 * i + 2))
                            done(dve.reciprocal(r_sum[0:np_, b], sums[0:np_, b]))
                            settle()
                            at_least(dve, av_done, u * QB + (i + 1))
                            for m in range(2):
                                last = dve.tensor_scalar(o_tm[par][0:np_, i, 64 * m:64 * m + 64], outp[0:np_, 64 * m:64 * m + 64],
                                                         r_sum[0:np_, b, m:m + 1], None, ALU.mult)
                            last.then_inc(out_free, 1)
                        else:
                            at_least(dve, av_done, u * QB + (i + 1))
                            dve.tensor_scalar(o_tm[par][0:np_, i], outp[0:np_, 0:P], r_sum[0:np_, b, 0:1], None,
                                              ALU.mult).then_inc(out_free, 1)
                if kind == "B":
                    at_least(dve, out_free, (u + 1) * QB)
                    done(dve.tensor_tensor(o_sq[:, :, :], o_tm[par][:, :, :], o_tm[par][:, :, :], ALU.mult))
                    settle()
                    done(dve.tensor_reduce(o_ms[:, par], o_sq[:, :, :], AX.X, ALU.add))
                    settle()
                    dve.tensor_scalar(o_ms[:, par], o_ms[:, par], 1.0 / P, EPS, ALU.mult, ALU.add).then_inc(o_summed, 1)

            def normalise(u, par):
                at_least(dve, o_rooted, u + (1 - NA))
                dve.tensor_tensor(o_tm[par][:, :, :], o_tm[par][:, :, :], o_r[:, :].unsqueeze(2).broadcast_to([P, QB, P]),
                                  ALU.mult).then_inc(o_normed, 1)

            def out_lo(u, kind, src, cols):
                hi, lo = (oa_hi, oa_lo) if kind == "A" else (mid_hi, mid_lo)
                hi, lo = out_block(hi, u, kind, cols).bitcast(F32), out_block(lo, u, kind, cols)
                if kind == "A":
                    dve.tensor_tensor(lo, src, hi, ALU.subtract).then_inc(turn_free, 1)
                else:
                    dve.scalar_tensor_tensor(out=lo, in0=src, scalar=gcol[:, G_SUBL:G_SUBL + 1], in1=hi,
                                             op0=ALU.mult, op1=ALU.subtract).then_inc(turn_free, 1)

            for u in range(NA):
                unit(Count(u), "A", u % 2, True, "A" if u else None)
            unit(Count(NA), "B", 0, True, "A")
            unit(Count(NA + 1), "B", 1, True, "B")
            enter, leave = loop((NB - 4) // 2, 2 * (2 * QB + 2))
            with dve.Fori(0, (NB - 4) // 2) as it:
                enter(it)
                for v in range(2):
                    unit(Count(NA + 2 + v, [(it, 2)]), "B", v, True, "B")
                leave(it)
            unit(Count(NU - 2), "B", 0, True, "B")
            unit(Count(NU - 1), "B", 1, False, "B")
            normalise(Count(NU - 1), 1)
            dve.wait_ge(o_hi, 2 * NU - 1)
            out_lo(Count(NU - 1), "B", turn[:, 0:SEQ], slice(0, SEQ))
            dve.wait_ge(o_hi, 2 * NU)
            out_lo(Count(NU - 1), "B", turn[:, 2 * P:2 * P + SMP], slice(SEQ, T))
            for k in range(2):
                dve.wait_ge(p_hi, k + 1)
                dve.tensor_tensor(pT_lo[:, k], pair[k][:, 0:T], pT_hi[:, k].bitcast(F32), ALU.subtract).then_inc(p_split, 1)
            dve.memset(sq_sum[:, T:QB * P], 0.0).then_inc(sq_cleared, 1)

            with dve.Fori(0, KB // RING) as it:
                for j in range(RING):
                    at_least(dve, w_used, Count(PC_BRA + j + 1, [(it, RING)]))
                    b = (PJ_BRA + j) % 2
                    w = block_of(wide, Count(j, [(it, RING)]))
                    dve.tensor_tensor(halves(w), acc[b], halves(w), ALU.mult).then_inc(proj_free[b], 1)
            with dve.Fori(0, KB // 2) as it:
                for j in range(2):
                    n = Count(j, [(it, 2)])
                    at_least(dve, w_used, Count(PC_BRB + 2 * j + 2, [(it, RING)]))
                    b = (PJ_BRB + j) % 2
                    wa, wb = block_of(wide, n), block_of(wide, n + KB)
                    dve.tensor_tensor(halves(wb), acc[b], halves(wb), ALU.mult).then_inc(proj_free[b], 1)
                    at_least(dve, proj_free[b], Count((PJ_BRB + j) // 2 + 1, [(it, 1)]))
                    dve.tensor_tensor(wa, wa, wb, ALU.add).then_inc(br_mixed, 1)
                    at_least(dve, m_hi, n + 1)
                    dve.tensor_tensor(block_of(act_lo, n), wa, block_of(act_hi, n).bitcast(F32), ALU.subtract).then_inc(m_split, 1)

            def add_square(n):
                dve.wait_ge(squared, n + 1)
                if n % KB == 0:
                    dve.tensor_copy(sq_sum[:, 0:T], sq[n % 2][:, :]).then_inc(sq_added, 1)
                else:
                    dve.wait_ge(sq_added, n)
                    dve.tensor_tensor(sq_sum[:, 0:T], sq_sum[:, 0:T], sq[n % 2][:, :], ALU.add).then_inc(sq_added, 1)

            def row_of_norm(n):
                dve.wait_ge(sum_turned, n + 1)
                dve.tensor_scalar(ms_t[:, :], turn[:, 0:QB], 1.0 / D, EPS, ALU.mult, ALU.add).then_inc(ms_ready, 1)
                dve.wait_ge(r_ready, n + 1)
                dve.tensor_tensor(diag[:, :, :], ident[:, :].unsqueeze(1).broadcast_to([P, QB, P]),
                                  r_t[:, :].unsqueeze(2).broadcast_to([P, QB, P]), ALU.mult).then_inc(diag_ready, 1)
                dve.wait_ge(row_ready, n + 1)

            def normed(x, k, g):
                return dve.scalar_tensor_tensor(out=x[:, k], in0=x[:, k], scalar=gcol[:, g + k:g + k + 1],
                                                in1=score[:, 0:T], op0=ALU.mult, op1=ALU.mult)

            for m in range(KB):
                b = (PJ_PLE + m) % 2
                if m % 2 == 0:
                    dve.wait_ge(ple_first, m // 2 + 1)
                else:
                    dve.wait_ge(w_used, PC_PLE + m // 2 + 1)
                dve.tensor_copy(halves(ple[:, m]), acc[b]).then_inc(proj_free[b], 1)
                if m:
                    add_square(m - 1)
            add_square(KB - 1)

            def keep_out(m):
                b = (PJ_OUT + m) % 2
                dve.wait_ge(w_used, PC_OUT + 2 * m + 2)
                dve.tensor_copy(halves(mixed[:, m]), acc[b]).then_inc(proj_free[b], 1)

            keep_out(0)
            keep_out(1)
            row_of_norm(0)
            for k in range(KB):
                last = normed(ple, k, G_PLE)
            done(last)
            for m in range(2, KB):
                keep_out(m)
                if m == 2:
                    add_square(KB)
                add_square(KB + m - 1)
            add_square(2 * KB - 1)

            def update(n, x, g):
                def rest(k):
                    dve.wait_ge(h_hi, n * KB + k + 1)
                    if n == 0:
                        dve.scalar_tensor_tensor(out=act_lo[:, k], in0=hT[:, k], scalar=gcol[:, G_FPRE + k:G_FPRE + k + 1],
                                                 in1=act_hi[:, k].bitcast(F32), op0=ALU.mult, op1=ALU.subtract).then_inc(h_split, 1)
                    else:
                        dve.tensor_tensor(act_lo[:, k], hT[:, k], act_hi[:, k].bitcast(F32), ALU.subtract).then_inc(h_split, 1)

                for k in range(KB):
                    done(normed(x, k, g))
                    settle()
                    dve.tensor_tensor(hT[:, k], hT[:, k], x[:, k], ALU.add).then_inc(h_updated, 1)
                    if k:
                        rest(k - 1)
                rest(KB - 1)

            row_of_norm(1)
            update(0, mixed, G_POST)
            for k in range(KB):
                add_square(2 * KB + k)
            row_of_norm(2)
            dve.tensor_copy(r_row[:, :], score[:, 0:T]).then_inc(row_read, 1)
            dve.wait_ge(row_read, 1)
            dve.wait_ge(down_cleared, 1)

            with dve.Fori(0, FG) as g:
                with dve.Fori(0, KB // 2) as it:
                    for j in range(2):
                        b = (PJ_FF + j) % 2
                        at_least(dve, w_used, Count(PC_FF + 2 * j + 2, [(g, 4 * KB), (it, RING)]))
                        dve.tensor_tensor(halves(up_t[:, :]), acc[b], halves(r_row[:, :]), ALU.mult).then_inc(proj_free[b], 1)
                        at_least(dve, proj_free[b], Count((PJ_FF + j) // 2 + 1, [(g, KB), (it, 1)]))
                        dve.scalar_tensor_tensor(out=up_a[:, :], in0=up_t[:, :], scalar=0.0, in1=up_t[:, :],
                                                 op0=ALU.max, op1=ALU.mult).then_inc(up_ready, 1)
                        n = Count(j, [(it, 2)])
                        at_least(dve, up_hi, Count(j + 1, [(g, KB), (it, 2)]))
                        dve.tensor_tensor(block_of(mid_lo, n), up_a[:, :], block_of(mid_hi, n).bitcast(F32),
                                          ALU.subtract).then_inc(up_split, 1)
                with dve.Fori(0, KB // 2) as it:
                    for j in range(2):
                        b = (PJ_FF + KB + j) % 2
                        at_least(dve, w_used, Count(PC_FF + 2 * KB + 2 * j + 2, [(g, 4 * KB), (it, RING)]))
                        d = block_of(wide, Count(j, [(it, 2)]))
                        dve.tensor_tensor(halves(d), acc[b], halves(d), ALU.add).then_inc(proj_free[b], 1)

            for k in range(KB):
                add_square(3 * KB + k)
            row_of_norm(3)
            update(1, down_sum, G_FPOST)
            for m in range(KB):
                b = (PJ_PG + m) % 2
                dve.wait_ge(proj_free[b], (PJ_PG + m) // 2 + 1)
                y = y_f[m % 2][:, :]
                done(dve.tensor_tensor(y, y, ple[:, m], ALU.mult))
                settle()
                dve.tensor_tensor(y, y, hT[:, m], ALU.add).then_inc(y_ready, 1)

        @block.tensor
        def _(pe):
            def wait_projection(n):
                b = n.mod(2)
                at_least(pe, proj_free[b], (n + (-b)).over(2))

            def k_steps(n, p, hi, lo, blocks=KB, input_ready=None):
                out = acc[n.mod(2)]
                for k in range(blocks):
                    if k == 0:
                        wait_projection(n)
                    if k % 4 == 0:
                        at_least(pe, lo_done, p + (k // 4 + 1))
                    if input_ready:
                        input_ready(k)
                    slot, at = (p + k // 4).mod(RING), slice(P * (k % 4), P * (k % 4) + P)
                    for s, (w, x) in enumerate(((w_hi, hi), (w_lo, hi), (w_hi, lo))):
                        for h in range(2):
                            last = pe.matmul(out[:, h], w[:, slot, at], x[:, k, HALF * h:HALF * h + HALF],
                                             start=(k == 0 and s == 0), stop=(k == blocks - 1 and s == 2))
                    if k % 4 == 3:
                        last.then_inc(w_used, 1)
                    yield

            def project(*args, **kw):
                for _ in k_steps(*args, **kw):
                    pass

            def unit_steps(u):
                for n in range(3):
                    yield from k_steps(u * 3 + (PJ_IN + n), u * 6 + 2 * n, act_hi, act_lo)

            pe.wait_ge(consts, 1)
            pe.wait_ge(rows_loaded, 16 * 6)
            pe.transpose(turn[:, 0:41], gain_rows[:, :], ident[0:41, 0:41]).then_inc(rows_turned, 1)
            pe.wait_ge(x_ready, QB)
            for k in range(KB):
                wait_projection(Count(k))
                for t in range(QB):
                    n = rows(t)
                    last = pe.transpose(proj[k % 2][:, P * t:P * t + n], x_scaled[0:n, t, P * k:P * k + P], ident[0:n, 0:n])
                last.then_inc(u_turned, 1)
            for b in range(2):
                pe.wait_ge(proj_free[b], KB // 2)
            pe.wait_ge(gains_ready, 1)
            steps = unit_steps(Count(0))
            for j in range(KB):
                for _ in range(3):
                    next(steps)
                if j >= 2:
                    pe.wait_ge(x_kept, j - 1)
                for t in range(QB):
                    n = rows(t)
                    last = pe.transpose(pair[j % 2][:, P * t:P * t + n], x_tm[0:n, t, P * j:P * j + P], ident[0:n, 0:n])
                last.then_inc(x_turned, 1)
            pe.wait_ge(x_kept, KB)

            def unit(u, kind, par, projections, prev):
                steps = A_STEPS if kind == "A" else B_STEPS
                turns = turn_base(u, kind)
                projected = unit_steps(u + 1)

                def scores(i, m):
                    n, np_, h = keys(i), rows(i), slice(64 * m, 64 * m + 64)
                    job = 2 * i + m
                    at_least_alone(pe, biased, u * 10 + (0 if i == 0 else job if i == QB - 1 else job - 1))
                    q = qT[par][h, P * i:P * i + np_]
                    if i < QB - 1:
                        last = pe.matmul(score[:, 512 * m:512 * m + n], q, kT[par][h, 0:n], start=True, stop=True)
                    else:
                        pe.matmul(score[0:np_, 0:SEQ], q, ckT[h, :], start=True, stop=True)
                        last = pe.matmul(score[0:np_, SEQ:T], q, kT[par][h, SEQ:T], start=True, stop=True)
                    last.then_inc(scored, 1)

                for name, arg, t in walk(steps, projections, prev is not None):
                    if name == "k":
                        next(projected)
                        continue
                    if t is not None:
                        at_least_alone(pe, turn_free, turns + t)
                    if name == "S":
                        if arg == 0:
                            for n in (1, 2):
                                job = u * 3 + (PJ_IN + n)
                                b = job.mod(2)
                                at_least(pe, proj_free[b], (job + (-b)).over(2) + 1)
                        scores(arg, 0)
                        scores(arg, 1)
                    elif name in ("Sa", "Sb"):
                        scores(QB - 1, int(name == "Sb"))
                    elif name in ("V4", "K4"):
                        src = vT[par] if name == "V4" else kT[par]
                        for j in range(QB - 1):
                            last = pe.transpose(turn[:, P * j:P * j + P], src[:, P * j:P * j + P], ident[:, :])
                        last.then_inc(turned, 1)
                    elif name == "CK":
                        at_least(pe, ck_loaded, (u + 1) * 16)
                        for j in range(QB - 1):
                            last = pe.transpose(turn[:, P * j:P * j + P], ck[:, P * j:P * j + P], ident[:, :])
                        last.then_inc(turned, 1)
                    elif name == "Tail":
                        last = pe.transpose(turn[0:SMP, 0:P], vT[par][:, SEQ:T], ident[:, :])
                        last = pe.transpose(turn[0:SMP, P:2 * P], kT[par][:, SEQ:T], ident[:, :])
                        if prev is not None:
                            last = out_tail(1 - par)
                        last.then_inc(turned, 1)
                    elif name == "OT":
                        outputs_ready(u + (-1), prev)
                        out_main(1 - par)
                    elif name == "T":
                        i, m = arg
                        np_ = rows(i)
                        if kind == "A":
                            at_least_alone(pe, exped, u * 10 + (2 * i + m + 1))
                        else:
                            at_least_alone(pe, combined, (u + (-NA)) * QB + (i + 1))
                        for j in range(n_key_blocks(i)):
                            nk = P if j < QB - 1 else SMP
                            last = pe.transpose(turn[0:nk, np_ * j:np_ * j + np_], prob[i % 2][m][0:np_, P * j:P * j + nk],
                                                ident[0:np_, 0:np_])
                        last.then_inc(turned, 1)
                    elif name == "AV":
                        i = arg
                        np_ = rows(i)
                        last_turn = max(tt for nn, aa, tt in walk(steps, projections, prev is not None)
                                        if nn == "T" and aa[0] == i)
                        at_least(pe, turn_free, turns + (last_turn + 1))
                        at_least(pe, out_free, u * QB + i)
                        if i == QB - 1:
                            at_least(pe, cv_loaded, (u + 1) * 16)
                        for m in range(2 if kind == "A" else 1):
                            c = slice(64 * m, 64 * m + 64) if kind == "A" else slice(0, P)
                            for j in range(n_key_blocks(i)):
                                if i < QB - 1:
                                    v, nk = v_tm[:, j, c], P
                                elif j < QB - 1:
                                    v, nk = cv[:, P * j + c.start:P * j + c.stop], P
                                else:
                                    v, nk = v_tm[0:SMP, j, c], SMP
                                last = pe.matmul(outp[0:np_, c], probT[m][0:nk, np_ * j:np_ * j + np_], v,
                                                 start=(j == 0), stop=(j == n_key_blocks(i) - 1))
                        last.then_inc(av_done, 1)

            def outputs_ready(u, kind):
                if kind == "A":
                    at_least(pe, out_free, (u + 1) * QB)
                else:
                    at_least(pe, o_normed, u + (1 - NA))

            def out_main(b):
                for j in range(QB - 1):
                    last = pe.transpose(turn[:, P * j:P * j + P], o_tm[b][:, j], ident[:, :])
                last.then_inc(turned, 1)

            def out_tail(b):
                return pe.transpose(turn[:, 2 * P:2 * P + SMP], o_tm[b][0:SMP, QB - 1], ident[0:SMP, 0:SMP])

            for u in range(NA):
                unit(Count(u), "A", u % 2, True, "A" if u else None)
            unit(Count(NA), "B", 0, True, "A")
            unit(Count(NA + 1), "B", 1, True, "B")
            with pe.Fori(0, (NB - 4) // 2) as it:
                for v in range(2):
                    unit(Count(NA + 2 + v, [(it, 2)]), "B", v, True, "B")
            unit(Count(NU - 2), "B", 0, True, "B")
            unit(Count(NU - 1), "B", 1, False, "B")

            for n in range(2):
                project(Count(PJ_GATE + n), Count(PC_GATE + 2 * n), act_hi, act_lo)
            outputs_ready(Count(NU - 1), "B")
            pe.wait_ge(turn_free, TURN_END)
            out_main(1)
            pe.wait_ge(turn_free, TURN_END + 1)
            out_tail(1).then_inc(turned, 1)
            with pe.Fori(0, KB - 1) as it:
                for j in range(2):
                    project(Count(PJ_GATE + 2 + j, [(it, 2)]), Count(PC_GATE + 4 + 2 * j, [(it, RING)]), act_hi, act_lo)
            pe.wait_ge(p_loaded, 32)
            pe.wait_ge(turn_free, TURN_END + 2)
            for k in range(2):
                for t in range(QB):
                    n = rows(t)
                    last = pe.transpose(pair[k][:, P * t:P * t + n], p_tm[0:n, t, P * k:P * k + P], ident[0:n, 0:n])
                last.then_inc(p_turned, 1)
            with pe.Fori(0, KB // RING) as it:
                for j in range(RING):
                    project(Count(PJ_BRA + j, [(it, RING)]), Count(PC_BRA + j, [(it, RING)]), oa_hi, oa_lo, blocks=NA)
            with pe.Fori(0, KB // 2) as it:
                for j in range(2):
                    project(Count(PJ_BRB + j, [(it, 2)]), Count(PC_BRB + 2 * j, [(it, RING)]), mid_hi, mid_lo)
            pe.wait_ge(p_split, 2)
            for m in range(KB):
                p = Count(PC_PLE + m // 2)
                wait_projection(Count(PJ_PLE + m))
                at_least(pe, lo_done, p + 1)
                for k in range(2):
                    at = slice(2 * P * k + P * (m % 2), 2 * P * k + P * (m % 2) + P)
                    for s, (w, x) in enumerate(((w_hi, pT_hi), (w_lo, pT_hi), (w_hi, pT_lo))):
                        for h in range(2):
                            last = pe.matmul(acc[(PJ_PLE + m) % 2][:, h], w[:, p.mod(RING), at], x[:, k, HALF * h:HALF * h + HALF],
                                             start=(k == 0 and s == 0), stop=(k == 1 and s == 2))
                last.then_inc(w_used if m % 2 else ple_first, 1)

            def norm_row(n):
                if n == 0:
                    pe.wait_ge(sq_cleared, 1)
                pe.wait_ge(sq_added, KB * (n + 1))
                for t in range(QB):
                    last = pe.matmul(turn[:, t:t + 1], sq_sum[:, P * t:P * t + P], ones[:, 0:1], start=True, stop=True)
                last.then_inc(sum_turned, 1)
                pe.wait_ge(diag_ready, n + 1)
                for t in range(QB):
                    last = pe.matmul(score[:, P * t:P * t + rows(t)], ones[:, :], diag[:, t, 0:rows(t)], start=True, stop=True)
                last.then_inc(row_ready, 1)

            pe.wait_ge(m_split, KB)
            for m in range(2):
                project(Count(PJ_OUT + m), Count(PC_OUT + 2 * m), act_hi, act_lo)
            norm_row(0)
            with pe.Fori(0, KB // 2 - 1) as it:
                for j in range(2):
                    project(Count(PJ_OUT + 2 + j, [(it, 2)]), Count(PC_OUT + 4 + 2 * j, [(it, RING)]), act_hi, act_lo)
            norm_row(1)
            norm_row(2)
            pe.wait_ge(h_split, KB)
            with pe.Fori(0, FG) as g:
                with pe.Fori(0, KB // 2) as it:
                    for j in range(2):
                        project(Count(PJ_FF + j, [(g, 2 * KB), (it, 2)]), Count(PC_FF + 2 * j, [(g, 4 * KB), (it, RING)]),
                                act_hi, act_lo)
                with pe.Fori(0, KB // 2) as it:
                    for j in range(2):
                        project(Count(PJ_FF + KB + j, [(g, 2 * KB), (it, 2)]),
                                Count(PC_FF + 2 * KB + 2 * j, [(g, 4 * KB), (it, RING)]), mid_hi, mid_lo,
                                input_ready=lambda k: at_least(pe, up_split, Count(k + 1, [(g, KB)])))
            norm_row(3)

            def turn_y(m):
                pe.wait_ge(y_ready, m + 1)
                if m >= 2:
                    pe.wait_ge(y_copied, m - 1)
                for t in range(QB):
                    n = rows(t)
                    last = pe.transpose(pair[m % 2][0:n, P * t:P * t + P], y_f[m % 2][:, P * t:P * t + n], ident[:, :])
                last.then_inc(y_turned, 1)

            for m in range(KB):
                project(Count(PJ_PG + m), Count(PC_PG + 2 * m), act_hi, act_lo,
                        input_ready=(lambda k: pe.wait_ge(h_split, KB + k + 1)) if m == 0 else None)
                if m:
                    turn_y(m - 1)
            turn_y(KB - 1)


def kernel(**inputs):
    import numpy as np
    import concourse.bacc as bacc
    from concourse.bass_utils import run_bass_kernel_spmd

    names = ["x_prompt", "x_sample", "cache_a_k", "cache_a_v", "cache_b_k", "cache_b_v", "p_prompt", "p_sample",
             "w_in", "rel_bias", "diff_lambda", "diff_subln", "w_gate", "w_branch_a", "w_branch_b", "w_out",
             "g_mix_pre", "g_mix_post", "g_ffn_pre", "g_ffn_post", "w_up", "w_down", "w_ple", "g_ple", "w_ple_gate"]
    arrays = {n: np.ascontiguousarray(inputs[n]) for n in names}
    arrays["rel_bias"] = np.ascontiguousarray(arrays["rel_bias"][:, :, ::-1])
    d, bsz, s, m = 1, 1, arrays["x_prompt"].shape[1], arrays["x_sample"].shape[1]
    ha, hd = arrays["cache_a_k"].shape[3:]
    hb = arrays["cache_b_k"].shape[3]
    keep = min(8 * 64, s)
    shapes = [arrays["x_prompt"].shape, arrays["x_sample"].shape,
              (d, bsz, keep, ha, hd), (d, bsz, keep, ha, hd), (d, bsz, s, hb, 2, hd), (d, bsz, s, hb, 2 * hd),
              (d, bsz, m, ha, hd), (d, bsz, m, ha, hd), (d, bsz, m, hb, 2, hd), (d, bsz, m, hb, 2 * hd)]
    nc = bacc.Bacc("TRN2", target_bir_lowering=False, num_devices=1)
    ins = [nc.dram_tensor(n, arrays[n].shape, mybir.dt.from_np(arrays[n].dtype), kind="ExternalInput").ap() for n in names]
    outs = [nc.dram_tensor(f"out_{i}", sh, F32, kind="ExternalOutput").ap() for i, sh in enumerate(shapes)]
    encoder_layer(nc, *ins, *outs)
    r = run_bass_kernel_spmd(nc, [arrays], core_ids=[0])
    return tuple(r.results[0][f"out_{i}"] for i in range(len(shapes)))
```

```python
from contextlib import ExitStack

import concourse.bass as bass
from concourse import mybir

F32, F32R, I32 = mybir.dt.float32, mybir.dt.float32r, mybir.dt.int32
ALU, ACT, AX = mybir.AluOpType, mybir.ActivationFunctionType, mybir.AxisListType

P = 128
EPS = 1e-6
LAM0 = 0.2
MASK = -1e30
RING = 4
PIECE = 512

A_STEPS = [("V4", 0, 0), ("S", 0, 2), ("S", 1, 1), ("K4", 0, 1), ("T", (0, 0), 1), ("T", (0, 1), 1),
           ("OT", 0, 1), ("AV", 0, 1), ("S", 2, 0), ("Tail", 0, 1), ("T", (1, 0), 1), ("T", (1, 1), 1),
           ("CK", 0, 1), ("AV", 1, 1), ("S", 3, 0), ("T", (2, 0), 1), ("T", (2, 1), 1), ("AV", 2, 0),
           ("Sa", 4, 1), ("T", (3, 0), 2), ("T", (3, 1), 1), ("Sb", 4, 1), ("AV", 3, 1), ("T", (4, 0), 0),
           ("T", (4, 1), 1), ("AV", 4, 2)]
B_STEPS = [("V4", 0, 0), ("S", 0, 2), ("K4", 0, 1), ("C", 0, 1), ("T", (0, 0), 1), ("S", 1, 0), ("C", 1, 0),
           ("AV", 0, 1), ("S", 2, 2), ("T", (1, 0), 1), ("OT", 0, 1), ("S", 3, 0), ("C", 2, 2), ("AV", 1, 0),
           ("Tail", 0, 1), ("CK", 0, 2), ("T", (2, 0), 1), ("C", 3, 0), ("AV", 2, 1), ("Sa", 4, 0),
           ("T", (3, 0), 1), ("Sb", 4, 0), ("C", 4, 1), ("AV", 3, 2), ("T", (4, 0), 1), ("AV", 4, 2)]


def walk(steps, with_outputs):
    k, turn = 0, 0
    for name, arg, before in steps:
        for _ in range(before):
            yield "k", k, None
            k += 1
        if name == "OT" and not with_outputs:
            continue
        if name in ("V4", "K4", "T", "OT", "Tail", "CK"):
            yield name, arg, turn
            turn += 1
        else:
            yield name, arg, None


class Count:

    def __init__(self, const, terms=()):
        self.const, self.terms = const, tuple(terms)

    def __add__(self, n):
        if isinstance(n, Count):
            return Count(self.const + n.const, self.terms + n.terms)
        return Count(self.const + n, self.terms)

    def __mul__(self, n):
        return Count(self.const * n, [(r, f * n) for r, f in self.terms])

    def over(self, n):
        assert all(f % n == 0 for _, f in self.terms)
        return Count(self.const // n, [(r, f // n) for r, f in self.terms])

    def mod(self, n):
        assert all(f % n == 0 for _, f in self.terms)
        return self.const % n

    def value(self):
        v = self.const
        for register, factor in self.terms:
            v = register * factor + v
        return v


def at_least(eng, sem, count):
    v = count.value()
    assert not count.terms or count.const > 0
    if not isinstance(v, int) or v > 0:
        eng.wait_ge(sem, v)


def at_least_alone(eng, sem, count):
    at_least(eng, sem, count)
    if count.terms:
        eng.nop(nofuse=True)


def encoder_layer(nc, x_prompt, x_sample, cache_a_k, cache_a_v, cache_b_k, cache_b_v, p_prompt, p_sample,
                  w_in, rel_bias_reversed, diff_lambda, diff_subln, w_gate, w_branch_a, w_branch_b, w_out,
                  g_mix_pre, g_mix_post, g_ffn_pre, g_ffn_post, w_up, w_down, w_ple, g_ple, w_ple_gate,
                  y_prompt, y_sample, ak_p, av_p, bk_p, bv_p, ak_s, av_s, bk_s, bv_s):
    SEQ, D = x_prompt.shape[1:]
    SMP = x_sample.shape[1]
    T = SEQ + SMP
    HALF = T // 2
    QB = SEQ // P + 1
    KB = D // P
    AW = cache_a_k.shape[3] * cache_a_k.shape[4]
    NA = AW // P
    NB = cache_b_k.shape[3]
    NU = NA + NB
    FF = w_up.shape[2]
    FG = FF // D
    REL = rel_bias_reversed.shape[2] // 2
    TW = SEQ + P
    assert T == 576 and NA == 4 and NB == 8 and REL == P and cache_a_k.shape[2] == SEQ

    xp, xs_d = x_prompt[0], x_sample[0]
    cak, cav = [c[0, 0].rearrange("t h d -> t (h d)") for c in (cache_a_k, cache_a_v)]
    cbk, cbv = cache_b_k[0, 0].rearrange("t h c d -> t (h c d)"), cache_b_v[0, 0].rearrange("t h d -> t (h d)")
    out_a = [o[0, 0].rearrange("t h d -> t (h d)") for o in (ak_p, av_p, ak_s, av_s)]
    out_b = [bk_p[0, 0].rearrange("t h c d -> t (h c d)"), bv_p[0, 0].rearrange("t h d -> t (h d)"),
             bk_s[0, 0].rearrange("t h c d -> t (h c d)"), bv_s[0, 0].rearrange("t h d -> t (h d)")]
    rev = rel_bias_reversed[0]
    BW = P + 2 * REL
    band = nc.dram_tensor("band_bias", [2 * NA, P, BW], F32, kind="Internal").ap()

    PC_GATE = 6 * NU
    PC_BRA = PC_GATE + 2 * 2 * KB
    PC_BRB = PC_BRA + KB
    PC_OUT = PC_BRB + 2 * KB
    PC_PLE = (PC_OUT + 2 * KB, PC_OUT + 2 * KB + KB // 4 + FG * 4 * KB)
    PC_FF = PC_PLE[0] + KB // 4
    PC_PG = PC_PLE[1] + KB // 4
    PC_END = PC_PG + 2 * KB
    PJ_IN = 0
    PJ_GATE = PJ_IN + 3 * NU
    PJ_BRA = PJ_GATE + 2 * KB
    PJ_BRB = PJ_BRA + KB
    PJ_OUT = PJ_BRB + KB
    PJ_PLE = (PJ_OUT + KB, PJ_OUT + KB + KB // 2 + FG * 2 * KB)
    PJ_FF = PJ_PLE[0] + KB // 2
    PJ_PG = PJ_PLE[1] + KB // 2
    N_POST, N_FPRE, N_FPOST, N_PLE = range(4)
    RAW = 6
    Y_AFTER = {m: (2 * m - 8, 2 * m - 7) if m >= KB // 2 else () for m in range(KB)}
    BY_POOL = (0, 1, 3, 5)
    BY_VECTOR = (2, 4, 6, 7)
    A_TURNS, B_TURNS = 15, 10
    TURN_B = A_TURNS * NA - 1
    TURN_END = TURN_B + B_TURNS * NB

    with ExitStack() as ctx:
        def sb(name, shape, dt=F32, stack=ctx):
            return stack.enter_context(nc.sbuf_tensor(name, shape, dt))

        def sem(name):
            return ctx.enter_context(nc.semaphore(name))

        ident, ones = sb("ident", [P, P]), sb("ones", [P, P])
        gcol = sb("gcol", [P, 48])
        G_PRE, G_POST, G_FPRE, G_FPOST, G_PLE, G_SUB, G_SUBL = 0, 8, 16, 24, 32, 40, 41
        neg_half, neg_lam = sb("neg_half", [P, QB]), sb("neg_lam", [P, 1])
        act_hi, act_lo = sb("act_hi", [P, KB, T], F32R), sb("act_lo", [P, KB, T], F32R)
        w_raw = sb("w_raw", [P, RING, PIECE])
        w_hi, w_lo = sb("w_hi", [P, RING, PIECE], F32R), sb("w_lo", [P, RING, PIECE], F32R)
        hT = sb("hT", [P, KB, T])
        small = sb("small", [P, 64])
        ss_x, sq_x, r_x = small[:, 0:5], small[:, 8:13], small[:, 16:21]
        with ExitStack() as start:
            x_tm = sb("x_tm", [P, QB, D], F32, start)
            x_u = sb("x_u", [P, KB, T], F32, start)
            x_sq = [x_u[:, :, :].rearrange("p k t -> p (k t)")[:, D * t:D * t + D] for t in range(QB - 1)]
            x_sq.append(sb("x_sq", [P, D], F32, start)[:, :])
            gain_rows = sb("gain_rows", [41, P], F32, start)
            lam_in = sb("lam_in", [P, 4, 64], F32, start)
            lam_pr = sb("lam_pr", [P, 2, 64], F32, start)
            lam_s = sb("lam_s", [P, 4], F32, start)
            dist_i = sb("dist_i", [P, TW], I32, start)
            dist = sb("dist", [P, TW], F32, start)
            band_sb = sb("band_sb", [2 * NA, BW], F32, start)
        mid_hi, mid_lo = sb("mid_hi", [P, NB, T], F32R), sb("mid_lo", [P, NB, T], F32R)
        with ExitStack() as branch_a:
            oa_hi, oa_lo = sb("oa_hi", [P, NA, T], F32R, branch_a), sb("oa_lo", [P, NA, T], F32R, branch_a)
            with ExitStack() as att:
                vT, kT, qT = ([], [], [])
                for b in range(2):
                    for name, x in (("vT", vT), ("kT", kT), ("qT", qT)):
                        x.append(sb(f"{name}{b}", [P, T], F32, att))
                k_tm, v_tm = sb("k_tm", [P, QB, P], F32, att), sb("v_tm", [P, QB, P], F32, att)
                ck, cv, ckT = (sb(n, [P, SEQ], F32, att) for n in ("ck", "cv", "ckT"))
                tab_a = [sb(f"tab_a{b}", [P, 2, TW], F32, att) for b in range(2)]
                tab_b = [sb(f"tab_b{b}", [P, TW], F32, att) for b in range(2)]
                prob = [[sb(f"prob{b}{m}", [P, T], F32, att) for m in range(2)] for b in range(2)]
                probT = [sb(f"probT{m}", [P, SEQ], F32, att) for m in range(2)]
                neg_max = sb("neg_max", [P, 2, 2], F32, att)
                sums, r_sum = sb("sums", [P, 2, 2], F32, att), sb("r_sum", [P, 2, 2], F32, att)
                c_map = sb("c_map", [P, 2], F32, att)
                o_tm = [sb(f"o_tm{b}", [P, QB, P], F32, att) for b in range(2)]
                o_sq = sb("o_sq", [P, 2, P], F32, att)
                o_ms = sb("o_ms", [P, 2, QB], F32, att)
                o_r = sb("o_r", [P, QB], F32, att)
            wide = sb("wide", [P, 2 * KB, T], F32, branch_a)
            down_sum, mixed = wide[:, 0:KB], wide[:, KB:2 * KB]
            sq = [sb(f"sq{b}", [P, T], F32, branch_a) for b in range(2)]
            sq_sum = sb("sq_sum", [P, QB * P], F32, branch_a)
            pT_hi, pT_lo = sb("pT_hi", [P, 2, T], F32R, branch_a), sb("pT_lo", [P, 2, T], F32R, branch_a)
            ms_t, r_t = sb("ms_t", [P, QB], F32, branch_a), sb("r_t", [P, QB], F32, branch_a)
            up_raw, y_f = ([mixed[:, m] for m in range(KB)] for _ in range(2))
            with ExitStack() as ple_in:
                p_tm = sb("p_tm", [P, QB, 2 * P], F32, ple_in)
            r_row = sb("r_row", [P, T], F32, branch_a)
            up_t, up_a = sb("up_t", [P, T], F32, branch_a), sb("up_a", [P, T], F32, branch_a)
            y_tm = [sb(f"y_tm{b}", [P, QB, P], F32, branch_a) for b in range(2)]
        ple = sb("ple", [P, KB, T])
        assert KB == 2 * NA

        proj = [ctx.enter_context(nc.psum_tensor(f"proj{b}", [P, 1024], F32)) for b in range(2)]
        score = ctx.enter_context(nc.psum_tensor("score", [P, 1024], F32))
        turn_out = ctx.enter_context(nc.psum_tensor("turn_out", [P, 1024], F32))
        turn, outp = turn_out[:, 0:512], turn_out[:, 512:1024]
        pair = [score, turn_out]
        X_EARLY = KB - 2

        def x_bank(j):
            return (proj[0], proj[1], turn_out)[j % 3 if j < X_EARLY else 2]

        acc = [p[:, :].rearrange("p (h n) -> p h n", h=2)[:, :, 0:HALF] for p in proj]

        def halves(ap):
            return ap.rearrange("p (h n) -> p h n", h=2)

        w_loaded = [sem(f"w_loaded{s}") for s in range(RING)]
        hi_done, lo_done = sem("hi_done"), sem("lo_done")
        w_used = sem("w_used")
        proj_free = [sem(f"proj_free{b}") for b in range(2)]
        x_loaded = [sem(f"x_loaded{t}") for t in range(QB)]
        rows_loaded, lam_loaded, rel_loaded = sem("rows_loaded"), sem("lam_loaded"), sem("rel_loaded")
        band_made = sem("band_made")
        band_kept = [sem("band_kept_first"), sem("band_kept_others")]
        consts, dist_made = sem("consts"), sem("dist_made")
        vec = sem("vec")
        act_own, pool_own = sem("act_own"), sem("pool_own")
        rows_turned, gains_ready = sem("rows_turned"), sem("gains_ready")
        lam_ready, lam_exped = sem("lam_ready"), sem("lam_exped")
        x_squared, x_mean, x_rooted = sem("x_squared"), sem("x_mean"), sem("x_rooted")
        x_turned, x_kept = sem("x_turned"), [sem("x_kept_even"), sem("x_kept_odd")]
        x_row_ready, u_ready, u_hi, u_split = (sem(n) for n in ("x_row_ready", "u_ready", "u_hi", "u_split"))
        tab_loaded = [sem(f"tab_loaded{b}") for b in range(2)]
        tab_ready = sem("tab_ready")
        ck_loaded, cv_loaded, kv_stored = sem("ck_loaded"), sem("cv_loaded"), sem("kv_stored")
        scored, biased, exped, combined = sem("scored"), sem("biased"), sem("exped"), sem("combined")
        turned, turn_free = sem("turned"), sem("turn_free")
        tail_copied, o_hi = sem("tail_copied"), sem("o_hi")
        av_done, out_free = sem("av_done"), sem("out_free")
        o_squared = sem("o_squared")
        o_summed, o_rooted, o_normed = sem("o_summed"), sem("o_rooted"), sem("o_normed")
        early_gates = sem("early_gates")
        br_mixed, m_hi, m_split = sem("br_mixed"), sem("m_hi"), sem("m_split")
        sq_cleared, squared, sq_added = sem("sq_cleared"), sem("squared"), sem("sq_added")
        sum_turned, ms_ready, r_ready = sem("sum_turned"), sem("ms_ready"), sem("r_ready")
        row_ready, row_read = sem("row_ready"), sem("row_read")
        block_normed = sem("block_normed")
        h_added = [sem("h_added_pool"), sem("h_added_vector")]
        h_hi, h_split = sem("h_hi"), sem("h_split")
        down_cleared, up_ready, up_hi, up_split = (sem(n) for n in ("down_cleared", "up_ready", "up_hi", "up_split"))
        p_loaded, p_turned, p_hi, p_split = sem("p_loaded"), sem("p_turned"), sem("p_hi"), sem("p_split")
        ple_first = sem("ple_first")
        y_ready, y_turned, y_copied = sem("y_ready"), sem("y_turned"), sem("y_copied")
        y_stored = [sem(f"y_stored{b}") for b in range(2)]

        block = ctx.enter_context(nc.Block())

        def rows(i):
            return P if i < QB - 1 else SMP

        def keys(i):
            return P * (i + 1) if i < QB - 1 else T

        def n_key_blocks(i):
            return min(i + 1, QB)

        def out_block(x, u, kind, cols):
            n = u if kind == "A" else u + (-NA)
            return x[:, bass.ds(n.value(), 1), cols].rearrange("p a n -> p (a n)")

        def block_of(x, n):
            return x[:, bass.ds(n.value(), 1)].rearrange("p a n -> p (a n)")

        def turn_base(u, kind):
            if kind == "A":
                return u * A_TURNS + (-1) if u.const else u
            return (u + (-NA)) * B_TURNS + TURN_B

        @block.sync
        def _(sp):
            def piece(p, src, shaped=None):
                slot = p.mod(RING)
                at_least(sp, lo_done, p + (1 - RING))
                dst = w_raw[:, slot].rearrange("p (k n) -> p k n", n=shaped or P)
                sp.dma_start(dst, src).then_inc(w_loaded[slot], 16)

            def k_half(w, kh, col, n=P, kblocks=4, row0=0):
                return w[bass.ds(row0 + kh * 512, P * kblocks), bass.ds(col, n)].rearrange(
                    "(k p) n -> p k n", p=P)

            for t in range(QB - 1):
                sp.dma_start(x_tm[:, t], xp[P * t:P * t + P]).then_inc(x_loaded[t], 16)
            sp.dma_start(x_tm[0:SMP, QB - 1], xs_d).then_inc(x_loaded[QB - 1], 16)
            for g, at in ((g_mix_pre, 0), (g_mix_post, 8), (g_ffn_pre, 16), (g_ffn_post, 24), (g_ple, 32)):
                sp.dma_start(gain_rows[at:at + 8], g[0].rearrange("(k p) -> k p", p=P)).then_inc(rows_loaded, 16)
            sp.dma_start(gain_rows[40:41], diff_subln).then_inc(rows_loaded, 16)
            sp.dma_start(band_sb[:, P:BW], rev[:, 0:2 * REL]).then_inc(rel_loaded, 16)

            def two_tasks(p0, w, cols):
                for kh in range(2):
                    for j in range(2):
                        piece(Count(p0 + 2 * kh + j), k_half(w, kh, cols[j]))

            def unit_pieces(u0, u, cols):
                for n, base in enumerate(cols):
                    for kh in range(2):
                        piece(u * 6 + (2 * n + kh), k_half(w_in[0], kh, ((u + (-u0)) * P + base).value()))

            a_cols = (2 * AW, AW, 0)
            b_cols = (3 * AW + 2 * NB * P, 3 * AW + NB * P, 3 * AW)
            two_tasks(0, w_in[0], a_cols[0:2])
            for kh in range(2):
                piece(Count(4 + kh), k_half(w_in[0], kh, a_cols[2]))
            sp.dma_start(lam_in[:, :, :], bass.AP(diff_lambda.tensor, 0, [[0, P], [64, 4], [1, 64]])).then_inc(lam_loaded, 16)
            sp.wait_ge(band_made, 1)
            for u in range(NA):
                sp.dma_start(band[2 * u:2 * u + 2], band_sb[2 * u:2 * u + 2].unsqueeze(1).broadcast_to([2, P, BW])
                             ).then_inc(band_kept[min(u, 1)], 16)
            with sp.Fori(0, (NA - 2) // 2) as it:
                for v in range(2):
                    unit_pieces(0, Count(1 + v, [(it, 2)]), a_cols)
            unit_pieces(0, Count(NA - 1), a_cols)
            with sp.Fori(0, NB // 2) as it:
                for v in range(2):
                    unit_pieces(NA, Count(NA + v, [(it, 2)]), b_cols)

            def stage(p0, w, n, kblocks=4, halves_=2):
                per = RING // halves_
                with sp.Fori(0, n // per) as it:
                    for j in range(per):
                        for kh in range(halves_):
                            piece(Count(p0 + j * halves_ + kh, [(it, RING)]),
                                  k_half(w, kh, Count(P * j, [(it, P * per)]).value()))

            stage(PC_GATE, w_gate[0], 2 * KB)
            sp.wait_ge(av_done, NU * QB)
            sp.dma_start(p_tm[:, 0:QB - 1], p_prompt[0, 0].rearrange("(j p) n -> p j n", p=P)).then_inc(p_loaded, 16)
            sp.dma_start(p_tm[0:SMP, QB - 1], p_sample[0, 0]).then_inc(p_loaded, 16)
            stage(PC_BRA, w_branch_a[0], KB, halves_=1)
            stage(PC_BRB, w_branch_b[0], KB)
            stage(PC_OUT, w_out[0], KB)

            def ple_pieces(half):
                for n in range(KB // 4):
                    col = 2 * P * (half * (KB // 4) + n)
                    piece(Count(PC_PLE[half] + n), k_half(w_ple[0], 0, col, n=2 * P, kblocks=2), shaped=2 * P)

            def blocks(p0, w, first, n, group=Count(0), col=0, row=0):
                with sp.Fori(0, n // 2) as it:
                    for j in range(2):
                        for kh in range(2):
                            piece(group * (4 * KB) + Count(p0 + 2 * j + kh, [(it, RING)]),
                                  k_half(w, kh, (group * col + Count(P * (first + j), [(it, 2 * P)])).value(),
                                         row0=(group * row).value()))

            ple_pieces(0)
            two_tasks(PC_FF, w_up[0], (0, P))
            blocks(PC_FF + 4, w_up[0], 2, KB - 2)
            blocks(PC_FF + 2 * KB, w_down[0], 0, KB)
            with sp.Fori(1, FG) as g:
                blocks(PC_FF, w_up[0], 0, KB, Count(0, [(g, 1)]), col=D)
                blocks(PC_FF + 2 * KB, w_down[0], 0, KB, Count(0, [(g, 1)]), row=D)
            ple_pieces(1)
            two_tasks(PC_PG, w_ple_gate[0], (0, P))
            blocks(PC_PG + 4, w_ple_gate[0], 2, KB - 2)
            for m in range(KB):
                sp.wait_ge(y_copied, m + 1)
                yt, cols = y_tm[m % 2], slice(P * m, P * m + P)
                sp.dma_start(y_prompt[0, :, cols].rearrange("(j p) n -> p j n", p=P),
                             yt[:, 0:QB - 1]).then_inc(y_stored[m % 2], 16)
                sp.dma_start(y_sample[0, :, cols], yt[0:SMP, QB - 1]).then_inc(y_stored[m % 2], 16)
            for b in range(2):
                sp.wait_ge(y_stored[b], 32 * KB // 2)
            sp.wait_ge(kv_stored, 64 * NU)

        @block.gpsimd
        def _(pool):
            def lo_part(p):
                slot = p.mod(RING)
                at_least(pool, hi_done, p + 1)
                pool.tensor_tensor(w_lo[:, slot], w_raw[:, slot], w_hi[:, slot].bitcast(F32),
                                   ALU.subtract).then_inc(lo_done, 1)

            def load_table(u):
                src = bass.AP(band.tensor, 2 * u * P * BW + P, [[BW - 1, P], [P * BW, 2], [1, 2 * REL]])
                pool.dma_start(tab_a[u % 2][:, :, TW - 2 * REL:TW], src).then_inc(tab_loaded[u % 2], 16)

            def finish_table(u):
                pool.wait_ge(tab_loaded[u % 2], 16 * (u // 2 + 1))
                tab, flat = tab_a[u % 2], TW - 2 * REL
                pool.tensor_copy(tab[:, :, 0:flat], tab[:, :, flat:flat + 1].broadcast_to([P, 2, flat])).then_inc(pool_own, 1)
                pool.wait_ge(pool_own, u + 3)
                pool.memset(tab[0:SMP, :, TW - SMP:TW], MASK).then_inc(tab_ready, 1)

            pool.memset(ident[:, :], 0.0).then_inc(pool_own, 1)
            pool.memset(ones[:, :], 1.0)
            pool.memset(neg_half[:, :], -0.5).then_inc(pool_own, 1)
            pool.iota(dist_i[:, :], [[-1, TW]], base=SEQ, channel_multiplier=1).then_inc(dist_made, 1)
            pool.wait_ge(pool_own, 2)
            pool.affine_select(out=ident[:, :], in_=ident[:, :], compare_op=ALU.not_equal, fill=1.0,
                               base=0, pattern=[[-1, P]], channel_multiplier=1).then_inc(consts, 1)
            for t in range(QB):
                n = rows(t)
                pool.wait_ge(x_mean, t + 1)
                pool.tensor_tensor(r_x[0:n, t:t + 1], sq_x[0:n, t:t + 1], neg_half[0:n, 0:1], ALU.pow).then_inc(x_rooted, 1)
            for p in range(RING):
                lo_part(Count(p))
            pool.dma_start(ck[:, :].rearrange("p (j n) -> p j n", n=P), cak[:, 0:P].rearrange("(j p) n -> p j n", p=P)).then_inc(ck_loaded, 16)
            pool.dma_start(cv[:, :].rearrange("p (j n) -> p j n", n=P), cav[:, 0:P].rearrange("(j p) n -> p j n", p=P)).then_inc(cv_loaded, 16)
            for u in range(2):
                pool.wait_ge(band_kept[u], (1, NA - 1)[u] * 16)
                load_table(u)
            finish_table(0)
            for n in range(2):
                lo_part(Count(RING + n))
            finish_table(1)
            for n in range(2, 6):
                lo_part(Count(RING + n))

            def unit(u, kind, next_kind, par, prev):
                steps = A_STEPS if kind == "A" else B_STEPS
                turns = turn_base(u, kind)
                cols = ((u + (0 if kind == "A" else -NA)) * P).value()
                outs = out_a if kind == "A" else out_b
                for name, arg, t in walk(steps, prev is not None):
                    if name == "k" and arg % 4 == 3:
                        lo_part((u + 1) * 6 + (arg // 4 + RING))
                    elif name == "V4" and prev == "B":
                        at_least(pool, o_summed, u + (-NA))
                        pool.tensor_tensor(o_r[:, :], o_ms[:, 1 - par], neg_half[:, :], ALU.pow).then_inc(o_rooted, 1)
                    elif name == "Tail":
                        at_least_alone(pool, turn_free, turns + (t + 1))
                        for src, dst_p, dst_s in ((k_tm, outs[0], outs[2]), (v_tm, outs[1], outs[3])):
                            pool.dma_start(dst_p[:, bass.ds(cols, P)].rearrange("(j p) n -> p j n", p=P),
                                           src[:, 0:QB - 1]).then_inc(kv_stored, 16)
                            pool.dma_start(dst_s[:, bass.ds(cols, P)], src[0:SMP, QB - 1]).then_inc(kv_stored, 16)
                    elif name == "CK" and next_kind:
                        at_least_alone(pool, turned, turns + (t + 1))
                        c = cak if next_kind == "A" else cbk
                        col = ((u + (1 if next_kind == "A" else 1 - NA)) * P).value()
                        pool.dma_start(ck[:, :].rearrange("p (j n) -> p j n", n=P),
                                       c[:, bass.ds(col, P)].rearrange("(j p) n -> p j n", p=P)).then_inc(ck_loaded, 16)
                if next_kind:
                    at_least_alone(pool, av_done, (u + 1) * QB)
                    c = cav if next_kind == "A" else cbv
                    col = ((u + (1 if next_kind == "A" else 1 - NA)) * P).value()
                    pool.dma_start(cv[:, :].rearrange("p (j n) -> p j n", n=P),
                                   c[:, bass.ds(col, P)].rearrange("(j p) n -> p j n", p=P)).then_inc(cv_loaded, 16)

            for u in range(NA):
                if u >= 1 and u + 1 < NA:
                    finish_table(u + 1)
                unit(Count(u), "A", "A" if u + 1 < NA else "B", u % 2, "A" if u else None)
                if u + 2 < NA:
                    pool.wait_ge(biased, 10 * (u + 1))
                    load_table(u + 2)

            def b_unit(u, par, next_kind="B", prev="B"):
                if next_kind:
                    at_least(pool, tab_ready, u)
                    at_least_alone(pool, biased, u * 10)
                    pool.tensor_scalar(tab_b[1 - par][:, :], tab_b[par][:, :], 0.5, None, ALU.mult).then_inc(tab_ready, 1)
                unit(u, "B", next_kind, par, prev)

            b_unit(Count(NA), 0, prev="A")
            b_unit(Count(NA + 1), 1)
            with pool.Fori(0, (NB - 4) // 2) as it:
                for v in range(2):
                    b_unit(Count(NA + 2 + v, [(it, 2)]), v)
            b_unit(Count(NU - 2), 0)
            b_unit(Count(NU - 1), 1, next_kind=None)
            pool.wait_ge(o_summed, NB)
            pool.tensor_tensor(o_r[:, :], o_ms[:, 1], neg_half[:, :], ALU.pow).then_inc(o_rooted, 1)

            def root(n):
                pool.wait_ge(ms_ready, n + 1)
                pool.tensor_tensor(r_t[:, :], ms_t[:, :], neg_half[:, :], ALU.pow).then_inc(r_ready, 1)

            def split(p0, end):
                loops = (end - p0) // RING
                if loops > 1:
                    with pool.Fori(0, loops) as it:
                        for j in range(RING):
                            lo_part(Count(p0 + j, [(it, RING)]))
                    p0 += loops * RING
                for p in range(p0, end):
                    lo_part(Count(p))

            def update(n, x):
                for k in BY_POOL:
                    if k == BY_POOL[2]:
                        split((PC_FF, PC_PG)[n] + 2, (PC_FF, PC_PG)[n] + RING)
                    pool.wait_ge(block_normed, n * KB + k + 1)
                    pool.tensor_tensor(hT[:, k], hT[:, k], x[:, k], ALU.add).then_inc(h_added[0], 1)

            split(PC_GATE + 6 + RING, PC_OUT + 2 * RING)
            pool.wait_ge(m_hi, KB)
            pool.memset(down_sum, 0.0).then_inc(down_cleared, 1)
            split(PC_OUT + 2 * RING, PC_FF + 2)
            root(N_POST)
            update(0, mixed)
            split(PC_FF + RING, PC_FF + RING + 4)
            root(N_FPRE)
            split(PC_FF + RING + 4, PC_PG + 2)
            root(N_FPOST)
            update(1, down_sum)
            split(PC_PG + RING, PC_PG + RING + 4)
            root(N_PLE)
            split(PC_PG + RING + 4, PC_END)

        @block.scalar
        def _(act):
            def hi_part(p):
                slot = p.mod(RING)
                at_least(act, w_loaded[slot], (p.over(RING) + 1) * 16)
                at_least(act, w_used, p + (1 - RING))
                act.activation(w_hi[:, slot], w_raw[:, slot], ACT.Copy).then_inc(hi_done, 1)

            def square_x(t):
                act.wait_ge(x_loaded[t], 16)
                n = rows(t)
                act.activation(x_sq[t][0:n], x_tm[0:n, t], ACT.Square, accum_out=ss_x[0:n, t:t + 1]).then_inc(x_squared, 1)

            for t in range(QB):
                square_x(t)
            def keep_x(j):
                act.wait_ge(x_turned, j + 1)
                act.activation(hT[:, j], x_bank(j)[:, 0:T], ACT.Copy).then_inc(x_kept[1], 1)

            for j in (1, 3):
                keep_x(j)
                hi_part(Count(j // 2))
            for k in range(KB):
                if k == 1:
                    keep_x(X_EARLY - 1)
                if k == KB // 2:
                    keep_x(KB - 1)
                if k in (2, 3):
                    hi_part(Count(k))
                if k == KB - 1:
                    hi_part(Count(RING))
                    hi_part(Count(RING + 1))
                act.wait_ge(u_ready, k + 1)
                act.activation(act_hi[:, k], x_u[:, k], ACT.Copy).then_inc(u_hi, 1)
            act.wait_ge(lam_ready, 1)
            act.activation(lam_s[:, 2:4], lam_s[:, 0:2], ACT.Exp).then_inc(lam_exped, 1)
            for n in range(2, 6):
                hi_part(Count(RING + n))

            def unit(u, kind, par, prev):
                steps = A_STEPS if kind == "A" else B_STEPS
                turns = turn_base(u, kind)

                def expo(i, m):
                    n, np_, b = keys(i), rows(i), i % 2
                    at_least(act, biased, u * 10 + (2 * i + m + 1))
                    act.activation(prob[b][m][0:np_, 0:n], prob[b][m][0:np_, 0:n], ACT.Exp, scale=-1.0,
                                   bias=neg_max[0:np_, b, m:m + 1],
                                   accum_out=sums[0:np_, b, m:m + 1]).then_inc(exped, 1)

                def square_output(i):
                    np_ = rows(i)
                    at_least(act, out_free, u * QB + (i + 1))
                    act.activation(o_sq[0:np_, i % 2], o_tm[par][0:np_, i], ACT.Square,
                                   accum_out=o_ms[0:np_, par, i:i + 1]).then_inc(o_squared, 1)

                for name, arg, t in walk(steps, prev is not None):
                    if name == "AV" and kind == "B" and arg:
                        square_output(arg - 1)
                    if name == "k" and arg % 4 == 3:
                        hi_part((u + 1) * 6 + (arg // 4 + RING))
                    elif name == "S":
                        expo(arg, 0)
                        expo(arg, 1)
                    elif name in ("Sa", "Sb"):
                        expo(arg, int(name == "Sb"))
                    elif name == "T":
                        i, m = arg
                        at_least(act, turned, turns + (t + 1))
                        if i < QB - 1:
                            act.activation(probT[m][:, 0:P * (i + 1)], turn[:, 0:P * (i + 1)], ACT.Copy).then_inc(turn_free, 1)
                        else:
                            act.activation(probT[m][:, 0:4 * SMP], turn[:, 0:4 * SMP], ACT.Copy)
                            act.activation(probT[m][0:SMP, 4 * SMP:5 * SMP], turn[0:SMP, 4 * SMP:5 * SMP],
                                           ACT.Copy).then_inc(turn_free, 1)
                    elif name in ("V4", "K4"):
                        at_least(act, turned, turns + (t + 1))
                        at_least(act, kv_stored, u * 64)
                        dst = v_tm if name == "V4" else k_tm
                        act.activation(dst[:, 0:QB - 1].rearrange("p j n -> p (j n)"), turn[:, 0:SEQ], ACT.Copy).then_inc(turn_free, 1)
                    elif name == "CK":
                        at_least(act, turned, turns + (t + 1))
                        act.activation(ckT[:, :], turn[:, 0:SEQ], ACT.Copy).then_inc(turn_free, 1)
                    elif name == "OT":
                        at_least(act, turned, turns + (t + 1))
                        out_hi(u + (-1), prev, turn[:, 0:SEQ], slice(0, SEQ))
                    elif name == "Tail" and prev is not None:
                        at_least(act, tail_copied, u)
                        out_hi(u + (-1), prev, turn[:, 2 * P:2 * P + SMP], slice(SEQ, T))
                if kind == "B":
                    square_output(QB - 1)

            def out_hi(u, kind, src, cols):
                dst = out_block(oa_hi if kind == "A" else mid_hi, u, kind, cols)
                if kind == "A":
                    act.activation(dst, src, ACT.Copy).then_inc(o_hi, 1)
                else:
                    act.activation(dst, src, ACT.Copy, scale=gcol[:, G_SUBL:G_SUBL + 1]).then_inc(o_hi, 1)

            for u in range(NA):
                unit(Count(u), "A", u % 2, "A" if u else None)
            unit(Count(NA), "B", 0, "A")
            unit(Count(NA + 1), "B", 1, "B")
            with act.Fori(0, (NB - 4) // 2) as it:
                for v in range(2):
                    unit(Count(NA + 2 + v, [(it, 2)]), "B", v, "B")
            unit(Count(NU - 2), "B", 0, "B")
            unit(Count(NU - 1), "B", 1, "B")

            def gate(n, p):
                for kh in range(2):
                    hi_part(p + (kh + RING))
                at_least(act, w_used, p + 2)
                b = (n + PJ_GATE).mod(2)
                act.activation(halves(block_of(wide, n)), acc[b], ACT.Sigmoid).then_inc(proj_free[b], 1)

            act.wait_ge(av_done, NU * QB)
            act.wait_ge(out_free, NU * QB)
            act.wait_ge(o_summed, NB)
            gate(Count(3), Count(PC_GATE + 6))
            act.wait_ge(proj_free[(PJ_GATE + 2) % 2], (PJ_GATE + 2) // 2 + 1)
            for n in range(3):
                act.activation(wide[:, n], (vT, kT, qT)[n][0][:, :], ACT.Sigmoid).then_inc(early_gates, 1)
            gate(Count(4), Count(PC_GATE + 8))
            act.wait_ge(turned, TURN_END + 1)
            out_hi(Count(NU - 1), "B", turn[:, 0:SEQ], slice(0, SEQ))
            act.wait_ge(turned, TURN_END + 2)
            out_hi(Count(NU - 1), "B", turn[:, 2 * P:2 * P + SMP], slice(SEQ, T))
            act.wait_ge(kv_stored, 64 * NU)
            gate(Count(5), Count(PC_GATE + 10))
            with act.Fori(0, KB - 3) as it:
                for j in range(2):
                    gate(Count(6 + j, [(it, 2)]), Count(PC_GATE + 12 + 2 * j, [(it, 4)]))
            for k in range(2):
                act.wait_ge(p_turned, k + 1)
                act.activation(pT_hi[:, k], pair[k][:, 0:T], ACT.Copy).then_inc(p_hi, 1)
            with act.Fori(0, KB // RING) as it:
                for j in range(RING):
                    hi_part(Count(PC_BRA + RING + j, [(it, RING)]))
            with act.Fori(0, KB // 2) as it:
                for j in range(2):
                    n = Count(j, [(it, 2)])
                    for kh in range(2):
                        hi_part(Count(PC_BRB + RING + 2 * j + kh, [(it, RING)]))
                    at_least(act, br_mixed, n + 1)
                    act.activation(block_of(act_hi, n), block_of(wide, n), ACT.Copy).then_inc(m_hi, 1)

            def square(n, src):
                at_least(act, sq_added, Count(n - 1))
                act.activation(sq[n % 2][:, :], src, ACT.Square).then_inc(squared, 1)

            def keep_ple(half, i):
                act.wait_ge(*((w_used, PC_PLE[half] + i // 2 + 1) if i % 2 else (ple_first, half * (KB // 4) + i // 2 + 1)))
                b = (PJ_PLE[half] + i) % 2
                act.activation(halves(ple[:, half * (KB // 2) + i]), acc[b], ACT.Copy).then_inc(proj_free[b], 1)

            for m in range(KB):
                for kh in range(2):
                    hi_part(Count(PC_OUT + RING + 2 * m + kh))
                act.wait_ge(proj_free[(PJ_OUT + m) % 2], (PJ_OUT + m) // 2 + 1)
                square(m, mixed[:, m])

            def next_input(n, scale):
                p = (PC_FF, PC_PG)[n]
                for k in range(KB):
                    if k == 1:
                        keep_ple(n, KB // 2 - 1)
                        hi_part(Count(PC_PLE[n] + RING + 1))
                    if k == KB - 1:
                        hi_part(Count(p + RING))
                        hi_part(Count(p + RING + 1))
                    for done_by, added in ((BY_POOL, h_added[0]), (BY_VECTOR, h_added[1])):
                        if k in done_by:
                            act.wait_ge(added, n * len(done_by) + done_by.index(k) + 1)
                    if scale is None:
                        act.activation(act_hi[:, k], hT[:, k], ACT.Copy).then_inc(h_hi, 1)
                    else:
                        act.activation(act_hi[:, k], hT[:, k], ACT.Copy, scale=gcol[:, scale + k:scale + k + 1]).then_inc(h_hi, 1)

            for i in range(KB // 2 - 1):
                keep_ple(0, i)
                if i % 2:
                    hi_part(Count(PC_PLE[0] + RING + i // 2))
            next_input(0, G_FPRE)

            def up_hi_part(n, count):
                at_least(act, up_ready, count)
                act.activation(block_of(mid_hi, n), up_a[:, :], ACT.Copy).then_inc(up_hi, 1)

            def keep_up(j):
                act.wait_ge(w_used, PC_FF + (3 + j if j < 2 else 2 * j + 2))
                b = (PJ_FF + j) % 2
                act.activation(halves(up_raw[j]), acc[b], ACT.Copy).then_inc(proj_free[b], 1)

            for j in range(2):
                keep_up(j)
                hi_part(Count(PC_FF + RING + 2 + j))
            for k in range(KB):
                square(KB + k, hT[:, k])
            for j in range(2, KB):
                for kh in range(2):
                    hi_part(Count(PC_FF + RING + 2 * j + kh))
                if j < RAW:
                    keep_up(j)
                for i in range(2 * j - RAW, 2 * j - RAW + 2) if RAW // 2 <= j < RAW else (j,) if j >= RAW else ():
                    up_hi_part(Count(i), Count(i + 1))

            def up_group(group):
                with act.Fori(0, KB // 2) as it:
                    for j in range(2):
                        for kh in range(2):
                            hi_part(group * (4 * KB) + Count(PC_FF + RING + 2 * j + kh, [(it, RING)]))
                        up_hi_part(Count(j, [(it, 2)]), group * KB + Count(j + 1, [(it, 2)]))

            def down_group(group):
                with act.Fori(0, KB // 2) as it:
                    for j in range(RING):
                        hi_part(group * (4 * KB) + Count(PC_FF + 2 * KB + RING + j, [(it, RING)]))

            down_group(Count(0))
            with act.Fori(1, FG - 1) as g:
                up_group(Count(0, [(g, 1)]))
                down_group(Count(0, [(g, 1)]))
            last_piece = PC_FF + (FG - 1) * 4 * KB
            up_group(Count(FG - 1))
            for k in range(KB):
                for kh in range(2):
                    hi_part(Count(last_piece + 2 * KB + RING + 2 * k + kh))
                job = PJ_FF + (FG - 1) * 2 * KB + KB + k
                act.wait_ge(proj_free[job % 2], job // 2 + 1)
                square(2 * KB + k, down_sum[:, k])
            for i in range(KB // 2 - 1):
                keep_ple(1, i)
                if i % 2:
                    hi_part(Count(PC_PLE[1] + RING + i // 2))
            next_input(1, None)

            def y_rows(m):
                act.wait_ge(y_turned, m + 1)
                if m >= 2:
                    act.wait_ge(y_stored[m % 2], 32 * (m // 2))
                act.activation(y_tm[m % 2][:, 0:QB - 1], pair[m % 2][:, 0:SEQ].rearrange("p (j n) -> p j n", n=P), ACT.Copy)
                act.activation(y_tm[m % 2][0:SMP, QB - 1], pair[m % 2][0:SMP, SEQ:SEQ + P], ACT.Copy).then_inc(y_copied, 1)

            def gate_ple(m):
                act.wait_ge(w_used, PC_PG + (3 + m if m < 2 else 2 * m + 2))
                b = (PJ_PG + m) % 2
                act.activation(halves(y_f[m]), acc[b], ACT.Sigmoid).then_inc(proj_free[b], 1)

            for m in range(2):
                gate_ple(m)
                hi_part(Count(PC_PG + RING + 2 + m))
            for k in range(KB):
                square(3 * KB + k, ple[:, k])
            for m in range(2, KB):
                for kh in range(2):
                    if PC_PG + RING + 2 * m + kh < PC_END:
                        hi_part(Count(PC_PG + RING + 2 * m + kh))
                gate_ple(m)
                for i in Y_AFTER[m]:
                    y_rows(i)

        @block.vector
        def _(dve):
            own = [Count(0)]

            def done(ins):
                ins.then_inc(vec, 1)
                own[0] = own[0] + 1

            def settle():
                at_least(dve, vec, own[0])

            def loop(n, per):
                start = own[0]

                def enter(register):
                    own[0] = start + Count(0, [(register, per)])

                def leave(register):
                    got = own[0].const - start.const
                    assert got == per, got
                    own[0] = start + per * n
                return enter, leave

            for b in range(2):
                dve.memset(o_tm[b][SMP:P, QB - 1], 0.0)
                dve.memset(o_ms[SMP:P, b, QB - 1:QB], 0.0)
            for t in range(QB):
                n = rows(t)
                dve.wait_ge(x_squared, t + 1)
                dve.tensor_scalar(sq_x[0:n, t:t + 1], ss_x[0:n, t:t + 1], 1.0 / D, EPS, ALU.mult, ALU.add).then_inc(x_mean, 1)

            def keep_x(j):
                dve.wait_ge(x_turned, j + 1)
                dve.tensor_copy(hT[:, j], x_bank(j)[:, 0:T]).then_inc(x_kept[0], 1)

            for j in range(0, X_EARLY, 2):
                keep_x(j)
            dve.wait_ge(rows_turned, 1)
            done(dve.tensor_copy(gcol[:, 0:41], score[:, 0:41]))
            settle()
            dve.tensor_scalar(gcol[:, G_SUBL:G_SUBL + 1], gcol[:, G_SUB:G_SUB + 1], 1.0 - LAM0, None,
                              ALU.mult).then_inc(gains_ready, 1)
            dve.wait_ge(x_row_ready, 1)
            for k in range(KB + 1):
                if k == KB // 2:
                    keep_x(X_EARLY)
                if k < KB:
                    dve.wait_ge(x_kept[k % 2], k // 2 + 1)
                    dve.scalar_tensor_tensor(out=x_u[:, k], in0=hT[:, k], scalar=gcol[:, G_PRE + k:G_PRE + k + 1],
                                             in1=score[:, 0:T], op0=ALU.mult, op1=ALU.mult).then_inc(u_ready, 1)
                if k:
                    dve.wait_ge(u_hi, k)
                    dve.tensor_tensor(act_lo[:, k - 1], x_u[:, k - 1], act_hi[:, k - 1].bitcast(F32),
                                      ALU.subtract).then_inc(u_split, 1)
                if k == 1:
                    dve.wait_ge(rel_loaded, 16)
                    dve.tensor_copy(band_sb[:, 0:P], band_sb[:, P:P + 1].broadcast_to([2 * NA, P])).then_inc(band_made, 1)
            dve.wait_ge(lam_loaded, 16)
            done(dve.tensor_tensor(lam_pr[:, 0], lam_in[:, 0], lam_in[:, 1], ALU.mult))
            done(dve.tensor_tensor(lam_pr[:, 1], lam_in[:, 2], lam_in[:, 3], ALU.mult))
            settle()
            dve.tensor_reduce(lam_s[:, 0:2], lam_pr[:, :, :], AX.X, ALU.add).then_inc(lam_ready, 1)
            dve.wait_ge(dist_made, 1)
            done(dve.tensor_copy(dist[:, :], dist_i[:, :]))
            settle()
            done(dve.scalar_tensor_tensor(out=tab_b[0][:, :], in0=dist[:, :], scalar=-1.0, in1=dist[:, :],
                                          op0=ALU.mult, op1=ALU.max))
            settle()
            done(dve.memset(tab_b[0][0:SMP, TW - SMP:TW], -2e2 * MASK))
            settle()
            done(dve.tensor_scalar(tab_b[0][:, :], tab_b[0][:, :], -0.5, None, ALU.mult))
            dve.wait_ge(lam_exped, 1)
            done(dve.tensor_tensor(lam_s[:, 0:1], lam_s[:, 3:4], lam_s[:, 2:3], ALU.subtract))
            settle()
            done(dve.tensor_scalar(neg_lam[:, :], lam_s[:, 0:1], -LAM0, None, ALU.add))

            def projected(u, n, gates=False, pieces=None):
                b = (u * 3 + (PJ_IN + n)).mod(2)
                par = u.mod(2)
                at_least(dve, w_used, u * 6 + (pieces or 2 * n + 2))
                dst = (vT, kT, qT)[n][par][:, :]
                if n < 2 or gates:
                    dve.tensor_copy(halves(dst), acc[b]).then_inc(proj_free[b], 1)
                else:
                    dve.tensor_scalar(halves(dst), acc[b], 0.125, None, ALU.mult).then_inc(proj_free[b], 1)

            for n in range(3):
                projected(Count(0), n, pieces=3 + n + n // 2)

            def unit(u, kind, par, prev):
                steps = A_STEPS if kind == "A" else B_STEPS
                turns = turn_base(u, kind)

                def bias(i, m):
                    n, np_, b = keys(i), rows(i), i % 2
                    at_least_alone(dve, scored, u * 10 + (2 * i + m + 1))
                    tab = tab_a[par][:, m] if kind == "A" else tab_b[par][:, :]
                    tab = tab[:, TW - n:TW] if i < QB - 1 else tab[0:np_, 0:n]
                    src = score[0:np_, 512 * m:512 * m + n] if i < QB - 1 else score[0:np_, 0:n]
                    dve.tensor_tensor_reduce(prob[b][m][0:np_, 0:n], src, tab, -1.0, 3e38, ALU.add, ALU.min,
                                             neg_max[0:np_, b, m:m + 1]).then_inc(biased, 1)

                for name, arg, t in walk(steps, prev is not None):
                    if name == "k" and arg % 8 == 7:
                        projected(u + 1, arg // 8, u.const == NU - 1)
                    elif name == "S":
                        if arg == 0:
                            at_least(dve, tab_ready, u + int(kind == "A"))
                        bias(arg, 0)
                        bias(arg, 1)
                    elif name in ("Sa", "Sb"):
                        bias(arg, int(name == "Sb"))
                    elif name == "Tail":
                        at_least(dve, turned, turns + (t + 1))
                        dve.tensor_copy(v_tm[0:SMP, QB - 1], turn[0:SMP, 0:P])
                        if prev is None:
                            dve.tensor_copy(k_tm[0:SMP, QB - 1], turn[0:SMP, P:2 * P]).then_inc(turn_free, 1)
                        else:
                            dve.tensor_copy(k_tm[0:SMP, QB - 1], turn[0:SMP, P:2 * P]).then_inc(tail_copied, 1)
                            at_least(dve, o_hi, u * 2)
                            out_lo(u + (-1), prev, turn[:, 2 * P:2 * P + SMP], slice(SEQ, T))
                    elif name == "OT":
                        if prev == "B":
                            normalise(u + (-1), 1 - par)
                        at_least(dve, o_hi, u * 2 + (-1))
                        out_lo(u + (-1), prev, turn[:, 0:SEQ], slice(0, SEQ))
                    elif name == "C":
                        i, b, np_ = arg, arg % 2, rows(arg)
                        at_least(dve, out_free, u * QB + max(i - 1, 0))
                        at_least(dve, exped, u * 10 + (2 * i + 2))
                        done(dve.reciprocal(r_sum[0:np_, b], sums[0:np_, b]))
                        settle()
                        done(dve.scalar_tensor_tensor(out=c_map[0:np_, b:b + 1], in0=sums[0:np_, b, 0:1],
                                                      scalar=r_sum[0:np_, b, 1:2], in1=neg_lam[0:np_, :],
                                                      op0=ALU.mult, op1=ALU.mult))
                        settle()
                        n = keys(i)
                        dve.scalar_tensor_tensor(out=prob[b][0][0:np_, 0:n], in0=prob[b][1][0:np_, 0:n],
                                                 scalar=c_map[0:np_, b:b + 1], in1=prob[b][0][0:np_, 0:n],
                                                 op0=ALU.mult, op1=ALU.add).then_inc(combined, 1)
                    elif name == "AV":
                        i, b, np_ = arg, arg % 2, rows(arg)
                        if kind == "A":
                            at_least(dve, exped, u * 10 + (2 * i + 2))
                            done(dve.reciprocal(r_sum[0:np_, b], sums[0:np_, b]))
                            settle()
                            at_least(dve, av_done, u * QB + (i + 1))
                            for m in range(2):
                                last = dve.tensor_scalar(o_tm[par][0:np_, i, 64 * m:64 * m + 64], outp[0:np_, 64 * m:64 * m + 64],
                                                         r_sum[0:np_, b, m:m + 1], None, ALU.mult)
                            last.then_inc(out_free, 1)
                        else:
                            at_least(dve, av_done, u * QB + (i + 1))
                            dve.tensor_scalar(o_tm[par][0:np_, i], outp[0:np_, 0:P], r_sum[0:np_, b, 0:1], None,
                                              ALU.mult).then_inc(out_free, 1)
                if kind == "B":
                    at_least(dve, o_squared, (u + (1 - NA)) * QB)
                    dve.tensor_scalar(o_ms[:, par], o_ms[:, par], 1.0 / P, EPS, ALU.mult, ALU.add).then_inc(o_summed, 1)

            def normalise(u, par):
                at_least(dve, o_rooted, u + (1 - NA))
                dve.tensor_tensor(o_tm[par][:, :, :], o_tm[par][:, :, :], o_r[:, :].unsqueeze(2).broadcast_to([P, QB, P]),
                                  ALU.mult).then_inc(o_normed, 1)

            def out_lo(u, kind, src, cols):
                hi, lo = (oa_hi, oa_lo) if kind == "A" else (mid_hi, mid_lo)
                hi, lo = out_block(hi, u, kind, cols).bitcast(F32), out_block(lo, u, kind, cols)
                if kind == "A":
                    dve.tensor_tensor(lo, src, hi, ALU.subtract).then_inc(turn_free, 1)
                else:
                    dve.scalar_tensor_tensor(out=lo, in0=src, scalar=gcol[:, G_SUBL:G_SUBL + 1], in1=hi,
                                             op0=ALU.mult, op1=ALU.subtract).then_inc(turn_free, 1)

            for u in range(NA):
                unit(Count(u), "A", u % 2, "A" if u else None)
            unit(Count(NA), "B", 0, "A")
            unit(Count(NA + 1), "B", 1, "B")
            enter, leave = loop((NB - 4) // 2, 2 * 2 * QB)
            with dve.Fori(0, (NB - 4) // 2) as it:
                enter(it)
                for v in range(2):
                    unit(Count(NA + 2 + v, [(it, 2)]), "B", v, "B")
                leave(it)
            unit(Count(NU - 2), "B", 0, "B")
            unit(Count(NU - 1), "B", 1, "B")
            normalise(Count(NU - 1), 1)
            dve.wait_ge(o_hi, 2 * NU - 1)
            out_lo(Count(NU - 1), "B", turn[:, 0:SEQ], slice(0, SEQ))
            dve.wait_ge(o_hi, 2 * NU)
            out_lo(Count(NU - 1), "B", turn[:, 2 * P:2 * P + SMP], slice(SEQ, T))
            for k in range(2):
                dve.wait_ge(p_hi, k + 1)
                dve.tensor_tensor(pT_lo[:, k], pair[k][:, 0:T], pT_hi[:, k].bitcast(F32), ALU.subtract).then_inc(p_split, 1)
            dve.memset(sq_sum[:, T:QB * P], 0.0).then_inc(sq_cleared, 1)

            dve.wait_ge(early_gates, 3)
            with dve.Fori(0, KB // RING) as it:
                for j in range(RING):
                    at_least(dve, w_used, Count(PC_BRA + j + 1, [(it, RING)]))
                    b = (PJ_BRA + j) % 2
                    w = block_of(wide, Count(j, [(it, RING)]))
                    dve.tensor_tensor(halves(w), acc[b], halves(w), ALU.mult).then_inc(proj_free[b], 1)
            with dve.Fori(0, KB // 2) as it:
                for j in range(2):
                    n = Count(j, [(it, 2)])
                    at_least(dve, w_used, Count(PC_BRB + 2 * j + 2, [(it, RING)]))
                    b = (PJ_BRB + j) % 2
                    wa, wb = block_of(wide, n), block_of(wide, n + KB)
                    dve.tensor_tensor(halves(wb), acc[b], halves(wb), ALU.mult).then_inc(proj_free[b], 1)
                    at_least(dve, proj_free[b], Count((PJ_BRB + j) // 2 + 1, [(it, 1)]))
                    dve.tensor_tensor(wa, wa, wb, ALU.add).then_inc(br_mixed, 1)
                    at_least(dve, m_hi, n + 1)
                    dve.tensor_tensor(block_of(act_lo, n), wa, block_of(act_hi, n).bitcast(F32), ALU.subtract).then_inc(m_split, 1)

            def add_square(n):
                dve.wait_ge(squared, n + 1)
                if n % KB == 0:
                    dve.tensor_copy(sq_sum[:, 0:T], sq[n % 2][:, :]).then_inc(sq_added, 1)
                else:
                    dve.wait_ge(sq_added, n)
                    dve.tensor_tensor(sq_sum[:, 0:T], sq_sum[:, 0:T], sq[n % 2][:, :], ALU.add).then_inc(sq_added, 1)

            def row_of_norm(n):
                dve.wait_ge(sum_turned, n + 1)
                dve.tensor_scalar(ms_t[:, :], turn[:, 0:QB], 1.0 / D, EPS, ALU.mult, ALU.add).then_inc(ms_ready, 1)
                dve.wait_ge(row_ready, n + 1)

            def normed(x, k, g, row=score[:, 0:T]):
                return dve.scalar_tensor_tensor(out=x[:, k], in0=x[:, k], scalar=gcol[:, g + k:g + k + 1],
                                                in1=row, op0=ALU.mult, op1=ALU.mult)

            for m in range(KB):
                b = (PJ_OUT + m) % 2
                dve.wait_ge(w_used, PC_OUT + 2 * m + 2)
                dve.tensor_copy(halves(mixed[:, m]), acc[b]).then_inc(proj_free[b], 1)
                if m:
                    add_square(m - 1)
            add_square(KB - 1)

            def update(n, x, g):
                def rest(k):
                    dve.wait_ge(h_hi, n * KB + k + 1)
                    if n == 0:
                        dve.scalar_tensor_tensor(out=act_lo[:, k], in0=hT[:, k], scalar=gcol[:, G_FPRE + k:G_FPRE + k + 1],
                                                 in1=act_hi[:, k].bitcast(F32), op0=ALU.mult, op1=ALU.subtract).then_inc(h_split, 1)
                    else:
                        dve.tensor_tensor(act_lo[:, k], hT[:, k], act_hi[:, k].bitcast(F32), ALU.subtract).then_inc(h_split, 1)

                for k in range(KB):
                    normed(x, k, g).then_inc(block_normed, 1)
                    if k in BY_VECTOR:
                        dve.wait_ge(block_normed, n * KB + k + 1)
                        dve.tensor_tensor(hT[:, k], hT[:, k], x[:, k], ALU.add).then_inc(h_added[1], 1)
                    if k >= 2:
                        rest(k - 2)
                rest(KB - 2)
                rest(KB - 1)

            row_of_norm(N_POST)
            update(0, mixed, G_POST)
            for k in range(KB):
                add_square(KB + k)
            row_of_norm(N_FPRE)
            dve.tensor_copy(r_row[:, :], score[:, 0:T]).then_inc(row_read, 1)
            dve.wait_ge(row_read, 1)
            dve.wait_ge(down_cleared, 1)

            def up(n, src, free, count):
                ins = dve.tensor_tensor(halves(up_t[:, :]), src, halves(r_row[:, :]), ALU.mult)
                if free is None:
                    done(ins)
                    settle()
                else:
                    ins.then_inc(free[0], 1)
                    at_least(dve, *free)
                dve.scalar_tensor_tensor(out=up_a[:, :], in0=up_t[:, :], scalar=0.0, in1=up_t[:, :],
                                         op0=ALU.max, op1=ALU.mult).then_inc(up_ready, 1)
                at_least(dve, up_hi, count)
                dve.tensor_tensor(block_of(mid_lo, n), up_a[:, :], block_of(mid_hi, n).bitcast(F32),
                                  ALU.subtract).then_inc(up_split, 1)

            def up_blocks(first, n, group):
                with dve.Fori(0, n // 2) as it:
                    for j in range(2):
                        b = (PJ_FF + j) % 2
                        at_least(dve, w_used, group * (4 * KB) + Count(PC_FF + 2 * (first + j) + 2, [(it, RING)]))
                        up(Count(first + j, [(it, 2)]), acc[b],
                           (proj_free[b], group * KB + Count((PJ_FF + first + j) // 2 + 1, [(it, 1)])),
                           group * KB + Count(first + j + 1, [(it, 2)]))

            def down_blocks(group):
                with dve.Fori(0, KB // 2) as it:
                    for j in range(2):
                        b = (PJ_FF + KB + j) % 2
                        at_least(dve, w_used, group * (4 * KB) + Count(PC_FF + 2 * KB + 2 * j + 2, [(it, RING)]))
                        d = block_of(wide, Count(j, [(it, 2)]))
                        dve.tensor_tensor(halves(d), acc[b], halves(d), ALU.add).then_inc(proj_free[b], 1)

            for j in range(RAW):
                dve.wait_ge(proj_free[(PJ_FF + j) % 2], (PJ_FF + j) // 2 + 1)
                up(Count(j), halves(up_raw[j]), None, Count(j + 1))
            up_blocks(RAW, KB - RAW, Count(0))
            down_blocks(Count(0))
            with dve.Fori(1, FG - 1) as g:
                up_blocks(0, KB, Count(0, [(g, 1)]))
                down_blocks(Count(0, [(g, 1)]))
            up_blocks(0, KB, Count(FG - 1))
            for k in range(KB):
                job = PJ_FF + (FG - 1) * 2 * KB + KB + k
                dve.wait_ge(w_used, PC_FF + (FG - 1) * 4 * KB + 2 * KB + 2 * k + 2)
                dve.tensor_tensor(halves(down_sum[:, k]), acc[job % 2], halves(down_sum[:, k]), ALU.add).then_inc(proj_free[job % 2], 1)
                if k:
                    add_square(2 * KB + k - 1)
            add_square(3 * KB - 1)
            row_of_norm(N_FPOST)
            update(1, down_sum, G_FPOST)
            for k in range(KB):
                add_square(3 * KB + k)
            row_of_norm(N_PLE)
            done(dve.tensor_copy(r_row[:, :], score[:, 0:T]))
            settle()
            for m in range(KB):
                done(normed(ple, m, G_PLE, r_row[:, :]))
                dve.wait_ge(proj_free[(PJ_PG + m) % 2], (PJ_PG + m) // 2 + 1)
                settle()
                done(dve.tensor_tensor(y_f[m], y_f[m], ple[:, m], ALU.mult))
                settle()
                dve.tensor_tensor(y_f[m], y_f[m], hT[:, m], ALU.add).then_inc(y_ready, 1)

        @block.tensor
        def _(pe):
            def wait_projection(n):
                b = n.mod(2)
                at_least(pe, proj_free[b], (n + (-b)).over(2))

            def k_steps(n, p, hi, lo, blocks=KB, input_ready=None, apart=1):
                out = acc[n.mod(2)]
                for k in range(blocks):
                    if k == 0:
                        wait_projection(n)
                    if k % 4 == 0:
                        at_least(pe, lo_done, p + (apart * (k // 4) + 1))
                    if input_ready:
                        input_ready(k)
                    slot, at = (p + apart * (k // 4)).mod(RING), slice(P * (k % 4), P * (k % 4) + P)
                    for s, (w, x) in enumerate(((w_hi, hi), (w_lo, hi), (w_hi, lo))):
                        for h in range(2):
                            last = pe.matmul(out[:, h], w[:, slot, at], x[:, k, HALF * h:HALF * h + HALF],
                                             start=(k == 0 and s == 0), stop=(k == blocks - 1 and s == 2))
                    if k % 4 == 3:
                        last.then_inc(w_used, 1)
                    yield

            def project(*args, **kw):
                for _ in k_steps(*args, **kw):
                    pass

            def unit_steps(u):
                for n in range(3):
                    yield from k_steps(u * 3 + (PJ_IN + n), u * 6 + 2 * n, act_hi, act_lo)

            def two_tasks(n, p, ready, before, between=None):
                tasks = [k_steps(Count(n + j), Count(p + j), act_hi, act_lo, apart=2) for j in range(2)]
                for k in range(KB):
                    pe.wait_ge(ready, before + k + 1)
                    for task in tasks:
                        next(task)
                    if between:
                        between(k)

            def row_matmuls(r, valid):
                for t in range(QB):
                    n = valid(t)
                    last = pe.matmul(score[:, P * t:P * t + rows(t)], r[0:n, t:t + 1].broadcast_to([n, P]),
                                     ident[0:n, 0:rows(t)], start=True, stop=True)
                return last

            pe.wait_ge(consts, 1)

            def turn_x(j, t):
                n = rows(t)
                last = pe.transpose(x_bank(j)[:, P * t:P * t + n], x_tm[0:n, t, P * j:P * j + P], ident[0:n, 0:n])
                if t == QB - 1:
                    last.then_inc(x_turned, 1)

            def turn_block(j, bank_of):
                pe.wait_ge(x_kept[bank_of % 2], bank_of // 2 + 1)
                for t in range(QB):
                    turn_x(j, t)

            for t in range(QB):
                pe.wait_ge(x_loaded[t], 16)
                for j in range(3):
                    turn_x(j, t)
            turn_block(3, 0)
            turn_block(4, 1)
            pe.wait_ge(rows_loaded, 16 * 6)
            pe.transpose(score[:, 0:41], gain_rows[:, :], ident[0:41, 0:41]).then_inc(rows_turned, 1)
            pe.wait_ge(x_rooted, QB)
            pe.wait_ge(gains_ready, 1)
            row_matmuls(r_x, rows).then_inc(x_row_ready, 1)
            turn_block(5, 2)
            for j in (3, 4):
                pe.wait_ge(x_kept[j % 2], j // 2 + 1)
            two_tasks(PJ_IN, 0, u_split, 0, between=lambda k: turn_block(X_EARLY + k, X_EARLY + k - 1) if k < 2 else None)
            project(Count(PJ_IN + 2), Count(4), act_hi, act_lo)

            def unit(u, kind, par, prev):
                steps = A_STEPS if kind == "A" else B_STEPS
                turns = turn_base(u, kind)
                projected = unit_steps(u + 1)

                def scores(i, m):
                    n, np_, h = keys(i), rows(i), slice(64 * m, 64 * m + 64)
                    job = 2 * i + m
                    at_least_alone(pe, biased, u * 10 + (0 if i == 0 else job if i == QB - 1 else job - 1))
                    q = qT[par][h, P * i:P * i + np_]
                    if i < QB - 1:
                        last = pe.matmul(score[:, 512 * m:512 * m + n], q, kT[par][h, 0:n], start=True, stop=True)
                    else:
                        pe.matmul(score[0:np_, 0:SEQ], q, ckT[h, :], start=True, stop=True)
                        last = pe.matmul(score[0:np_, SEQ:T], q, kT[par][h, SEQ:T], start=True, stop=True)
                    last.then_inc(scored, 1)

                for name, arg, t in walk(steps, prev is not None):
                    if name == "k":
                        next(projected)
                        continue
                    if t is not None:
                        at_least_alone(pe, turn_free, turns + t)
                    if name == "S":
                        if arg == 0:
                            for n in (1, 2):
                                job = u * 3 + (PJ_IN + n)
                                b = job.mod(2)
                                at_least(pe, proj_free[b], (job + (-b)).over(2) + 1)
                        scores(arg, 0)
                        scores(arg, 1)
                    elif name in ("Sa", "Sb"):
                        scores(QB - 1, int(name == "Sb"))
                    elif name in ("V4", "K4"):
                        src = vT[par] if name == "V4" else kT[par]
                        for j in range(QB - 1):
                            last = pe.transpose(turn[:, P * j:P * j + P], src[:, P * j:P * j + P], ident[:, :])
                        last.then_inc(turned, 1)
                    elif name == "CK":
                        at_least(pe, ck_loaded, (u + 1) * 16)
                        for j in range(QB - 1):
                            last = pe.transpose(turn[:, P * j:P * j + P], ck[:, P * j:P * j + P], ident[:, :])
                        last.then_inc(turned, 1)
                    elif name == "Tail":
                        last = pe.transpose(turn[0:SMP, 0:P], vT[par][:, SEQ:T], ident[:, :])
                        last = pe.transpose(turn[0:SMP, P:2 * P], kT[par][:, SEQ:T], ident[:, :])
                        if prev is not None:
                            last = out_tail(1 - par)
                        last.then_inc(turned, 1)
                    elif name == "OT":
                        outputs_ready(u + (-1), prev)
                        out_main(1 - par)
                    elif name == "T":
                        i, m = arg
                        np_ = rows(i)
                        if kind == "A":
                            at_least_alone(pe, exped, u * 10 + (2 * i + m + 1))
                        else:
                            at_least_alone(pe, combined, (u + (-NA)) * QB + (i + 1))
                        for j in range(n_key_blocks(i)):
                            nk = P if j < QB - 1 else SMP
                            last = pe.transpose(turn[0:nk, np_ * j:np_ * j + np_], prob[i % 2][m][0:np_, P * j:P * j + nk],
                                                ident[0:np_, 0:np_])
                        last.then_inc(turned, 1)
                    elif name == "AV":
                        i = arg
                        np_ = rows(i)
                        last_turn = max(tt for nn, aa, tt in walk(steps, prev is not None)
                                        if nn == "T" and aa[0] == i)
                        at_least(pe, turn_free, turns + (last_turn + 1))
                        at_least(pe, out_free, u * QB + i)
                        if i == QB - 1:
                            at_least(pe, cv_loaded, (u + 1) * 16)
                        for m in range(2 if kind == "A" else 1):
                            c = slice(64 * m, 64 * m + 64) if kind == "A" else slice(0, P)
                            for j in range(n_key_blocks(i)):
                                if i < QB - 1:
                                    v, nk = v_tm[:, j, c], P
                                elif j < QB - 1:
                                    v, nk = cv[:, P * j + c.start:P * j + c.stop], P
                                else:
                                    v, nk = v_tm[0:SMP, j, c], SMP
                                last = pe.matmul(outp[0:np_, c], probT[m][0:nk, np_ * j:np_ * j + np_], v,
                                                 start=(j == 0), stop=(j == n_key_blocks(i) - 1))
                        last.then_inc(av_done, 1)

            def outputs_ready(u, kind):
                if kind == "A":
                    at_least(pe, out_free, (u + 1) * QB)
                else:
                    at_least(pe, o_normed, u + (1 - NA))

            def out_main(b):
                for j in range(QB - 1):
                    last = pe.transpose(turn[:, P * j:P * j + P], o_tm[b][:, j], ident[:, :])
                last.then_inc(turned, 1)

            def out_tail(b):
                return pe.transpose(turn[:, 2 * P:2 * P + SMP], o_tm[b][0:SMP, QB - 1], ident[0:SMP, 0:SMP])

            for u in range(NA):
                unit(Count(u), "A", u % 2, "A" if u else None)
            unit(Count(NA), "B", 0, "A")
            unit(Count(NA + 1), "B", 1, "B")
            with pe.Fori(0, (NB - 4) // 2) as it:
                for v in range(2):
                    unit(Count(NA + 2 + v, [(it, 2)]), "B", v, "B")
            unit(Count(NU - 2), "B", 0, "B")
            unit(Count(NU - 1), "B", 1, "B")

            for n in range(3, 5):
                project(Count(PJ_GATE + n), Count(PC_GATE + 2 * n), act_hi, act_lo)
            outputs_ready(Count(NU - 1), "B")
            pe.wait_ge(turn_free, TURN_END)
            out_main(1)
            project(Count(PJ_GATE + 5), Count(PC_GATE + 10), act_hi, act_lo)
            pe.wait_ge(turn_free, TURN_END + 1)
            out_tail(1).then_inc(turned, 1)
            with pe.Fori(0, KB - 3) as it:
                for j in range(2):
                    project(Count(PJ_GATE + 6 + j, [(it, 2)]), Count(PC_GATE + 12 + 2 * j, [(it, RING)]), act_hi, act_lo)
            pe.wait_ge(p_loaded, 32)
            pe.wait_ge(turn_free, TURN_END + 2)
            for k in range(2):
                for t in range(QB):
                    n = rows(t)
                    last = pe.transpose(pair[k][:, P * t:P * t + n], p_tm[0:n, t, P * k:P * k + P], ident[0:n, 0:n])
                last.then_inc(p_turned, 1)
            with pe.Fori(0, KB // RING) as it:
                for j in range(RING):
                    project(Count(PJ_BRA + j, [(it, RING)]), Count(PC_BRA + j, [(it, RING)]), oa_hi, oa_lo, blocks=NA)
            with pe.Fori(0, KB // 2) as it:
                for j in range(2):
                    project(Count(PJ_BRB + j, [(it, 2)]), Count(PC_BRB + 2 * j, [(it, RING)]), mid_hi, mid_lo)
            with pe.Fori(0, KB // 2) as it:
                for j in range(2):
                    project(Count(PJ_OUT + j, [(it, 2)]), Count(PC_OUT + 2 * j, [(it, RING)]), act_hi, act_lo,
                            input_ready=lambda k: pe.wait_ge(m_split, k + 1))

            def project_ple(half, i):
                if half == i == 0:
                    pe.wait_ge(p_split, 2)
                n, p = PJ_PLE[half] + i, Count(PC_PLE[half] + i // 2)
                wait_projection(Count(n))
                at_least(pe, lo_done, p + 1)
                for k in range(2):
                    at = slice(2 * P * k + P * (i % 2), 2 * P * k + P * (i % 2) + P)
                    for s, (w, x) in enumerate(((w_hi, pT_hi), (w_lo, pT_hi), (w_hi, pT_lo))):
                        for h in range(2):
                            last = pe.matmul(acc[n % 2][:, h], w[:, p.mod(RING), at], x[:, k, HALF * h:HALF * h + HALF],
                                             start=(k == 0 and s == 0), stop=(k == 1 and s == 2))
                last.then_inc(w_used if i % 2 else ple_first, 1)

            def norm_sums(n):
                if n == 0:
                    pe.wait_ge(sq_cleared, 1)
                pe.wait_ge(sq_added, KB * (n + 1))
                for t in range(QB):
                    last = pe.matmul(turn[:, t:t + 1], sq_sum[:, P * t:P * t + P], ones[:, 0:1], start=True, stop=True)
                last.then_inc(sum_turned, 1)

            def norm_row(n):
                pe.wait_ge(r_ready, n + 1)
                row_matmuls(r_t, lambda t: P).then_inc(row_ready, 1)

            def behind_norm(half, n, pj, pc):
                project_ple(half, 0)
                norm_sums(n)
                project_ple(half, 1)
                norm_row(n)
                project_ple(half, 2)
                project_ple(half, 3)
                two_tasks(pj, pc, h_split, half * KB)

            def late_norm(n, pj, pc):
                project(Count(pj + 2), Count(pc + 4), act_hi, act_lo)
                steps = k_steps(Count(pj + 3), Count(pc + 6), act_hi, act_lo)
                for _ in range(KB // 2):
                    next(steps)
                norm_sums(n)
                for _ in steps:
                    pass
                norm_row(n)

            def up_blocks(first, n, group):
                with pe.Fori(0, n // 2) as it:
                    for j in range(2):
                        project(group * (2 * KB) + Count(PJ_FF + first + j, [(it, 2)]),
                                group * (4 * KB) + Count(PC_FF + 2 * (first + j), [(it, RING)]), act_hi, act_lo)

            def down_blocks(group):
                with pe.Fori(0, KB // 2) as it:
                    for j in range(2):
                        project(group * (2 * KB) + Count(PJ_FF + KB + j, [(it, 2)]),
                                group * (4 * KB) + Count(PC_FF + 2 * KB + 2 * j, [(it, RING)]), mid_hi, mid_lo,
                                input_ready=lambda k: at_least(pe, up_split, group * KB + (k + 1)))

            behind_norm(0, N_POST, PJ_FF, PC_FF)
            late_norm(N_FPRE, PJ_FF, PC_FF)
            up_blocks(4, KB - 4, Count(0))
            down_blocks(Count(0))
            with pe.Fori(1, FG) as g:
                up_blocks(0, KB, Count(0, [(g, 1)]))
                down_blocks(Count(0, [(g, 1)]))
            behind_norm(1, N_FPOST, PJ_PG, PC_PG)
            late_norm(N_PLE, PJ_PG, PC_PG)

            def turn_y(m):
                pe.wait_ge(y_ready, m + 1)
                if m >= 2:
                    pe.wait_ge(y_copied, m - 1)
                for t in range(QB):
                    n = rows(t)
                    last = pe.transpose(pair[m % 2][0:n, P * t:P * t + P], y_f[m][:, P * t:P * t + n], ident[:, :])
                last.then_inc(y_turned, 1)

            for m in range(4, KB):
                project(Count(PJ_PG + m), Count(PC_PG + 2 * m), act_hi, act_lo)
                for i in Y_AFTER[m]:
                    turn_y(i)


def kernel(**inputs):
    import numpy as np
    import concourse.bacc as bacc
    from concourse.bass_utils import run_bass_kernel_spmd

    names = ["x_prompt", "x_sample", "cache_a_k", "cache_a_v", "cache_b_k", "cache_b_v", "p_prompt", "p_sample",
             "w_in", "rel_bias", "diff_lambda", "diff_subln", "w_gate", "w_branch_a", "w_branch_b", "w_out",
             "g_mix_pre", "g_mix_post", "g_ffn_pre", "g_ffn_post", "w_up", "w_down", "w_ple", "g_ple", "w_ple_gate"]
    arrays = {n: np.ascontiguousarray(inputs[n]) for n in names}
    arrays["rel_bias"] = np.ascontiguousarray(arrays["rel_bias"][:, :, ::-1])
    d, bsz, s, m = 1, 1, arrays["x_prompt"].shape[1], arrays["x_sample"].shape[1]
    ha, hd = arrays["cache_a_k"].shape[3:]
    hb = arrays["cache_b_k"].shape[3]
    keep = min(8 * 64, s)
    shapes = [arrays["x_prompt"].shape, arrays["x_sample"].shape,
              (d, bsz, keep, ha, hd), (d, bsz, keep, ha, hd), (d, bsz, s, hb, 2, hd), (d, bsz, s, hb, 2 * hd),
              (d, bsz, m, ha, hd), (d, bsz, m, ha, hd), (d, bsz, m, hb, 2, hd), (d, bsz, m, hb, 2 * hd)]
    nc = bacc.Bacc("TRN2", target_bir_lowering=False, num_devices=1)
    ins = [nc.dram_tensor(n, arrays[n].shape, mybir.dt.from_np(arrays[n].dtype), kind="ExternalInput").ap() for n in names]
    outs = [nc.dram_tensor(f"out_{i}", sh, F32, kind="ExternalOutput").ap() for i, sh in enumerate(shapes)]
    encoder_layer(nc, *ins, *outs)
    r = run_bass_kernel_spmd(nc, [arrays], core_ids=[0])
    return tuple(r.results[0][f"out_{i}"] for i in range(len(shapes)))
```

```python
from contextlib import ExitStack

import concourse.bass as bass
from concourse import mybir

F32, F32R, I32 = mybir.dt.float32, mybir.dt.float32r, mybir.dt.int32
ALU, ACT, AX = mybir.AluOpType, mybir.ActivationFunctionType, mybir.AxisListType

P = 128
EPS = 1e-6
LAM0 = 0.2
MASK = -1e30
RING = 4
PIECE = 512

A_STEPS = [("S", 0, 2), ("V4", 0, 0), ("S", 1, 0), ("K4", 0, 1), ("T", (0, 0), 2), ("T", (0, 1), 1),
           ("OT", 0, 1), ("AV", 0, 0), ("S", 2, 0), ("Tail", 0, 1), ("T", (1, 0), 3), ("T", (1, 1), 1),
           ("CK", 0, 2), ("AV", 1, 0), ("T", (2, 0), 0), ("T", (2, 1), 1), ("S", 3, 0), ("AV", 2, 0),
           ("S", 4, 1), ("T", (3, 0), 2), ("T", (3, 1), 1), ("AV", 3, 2), ("T", (4, 0), 0), ("T", (4, 1), 1),
           ("AV", 4, 2)]
B_STEPS = [("V4", 0, 0), ("S", 0, 2), ("K4", 0, 1), ("C", 0, 0), ("T", (0, 0), 2), ("S", 1, 0), ("C", 1, 0),
           ("AV", 0, 1), ("S", 2, 1), ("T", (1, 0), 2), ("OT", 0, 1), ("S", 3, 0), ("C", 2, 2), ("Tail", 0, 1),
           ("AV", 1, 0), ("CK", 0, 2), ("T", (2, 0), 1), ("C", 3, 0), ("AV", 2, 1), ("S", 4, 0),
           ("T", (3, 0), 1), ("AV", 3, 3), ("T", (4, 0), 0), ("T", (4, 1), 2), ("AV", 4, 1)]


def walk(steps, with_outputs):
    k, turn = 0, 0
    for name, arg, before in steps:
        for _ in range(before):
            yield "k", k, None
            k += 1
        if name == "OT" and not with_outputs:
            continue
        if name in ("V4", "K4", "T", "OT", "Tail", "CK"):
            yield name, arg, turn
            turn += 1
        else:
            yield name, arg, None


class Count:

    def __init__(self, const, terms=()):
        self.const, self.terms = const, tuple(terms)

    def __add__(self, n):
        if isinstance(n, Count):
            return Count(self.const + n.const, self.terms + n.terms)
        return Count(self.const + n, self.terms)

    def __mul__(self, n):
        return Count(self.const * n, [(r, f * n) for r, f in self.terms])

    def over(self, n):
        assert all(f % n == 0 for _, f in self.terms)
        return Count(self.const // n, [(r, f // n) for r, f in self.terms])

    def mod(self, n):
        assert all(f % n == 0 for _, f in self.terms)
        return self.const % n

    def value(self):
        v = self.const
        for register, factor in self.terms:
            v = register * factor + v
        return v


def at_least(eng, sem, count):
    v = count.value()
    assert not count.terms or count.const > 0
    if not isinstance(v, int) or v > 0:
        eng.wait_ge(sem, v)


def at_least_alone(eng, sem, count):
    at_least(eng, sem, count)
    if count.terms:
        eng.nop(nofuse=True)


def encoder_layer(nc, x_prompt, x_sample, cache_a_k, cache_a_v, cache_b_k, cache_b_v, p_prompt, p_sample,
                  w_in, rel_bias_reversed, diff_lambda, diff_subln, w_gate, w_branch_a, w_branch_b, w_out,
                  g_mix_pre, g_mix_post, g_ffn_pre, g_ffn_post, w_up, w_down, w_ple, g_ple, w_ple_gate,
                  y_prompt, y_sample, ak_p, av_p, bk_p, bv_p, ak_s, av_s, bk_s, bv_s):
    SEQ, D = x_prompt.shape[1:]
    SMP = x_sample.shape[1]
    T = SEQ + SMP
    HALF = T // 2
    QB = SEQ // P + 1
    KB = D // P
    AW = cache_a_k.shape[3] * cache_a_k.shape[4]
    NA = AW // P
    NB = cache_b_k.shape[3]
    NU = NA + NB
    FF = w_up.shape[2]
    FG = FF // D
    REL = rel_bias_reversed.shape[2] // 2
    TW = SEQ + P
    assert T == 576 and NA == 4 and NB == 8 and REL == P and cache_a_k.shape[2] == SEQ

    xp, xs_d = x_prompt[0], x_sample[0]
    cak, cav = [c[0, 0].rearrange("t h d -> t (h d)") for c in (cache_a_k, cache_a_v)]
    cbk, cbv = cache_b_k[0, 0].rearrange("t h c d -> t (h c d)"), cache_b_v[0, 0].rearrange("t h d -> t (h d)")
    out_a = [o[0, 0].rearrange("t h d -> t (h d)") for o in (ak_p, av_p, ak_s, av_s)]
    out_b = [bk_p[0, 0].rearrange("t h c d -> t (h c d)"), bv_p[0, 0].rearrange("t h d -> t (h d)"),
             bk_s[0, 0].rearrange("t h c d -> t (h c d)"), bv_s[0, 0].rearrange("t h d -> t (h d)")]
    rev = rel_bias_reversed[0]
    BW = P + 2 * REL
    band = nc.dram_tensor("band_bias", [2 * NA, P, BW], F32, kind="Internal").ap()

    PC_GATE = 6 * NU
    PC_BRA = PC_GATE + 2 * 2 * KB
    PC_BRB = PC_BRA + KB
    PC_OUT = PC_BRB + 2 * KB
    PC_PLE = (PC_OUT + 2 * KB, PC_OUT + 2 * KB + KB // 4 + FG * 4 * KB)
    PC_FF = PC_PLE[0] + KB // 4
    PC_PG = PC_PLE[1] + KB // 4
    PC_END = PC_PG + 2 * KB
    PJ_IN = 0
    PJ_GATE = PJ_IN + 3 * NU
    PJ_BRA = PJ_GATE + 2 * KB
    PJ_BRB = PJ_BRA + KB
    PJ_OUT = PJ_BRB + KB
    PJ_PLE = (PJ_OUT + KB, PJ_OUT + KB + KB // 2 + FG * 2 * KB)
    PJ_FF = PJ_PLE[0] + KB // 2
    PJ_PG = PJ_PLE[1] + KB // 2
    N_POST, N_FPRE, N_FPOST, N_PLE = range(4)
    RAW = 6
    Y_AFTER = {m: (2 * m - 8, 2 * m - 7) if m >= KB // 2 else () for m in range(KB)}
    BY_POOL, BY_VECTOR = (0, 1, 3, 4, 6), (2, 5, 7)
    A_TURNS, B_TURNS = 15, 11
    JOBS = 2 * (QB - 1) + 1
    TURN_B = A_TURNS * NA - 1
    TURN_END = TURN_B + B_TURNS * NB

    with ExitStack() as ctx:
        def sb(name, shape, dt=F32, stack=ctx):
            return stack.enter_context(nc.sbuf_tensor(name, shape, dt))

        def sem(name):
            return ctx.enter_context(nc.semaphore(name))

        ident, ones = sb("ident", [P, P]), sb("ones", [P, P])
        gcol = sb("gcol", [P, 48])
        G_PRE, G_POST, G_FPRE, G_FPOST, G_PLE, G_SUB, G_SUBL = 0, 8, 16, 24, 32, 40, 41
        neg_half, neg_lam = sb("neg_half", [P, QB]), sb("neg_lam", [P, 1])
        act_hi, act_lo = sb("act_hi", [P, KB, T], F32R), sb("act_lo", [P, KB, T], F32R)
        w_raw = sb("w_raw", [P, RING, PIECE])
        w_hi, w_lo = sb("w_hi", [P, RING, PIECE], F32R), sb("w_lo", [P, RING, PIECE], F32R)
        hT = sb("hT", [P, KB, T])
        small = sb("small", [P, 24])
        x_row = sb("x_row", [P, T])
        ss_x, sq_x, r_x = small[:, 0:5], small[:, 8:13], small[:, 16:21]
        with ExitStack() as start:
            x_tm = sb("x_tm", [P, QB, D], F32, start)
            x_sq = sb("x_sq", [P, QB, D], F32, start)
            gain_rows = sb("gain_rows", [41, P], F32, start)
            lam_in = sb("lam_in", [P, 4, 64], F32, start)
            lam_pr = sb("lam_pr", [P, 2, 64], F32, start)
            lam_s = sb("lam_s", [P, 4], F32, start)
            dist_i = sb("dist_i", [P, TW], I32, start)
            dist = sb("dist", [P, TW], F32, start)
            band_sb = sb("band_sb", [2 * NA, BW], F32, start)
        mid_hi, mid_lo = sb("mid_hi", [P, NB, T], F32R), sb("mid_lo", [P, NB, T], F32R)
        with ExitStack() as branch_a:
            oa_hi, oa_lo = sb("oa_hi", [P, NA, T], F32R, branch_a), sb("oa_lo", [P, NA, T], F32R, branch_a)
            with ExitStack() as att:
                vT, kT, qT = ([], [], [])
                for b in range(2):
                    for name, x in (("vT", vT), ("kT", kT), ("qT", qT)):
                        x.append(sb(f"{name}{b}", [P, T], F32, att))
                k_tm, v_tm = sb("k_tm", [P, QB, P], F32, att), sb("v_tm", [P, QB, P], F32, att)
                ck, cv, ckT = (sb(n, [P, SEQ], F32, att) for n in ("ck", "cv", "ckT"))
                tab_a = [sb(f"tab_a{b}", [P, 2, TW], F32, att) for b in range(2)]
                tab_b = [sb(f"tab_b{b}", [P, TW], F32, att) for b in range(2)]
                prob = [[sb(f"prob{b}{m}", [P, T], F32, att) for m in range(2)] for b in range(2)]
                probT = [sb(f"probT{m}", [P, SEQ], F32, att) for m in range(2)]
                neg_max = sb("neg_max", [P, 2, 2], F32, att)
                sums, r_sum = sb("sums", [P, 2, 2], F32, att), sb("r_sum", [P, 2, 2], F32, att)
                c_map = sb("c_map", [P, 2], F32, att)
                o_tm = [sb(f"o_tm{b}", [P, QB, P], F32, att) for b in range(2)]
                o_sq = sb("o_sq", [P, 2, P], F32, att)
                q_pad = [sb(f"q_pad{b}", [P, 2 * SMP], F32, att) for b in range(2)]
                o_second = sb("o_second", [SMP, P], F32, att)
                o_ms = sb("o_ms", [P, 2, QB], F32, att)
                o_r = sb("o_r", [P, QB], F32, att)
            wide = sb("wide", [P, 2 * KB, T], F32, branch_a)
            down_sum, mixed = wide[:, 0:KB], wide[:, KB:2 * KB]
            sq = [sb(f"sq{b}", [P, T], F32, branch_a) for b in range(2)]
            sq_sum = sb("sq_sum", [P, QB * P], F32, branch_a)
            pT_hi, pT_lo = sb("pT_hi", [P, 2, T], F32R, branch_a), sb("pT_lo", [P, 2, T], F32R, branch_a)
            ms_t, r_t = sb("ms_t", [P, QB], F32, branch_a), sb("r_t", [P, QB], F32, branch_a)
            up_raw, y_f = ([mixed[:, m] for m in range(KB)] for _ in range(2))
            with ExitStack() as ple_in:
                p_tm = sb("p_tm", [P, QB, 2 * P], F32, ple_in)
            r_row = sb("r_row", [P, T], F32, branch_a)
            up_t, up_a = sb("up_t", [P, T], F32, branch_a), sb("up_a", [P, T], F32, branch_a)
            y_tm = [sb(f"y_tm{b}", [P, QB, P], F32, branch_a) for b in range(2)]
        ple = sb("ple", [P, KB, T])
        assert KB == 2 * NA

        proj = [ctx.enter_context(nc.psum_tensor(f"proj{b}", [P, 1024], F32)) for b in range(2)]
        score = ctx.enter_context(nc.psum_tensor("score", [P, 1024], F32))
        turn_out = ctx.enter_context(nc.psum_tensor("turn_out", [P, 1024], F32))
        turn, outp = turn_out[:, 0:512], turn_out[:, 512:1024]
        pair = [score, turn_out]
        X_EARLY = 4

        def x_bank(j):
            return (score, turn_out, proj[0], proj[1])[j if j < X_EARLY else j % 2]

        acc = [p[:, :].rearrange("p (h n) -> p h n", h=2)[:, :, 0:HALF] for p in proj]

        def halves(ap):
            return ap.rearrange("p (h n) -> p h n", h=2)

        w_loaded = [sem(f"w_loaded{s}") for s in range(RING)]
        hi_done, lo_done = sem("hi_done"), sem("lo_done")
        w_used = sem("w_used")
        proj_free = [sem(f"proj_free{b}") for b in range(2)]
        x_loaded = [sem(f"x_loaded{t}") for t in range(QB)]
        rows_loaded, lam_loaded, rel_loaded = sem("rows_loaded"), sem("lam_loaded"), sem("rel_loaded")
        band_made = sem("band_made")
        band_kept = [sem("band_kept_first"), sem("band_kept_others")]
        consts, dist_made = sem("consts"), sem("dist_made")
        vec = sem("vec")
        pool_own = sem("pool_own")
        rows_turned, gains_ready = sem("rows_turned"), sem("gains_ready")
        lam_ready, lam_exped = sem("lam_ready"), sem("lam_exped")
        x_squared, x_mean, x_rooted = sem("x_squared"), sem("x_mean"), sem("x_rooted")
        x_turned, x_kept = sem("x_turned"), [sem("x_kept_even"), sem("x_kept_odd")]
        x_row_ready, g_hi, g_split = sem("x_row_ready"), sem("g_hi"), sem("g_split")
        first_row_loaded = sem("first_row_loaded")
        tab_loaded = [sem(f"tab_loaded{b}") for b in range(2)]
        tab_ready = sem("tab_ready")
        ck_loaded, cv_loaded, kv_stored = sem("ck_loaded"), sem("cv_loaded"), sem("kv_stored")
        scored, biased, exped, combined = sem("scored"), sem("biased"), sem("exped"), sem("combined")
        turned, turn_free = sem("turned"), sem("turn_free")
        tail_copied, o_hi = sem("tail_copied"), sem("o_hi")
        q_padded = sem("q_padded")
        av_done, out_free = sem("av_done"), sem("out_free")
        o_squared = sem("o_squared")
        o_summed, o_rooted, o_normed = sem("o_summed"), sem("o_rooted"), sem("o_normed")
        gated = sem("gated")
        br_mixed, m_hi, m_split = sem("br_mixed"), sem("m_hi"), sem("m_split")
        sq_cleared, squared, sq_added = sem("sq_cleared"), sem("squared"), sem("sq_added")
        sum_turned, ms_ready, r_ready = sem("sum_turned"), sem("ms_ready"), sem("r_ready")
        row_ready, row_read = sem("row_ready"), sem("row_read")
        block_normed = sem("block_normed")
        h_added = [sem("h_added_pool"), sem("h_added_vector")]
        h_hi, h_split = sem("h_hi"), sem("h_split")
        down_cleared, up_ready, up_hi, up_split = (sem(n) for n in ("down_cleared", "up_ready", "up_hi", "up_split"))
        p_loaded, p_turned, p_hi, p_split = sem("p_loaded"), sem("p_turned"), sem("p_hi"), sem("p_split")
        ple_first = sem("ple_first")
        y_ready, y_turned, y_copied = sem("y_ready"), sem("y_turned"), sem("y_copied")
        y_stored = [sem(f"y_stored{b}") for b in range(2)]

        block = ctx.enter_context(nc.Block())

        def rows(i):
            return P if i < QB - 1 else SMP

        def keys(i):
            return P * (i + 1) if i < QB - 1 else T

        def n_key_blocks(i):
            return min(i + 1, QB)

        def out_block(x, u, kind, cols):
            n = u if kind == "A" else u + (-NA)
            return x[:, bass.ds(n.value(), 1), cols].rearrange("p a n -> p (a n)")

        def block_of(x, n):
            return x[:, bass.ds(n.value(), 1)].rearrange("p a n -> p (a n)")

        def turn_base(u, kind):
            if kind == "A":
                return u * A_TURNS + (-1) if u.const else u
            return (u + (-NA)) * B_TURNS + TURN_B

        @block.sync
        def _(sp):
            def piece(p, src, shaped=None):
                slot = p.mod(RING)
                at_least(sp, lo_done, p + (1 - RING))
                dst = w_raw[:, slot].rearrange("p (k n) -> p k n", n=shaped or P)
                sp.dma_start(dst, src).then_inc(w_loaded[slot], 16)

            def k_half(w, kh, col, n=P, kblocks=4, row0=0):
                return w[bass.ds(row0 + kh * 512, P * kblocks), bass.ds(col, n)].rearrange(
                    "(k p) n -> p k n", p=P)

            sp.dma_start(gain_rows[0:8], g_mix_pre[0].rearrange("(k p) -> k p", p=P)).then_inc(first_row_loaded, 16)
            for t in range(QB - 1):
                sp.dma_start(x_tm[:, t], xp[P * t:P * t + P]).then_inc(x_loaded[t], 16)
            piece(Count(0), k_half(w_in[0], 0, 2 * AW))
            sp.dma_start(x_tm[0:SMP, QB - 1], xs_d).then_inc(x_loaded[QB - 1], 16)
            sp.dma_start(band_sb[:, P:BW], rev[:, 0:2 * REL]).then_inc(rel_loaded, 16)

            def two_tasks(p0, w, cols, done=0):
                for kh in range(2):
                    for j in range(2):
                        if 2 * kh + j >= done:
                            piece(Count(p0 + 2 * kh + j), k_half(w, kh, cols[j]))

            def unit_pieces(u0, u, cols):
                for n, base in enumerate(cols):
                    for kh in range(2):
                        piece(u * 6 + (2 * n + kh), k_half(w_in[0], kh, ((u + (-u0)) * P + base).value()))

            a_cols = (2 * AW, AW, 0)
            b_cols = (3 * AW + 2 * NB * P, 3 * AW + NB * P, 3 * AW)
            two_tasks(0, w_in[0], a_cols[0:2], done=1)
            for g, at in ((g_mix_post, 8), (g_ffn_pre, 16), (g_ffn_post, 24), (g_ple, 32)):
                sp.dma_start(gain_rows[at:at + 8], g[0].rearrange("(k p) -> k p", p=P)).then_inc(rows_loaded, 16)
            sp.dma_start(gain_rows[40:41], diff_subln).then_inc(rows_loaded, 16)
            for kh in range(2):
                piece(Count(4 + kh), k_half(w_in[0], kh, a_cols[2]))
            sp.dma_start(lam_in[:, :, :], bass.AP(diff_lambda.tensor, 0, [[0, P], [64, 4], [1, 64]])
                         ).then_inc(lam_loaded, 16)
            sp.wait_ge(band_made, 1)
            for u in range(NA):
                sp.dma_start(band[2 * u:2 * u + 2], band_sb[2 * u:2 * u + 2].unsqueeze(1).broadcast_to([2, P, BW])
                             ).then_inc(band_kept[min(u, 1)], 16)
            with sp.Fori(0, (NA - 2) // 2) as it:
                for v in range(2):
                    unit_pieces(0, Count(1 + v, [(it, 2)]), a_cols)
            unit_pieces(0, Count(NA - 1), a_cols)
            with sp.Fori(0, NB // 2) as it:
                for v in range(2):
                    unit_pieces(NA, Count(NA + v, [(it, 2)]), b_cols)

            def stage(p0, w, n, kblocks=4, halves_=2):
                per = RING // halves_
                with sp.Fori(0, n // per) as it:
                    for j in range(per):
                        for kh in range(halves_):
                            piece(Count(p0 + j * halves_ + kh, [(it, RING)]),
                                  k_half(w, kh, Count(P * j, [(it, P * per)]).value()))

            stage(PC_GATE, w_gate[0], 2 * KB)
            sp.wait_ge(av_done, NU * QB)
            sp.dma_start(p_tm[:, 0:QB - 1], p_prompt[0, 0].rearrange("(j p) n -> p j n", p=P)).then_inc(p_loaded, 16)
            sp.dma_start(p_tm[0:SMP, QB - 1], p_sample[0, 0]).then_inc(p_loaded, 16)
            stage(PC_BRA, w_branch_a[0], KB, halves_=1)
            stage(PC_BRB, w_branch_b[0], KB)
            stage(PC_OUT, w_out[0], KB)

            def ple_pieces(half):
                for n in range(KB // 4):
                    col = 2 * P * (half * (KB // 4) + n)
                    piece(Count(PC_PLE[half] + n), k_half(w_ple[0], 0, col, n=2 * P, kblocks=2), shaped=2 * P)

            def blocks(p0, w, first, n, group=Count(0), col=0, row=0):
                with sp.Fori(0, n // 2) as it:
                    for j in range(2):
                        for kh in range(2):
                            piece(group * (4 * KB) + Count(p0 + 2 * j + kh, [(it, RING)]),
                                  k_half(w, kh, (group * col + Count(P * (first + j), [(it, 2 * P)])).value(),
                                         row0=(group * row).value()))

            ple_pieces(0)
            two_tasks(PC_FF, w_up[0], (0, P))
            blocks(PC_FF + 4, w_up[0], 2, KB - 2)
            blocks(PC_FF + 2 * KB, w_down[0], 0, KB)
            with sp.Fori(1, FG) as g:
                blocks(PC_FF, w_up[0], 0, KB, Count(0, [(g, 1)]), col=D)
                blocks(PC_FF + 2 * KB, w_down[0], 0, KB, Count(0, [(g, 1)]), row=D)
            ple_pieces(1)
            two_tasks(PC_PG, w_ple_gate[0], (0, P))
            blocks(PC_PG + 4, w_ple_gate[0], 2, KB - 2)
            for m in range(KB):
                sp.wait_ge(y_copied, m + 1)
                yt, cols = y_tm[m % 2], slice(P * m, P * m + P)
                sp.dma_start(y_prompt[0, :, cols].rearrange("(j p) n -> p j n", p=P),
                             yt[:, 0:QB - 1]).then_inc(y_stored[m % 2], 16)
                sp.dma_start(y_sample[0, :, cols], yt[0:SMP, QB - 1]).then_inc(y_stored[m % 2], 16)
            for b in range(2):
                sp.wait_ge(y_stored[b], 32 * KB // 2)
            sp.wait_ge(kv_stored, 64 * NU)

        @block.gpsimd
        def _(pool):
            def lo_part(p):
                slot = p.mod(RING)
                at_least(pool, hi_done, p + 1)
                pool.tensor_tensor(w_lo[:, slot], w_raw[:, slot], w_hi[:, slot].bitcast(F32),
                                   ALU.subtract).then_inc(lo_done, 1)

            def load_table(u):
                src = bass.AP(band.tensor, 2 * u * P * BW + P, [[BW - 1, P], [P * BW, 2], [1, 2 * REL]])
                pool.dma_start(tab_a[u % 2][:, :, TW - 2 * REL:TW], src).then_inc(tab_loaded[u % 2], 16)

            def finish_table(u):
                pool.wait_ge(tab_loaded[u % 2], 16 * (u // 2 + 1))
                tab, flat = tab_a[u % 2], TW - 2 * REL
                pool.tensor_copy(tab[:, :, 0:flat], tab[:, :, flat:flat + 1].broadcast_to([P, 2, flat])
                                 ).then_inc(pool_own, 1)
                pool.wait_ge(pool_own, u + 3)
                pool.memset(tab[0:SMP, :, TW - SMP:TW], MASK).then_inc(tab_ready, 1)

            pool.memset(ident[:, :], 0.0).then_inc(pool_own, 1)
            pool.memset(ones[:, :], 1.0)
            pool.memset(neg_half[:, :], -0.5).then_inc(pool_own, 1)
            pool.iota(dist_i[:, :], [[-1, TW]], base=SEQ, channel_multiplier=1).then_inc(dist_made, 1)
            pool.wait_ge(pool_own, 2)
            pool.affine_select(out=ident[:, :], in_=ident[:, :], compare_op=ALU.not_equal, fill=1.0,
                               base=0, pattern=[[-1, P]], channel_multiplier=1).then_inc(consts, 1)
            def root_x(t):
                n = rows(t)
                pool.wait_ge(x_mean, t + 1)
                pool.tensor_tensor(r_x[0:n, t:t + 1], sq_x[0:n, t:t + 1], neg_half[0:n, 0:1], ALU.pow
                                   ).then_inc(x_rooted, 1)

            for t in range(QB - 1):
                root_x(t)
            for p in range(2):
                lo_part(Count(p))
            for p in range(2, RING):
                lo_part(Count(p))
            root_x(QB - 1)
            pool.dma_start(ck[:, :].rearrange("p (j n) -> p j n", n=P),
                           cak[:, 0:P].rearrange("(j p) n -> p j n", p=P)).then_inc(ck_loaded, 16)
            pool.dma_start(cv[:, :].rearrange("p (j n) -> p j n", n=P),
                           cav[:, 0:P].rearrange("(j p) n -> p j n", p=P)).then_inc(cv_loaded, 16)
            for u in range(2):
                pool.wait_ge(band_kept[u], (1, NA - 1)[u] * 16)
                load_table(u)
            for n in range(2):
                lo_part(Count(RING + n))
            finish_table(0)
            for n in range(2, 6):
                lo_part(Count(RING + n))
            finish_table(1)

            def unit(u, kind, next_kind, par, prev):
                steps = A_STEPS if kind == "A" else B_STEPS
                turns = turn_base(u, kind)
                cols = ((u + (0 if kind == "A" else -NA)) * P).value()
                outs = out_a if kind == "A" else out_b
                for name, arg, t in walk(steps, prev is not None):
                    if name == "k" and arg % 4 == 3:
                        lo_part((u + 1) * 6 + (arg // 4 + RING))
                    elif name == "V4" and prev == "B":
                        at_least(pool, o_summed, u + (-NA))
                        pool.tensor_tensor(o_r[:, :], o_ms[:, 1 - par], neg_half[:, :], ALU.pow).then_inc(o_rooted, 1)
                    elif name == "Tail":
                        at_least_alone(pool, turn_free, turns + (t + 1))
                        for src, dst_p, dst_s in ((k_tm, outs[0], outs[2]), (v_tm, outs[1], outs[3])):
                            pool.dma_start(dst_p[:, bass.ds(cols, P)].rearrange("(j p) n -> p j n", p=P),
                                           src[:, 0:QB - 1]).then_inc(kv_stored, 16)
                            pool.dma_start(dst_s[:, bass.ds(cols, P)], src[0:SMP, QB - 1]).then_inc(kv_stored, 16)
                    elif name == "CK" and next_kind:
                        at_least_alone(pool, turned, turns + (t + 1))
                        c = cak if next_kind == "A" else cbk
                        col = ((u + (1 if next_kind == "A" else 1 - NA)) * P).value()
                        pool.dma_start(ck[:, :].rearrange("p (j n) -> p j n", n=P),
                                       c[:, bass.ds(col, P)].rearrange("(j p) n -> p j n", p=P)).then_inc(ck_loaded, 16)
                if next_kind:
                    at_least_alone(pool, av_done, (u + 1) * QB)
                    c = cav if next_kind == "A" else cbv
                    col = ((u + (1 if next_kind == "A" else 1 - NA)) * P).value()
                    pool.dma_start(cv[:, :].rearrange("p (j n) -> p j n", n=P),
                                   c[:, bass.ds(col, P)].rearrange("(j p) n -> p j n", p=P)).then_inc(cv_loaded, 16)

            for u in range(NA):
                if u >= 1 and u + 1 < NA:
                    finish_table(u + 1)
                unit(Count(u), "A", "A" if u + 1 < NA else "B", u % 2, "A" if u else None)
                if u + 2 < NA:
                    pool.wait_ge(biased, JOBS * (u + 1))
                    load_table(u + 2)

            def b_unit(u, par, next_kind="B", prev="B"):
                if next_kind:
                    at_least(pool, tab_ready, u)
                    at_least_alone(pool, biased, u * JOBS)
                    pool.tensor_scalar(tab_b[1 - par][:, :], tab_b[par][:, :], 0.5, None, ALU.mult
                                       ).then_inc(tab_ready, 1)
                unit(u, "B", next_kind, par, prev)

            b_unit(Count(NA), 0, prev="A")
            b_unit(Count(NA + 1), 1)
            with pool.Fori(0, (NB - 4) // 2) as it:
                for v in range(2):
                    b_unit(Count(NA + 2 + v, [(it, 2)]), v)
            b_unit(Count(NU - 2), 0)
            b_unit(Count(NU - 1), 1, next_kind=None)
            pool.wait_ge(o_summed, NB)
            pool.tensor_tensor(o_r[:, :], o_ms[:, 1], neg_half[:, :], ALU.pow).then_inc(o_rooted, 1)

            def root(n):
                pool.wait_ge(ms_ready, n + 1)
                pool.tensor_tensor(r_t[:, :], ms_t[:, :], neg_half[:, :], ALU.pow).then_inc(r_ready, 1)

            def split(p0, end):
                loops = (end - p0) // RING
                if loops > 1:
                    with pool.Fori(0, loops) as it:
                        for j in range(RING):
                            lo_part(Count(p0 + j, [(it, RING)]))
                    p0 += loops * RING
                for p in range(p0, end):
                    lo_part(Count(p))

            def update(n, x):
                for k in BY_POOL:
                    if k == BY_POOL[2]:
                        split((PC_FF, PC_PG)[n] + 2, (PC_FF, PC_PG)[n] + RING)
                    pool.wait_ge(block_normed, n * KB + k + 1)
                    pool.tensor_tensor(hT[:, k], hT[:, k], x[:, k], ALU.add).then_inc(h_added[0], 1)

            split(PC_GATE + 6 + RING, PC_OUT + 2 * RING)
            pool.wait_ge(m_hi, KB)
            pool.memset(down_sum, 0.0).then_inc(down_cleared, 1)
            split(PC_OUT + 2 * RING, PC_FF + 2)
            root(N_POST)
            update(0, mixed)
            split(PC_FF + RING, PC_FF + RING + 4)
            root(N_FPRE)
            split(PC_FF + RING + 4, PC_PG + 2)
            root(N_FPOST)
            update(1, down_sum)
            split(PC_PG + RING, PC_PG + RING + 4)
            root(N_PLE)
            split(PC_PG + RING + 4, PC_END)

        @block.scalar
        def _(act):
            def hi_part(p):
                slot = p.mod(RING)
                at_least(act, w_loaded[slot], (p.over(RING) + 1) * 16)
                at_least(act, w_used, p + (1 - RING))
                act.activation(w_hi[:, slot], w_raw[:, slot], ACT.Copy).then_inc(hi_done, 1)

            def square_x(t):
                act.wait_ge(x_loaded[t], 16)
                n = rows(t)
                act.activation(x_sq[0:n, t], x_tm[0:n, t], ACT.Square, accum_out=ss_x[0:n, t:t + 1]
                               ).then_inc(x_squared, 1)

            for t in range(QB - 1):
                square_x(t)

            def keep_x(j):
                act.wait_ge(x_turned, j + 1)
                act.activation(hT[:, j], x_bank(j)[:, 0:T], ACT.Copy).then_inc(x_kept[1], 1)

            act.wait_ge(gains_ready, 1)
            for k in range(KB):
                if k < RING:
                    hi_part(Count(k))
                if k % 2 and k != 3:
                    keep_x(k)
                if k == RING:
                    square_x(QB - 1)
                if k == KB - 1:
                    hi_part(Count(RING))
                    hi_part(Count(RING + 1))
                if k == 0:
                    act.wait_ge(x_turned, 1)
                    x = x_bank(0)[:, 0:T]
                else:
                    act.wait_ge(x_kept[k % 2], max(k // 2 + 1, 2))
                    x = hT[:, k]
                act.activation(act_hi[:, k], x, ACT.Copy, scale=gcol[:, G_PRE + k:G_PRE + k + 1]).then_inc(g_hi, 1)
                if k == 0:
                    keep_x(3)
            act.wait_ge(lam_ready, 1)
            act.activation(lam_s[:, 2:4], lam_s[:, 0:2], ACT.Exp).then_inc(lam_exped, 1)
            for n in range(2, 6):
                hi_part(Count(RING + n))

            def unit(u, kind, par, prev):
                steps = A_STEPS if kind == "A" else B_STEPS
                turns = turn_base(u, kind)

                def expo(i, m):
                    n, np_, b = keys(i), (P if i < QB - 1 else 2 * SMP), i % 2
                    at_least(act, biased, u * JOBS + (2 * i + m + 1))
                    act.activation(prob[b][m][0:np_, 0:n], prob[b][m][0:np_, 0:n], ACT.Exp, scale=-1.0,
                                   bias=neg_max[0:np_, b, m:m + 1],
                                   accum_out=sums[0:np_, b, m:m + 1]).then_inc(exped, 1)

                def square_output(i):
                    np_ = rows(i)
                    at_least(act, out_free, u * QB + (i + 1))
                    act.activation(o_sq[0:np_, i % 2], o_tm[par][0:np_, i], ACT.Square,
                                   accum_out=o_ms[0:np_, par, i:i + 1]).then_inc(o_squared, 1)

                for name, arg, t in walk(steps, prev is not None):
                    if name == "AV" and kind == "B" and arg:
                        square_output(arg - 1)
                    if name == "k" and arg % 4 == 3:
                        hi_part((u + 1) * 6 + (arg // 4 + RING))
                    elif name == "S":
                        for m in range(2 if arg < QB - 1 else 1):
                            expo(arg, m)
                    elif name == "T":
                        i, m = arg
                        at_least(act, turned, turns + (t + 1))
                        np_, n = (SMP, P) if arg == (QB - 1, 1) else (P, P * min(i + 1, QB - 1))
                        act.activation(probT[m][0:np_, 0:n], turn[0:np_, 0:n], ACT.Copy).then_inc(turn_free, 1)
                    elif name in ("V4", "K4"):
                        at_least(act, turned, turns + (t + 1))
                        at_least(act, kv_stored, u * 64)
                        dst = v_tm if name == "V4" else k_tm
                        act.activation(dst[:, 0:QB - 1].rearrange("p j n -> p (j n)"), turn[:, 0:SEQ], ACT.Copy
                                       ).then_inc(turn_free, 1)
                    elif name == "CK":
                        at_least(act, turned, turns + (t + 1))
                        act.activation(ckT[:, :], turn[:, 0:SEQ], ACT.Copy).then_inc(turn_free, 1)
                    elif name == "OT":
                        at_least(act, turned, turns + (t + 1))
                        out_hi(u + (-1), prev, turn[:, 0:SEQ], slice(0, SEQ))
                    elif name == "Tail" and prev is not None:
                        at_least(act, tail_copied, u)
                        out_hi(u + (-1), prev, turn[:, 2 * P:2 * P + SMP], slice(SEQ, T))
                if kind == "B":
                    square_output(QB - 1)

            def out_hi(u, kind, src, cols):
                dst = out_block(oa_hi if kind == "A" else mid_hi, u, kind, cols)
                if kind == "A":
                    act.activation(dst, src, ACT.Copy).then_inc(o_hi, 1)
                else:
                    act.activation(dst, src, ACT.Copy, scale=gcol[:, G_SUBL:G_SUBL + 1]).then_inc(o_hi, 1)

            for u in range(NA):
                unit(Count(u), "A", u % 2, "A" if u else None)
            unit(Count(NA), "B", 0, "A")
            unit(Count(NA + 1), "B", 1, "B")
            with act.Fori(0, (NB - 4) // 2) as it:
                for v in range(2):
                    unit(Count(NA + 2 + v, [(it, 2)]), "B", v, "B")
            unit(Count(NU - 2), "B", 0, "B")
            unit(Count(NU - 1), "B", 1, "B")

            def gate(n, p):
                for kh in range(2):
                    hi_part(p + (kh + RING))
                b = (n + PJ_GATE).mod(2)
                at_least(act, proj_free[b], (n + (PJ_GATE - b)).over(2) + 1)
                x = block_of(wide, n)
                act.activation(x, x, ACT.Sigmoid).then_inc(gated, 1)

            act.wait_ge(av_done, NU * QB)
            act.wait_ge(out_free, NU * QB)
            act.wait_ge(o_summed, NB)
            for n in range(3):
                act.wait_ge(proj_free[(PJ_GATE + n) % 2], (PJ_GATE + n) // 2 + 1)
                act.activation(wide[:, n], (vT, kT, qT)[n][0][:, :], ACT.Sigmoid).then_inc(gated, 1)
            gate(Count(3), Count(PC_GATE + 6))
            gate(Count(4), Count(PC_GATE + 8))
            act.wait_ge(turned, TURN_END + 1)
            out_hi(Count(NU - 1), "B", turn[:, 0:SEQ], slice(0, SEQ))
            gate(Count(5), Count(PC_GATE + 10))
            act.wait_ge(turned, TURN_END + 2)
            out_hi(Count(NU - 1), "B", turn[:, 2 * P:2 * P + SMP], slice(SEQ, T))
            with act.Fori(0, KB - 3) as it:
                for j in range(2):
                    gate(Count(6 + j, [(it, 2)]), Count(PC_GATE + 12 + 2 * j, [(it, 4)]))
            for k in range(2):
                act.wait_ge(p_turned, k + 1)
                act.activation(pT_hi[:, k], pair[k][:, 0:T], ACT.Copy).then_inc(p_hi, 1)
            with act.Fori(0, KB // RING) as it:
                for j in range(RING):
                    hi_part(Count(PC_BRA + RING + j, [(it, RING)]))
            with act.Fori(0, KB // 2) as it:
                for j in range(2):
                    n = Count(j, [(it, 2)])
                    for kh in range(2):
                        hi_part(Count(PC_BRB + RING + 2 * j + kh, [(it, RING)]))
                    at_least(act, br_mixed, n + 1)
                    act.activation(block_of(act_hi, n), block_of(wide, n), ACT.Copy).then_inc(m_hi, 1)

            def square(n, src):
                at_least(act, sq_added, Count(n - 1))
                act.activation(sq[n % 2][:, :], src, ACT.Square).then_inc(squared, 1)

            def keep_ple(half, i):
                act.wait_ge(*((w_used, PC_PLE[half] + i // 2 + 1) if i % 2 else (ple_first, half * (KB // 4) + i // 2 + 1)))
                b = (PJ_PLE[half] + i) % 2
                act.activation(halves(ple[:, half * (KB // 2) + i]), acc[b], ACT.Copy).then_inc(proj_free[b], 1)

            for m in range(KB):
                for kh in range(2):
                    hi_part(Count(PC_OUT + RING + 2 * m + kh))
                act.wait_ge(proj_free[(PJ_OUT + m) % 2], (PJ_OUT + m) // 2 + 1)
                square(m, mixed[:, m])

            def next_input(n, scale):
                p = (PC_FF, PC_PG)[n]
                for k in range(KB):
                    if k == 1:
                        keep_ple(n, KB // 2 - 1)
                        hi_part(Count(PC_PLE[n] + RING + 1))
                    if k == KB - 1:
                        hi_part(Count(p + RING))
                        hi_part(Count(p + RING + 1))
                    for done_by, added in ((BY_POOL, h_added[0]), (BY_VECTOR, h_added[1])):
                        if k in done_by:
                            act.wait_ge(added, n * len(done_by) + done_by.index(k) + 1)
                    if scale is None:
                        act.activation(act_hi[:, k], hT[:, k], ACT.Copy).then_inc(h_hi, 1)
                    else:
                        act.activation(act_hi[:, k], hT[:, k], ACT.Copy, scale=gcol[:, scale + k:scale + k + 1]
                                       ).then_inc(h_hi, 1)

            for i in range(KB // 2 - 1):
                keep_ple(0, i)
                if i % 2:
                    hi_part(Count(PC_PLE[0] + RING + i // 2))
            next_input(0, G_FPRE)

            def up_hi_part(n, count):
                at_least(act, up_ready, count)
                act.activation(block_of(mid_hi, n), up_a[:, :], ACT.Copy).then_inc(up_hi, 1)

            def keep_up(j):
                act.wait_ge(w_used, PC_FF + (3 + j if j < 2 else 2 * j + 2))
                b = (PJ_FF + j) % 2
                act.activation(halves(up_raw[j]), acc[b], ACT.Copy).then_inc(proj_free[b], 1)

            for j in range(2):
                keep_up(j)
                hi_part(Count(PC_FF + RING + 2 + j))
            for k in range(KB):
                square(KB + k, hT[:, k])
            for j in range(2, KB):
                for kh in range(2):
                    hi_part(Count(PC_FF + RING + 2 * j + kh))
                if j < RAW:
                    keep_up(j)
                for i in range(2 * j - RAW, 2 * j - RAW + 2) if RAW // 2 <= j < RAW else (j,) if j >= RAW else ():
                    up_hi_part(Count(i), Count(i + 1))

            def up_group(group):
                with act.Fori(0, KB // 2) as it:
                    for j in range(2):
                        for kh in range(2):
                            hi_part(group * (4 * KB) + Count(PC_FF + RING + 2 * j + kh, [(it, RING)]))
                        up_hi_part(Count(j, [(it, 2)]), group * KB + Count(j + 1, [(it, 2)]))

            def down_group(group):
                with act.Fori(0, KB // 2) as it:
                    for j in range(RING):
                        hi_part(group * (4 * KB) + Count(PC_FF + 2 * KB + RING + j, [(it, RING)]))

            down_group(Count(0))
            with act.Fori(1, FG - 1) as g:
                up_group(Count(0, [(g, 1)]))
                down_group(Count(0, [(g, 1)]))
            last_piece = PC_FF + (FG - 1) * 4 * KB
            up_group(Count(FG - 1))
            for k in range(KB):
                for kh in range(2):
                    hi_part(Count(last_piece + 2 * KB + RING + 2 * k + kh))
                job = PJ_FF + (FG - 1) * 2 * KB + KB + k
                act.wait_ge(proj_free[job % 2], job // 2 + 1)
                square(2 * KB + k, down_sum[:, k])
            for i in range(KB // 2 - 1):
                keep_ple(1, i)
                if i % 2:
                    hi_part(Count(PC_PLE[1] + RING + i // 2))
            next_input(1, None)

            def y_rows(m):
                act.wait_ge(y_turned, m + 1)
                if m >= 2:
                    act.wait_ge(y_stored[m % 2], 32 * (m // 2))
                act.activation(y_tm[m % 2][:, 0:QB - 1], pair[m % 2][:, 0:SEQ].rearrange("p (j n) -> p j n", n=P), ACT.Copy)
                act.activation(y_tm[m % 2][0:SMP, QB - 1], pair[m % 2][0:SMP, SEQ:SEQ + P], ACT.Copy
                               ).then_inc(y_copied, 1)

            def gate_ple(m):
                act.wait_ge(w_used, PC_PG + (3 + m if m < 2 else 2 * m + 2))
                b = (PJ_PG + m) % 2
                act.activation(halves(y_f[m]), acc[b], ACT.Sigmoid).then_inc(proj_free[b], 1)

            for m in range(2):
                gate_ple(m)
                hi_part(Count(PC_PG + RING + 2 + m))
            for k in range(KB):
                square(3 * KB + k, ple[:, k])
            for m in range(2, KB):
                for kh in range(2):
                    if PC_PG + RING + 2 * m + kh < PC_END:
                        hi_part(Count(PC_PG + RING + 2 * m + kh))
                gate_ple(m)
                for i in Y_AFTER[m]:
                    y_rows(i)

        @block.vector
        def _(dve):
            own = [Count(0)]

            def done(ins):
                ins.then_inc(vec, 1)
                own[0] = own[0] + 1

            def settle():
                at_least(dve, vec, own[0])

            def loop(n, per):
                start = own[0]

                def enter(register):
                    own[0] = start + Count(0, [(register, per)])

                def leave(register):
                    got = own[0].const - start.const
                    assert got == per, got
                    own[0] = start + per * n
                return enter, leave

            for b in range(2):
                dve.memset(q_pad[b][:, :], 0.0)
                dve.memset(o_tm[b][SMP:P, QB - 1], 0.0)
                dve.memset(o_ms[SMP:P, b, QB - 1:QB], 0.0)
            dve.wait_ge(rows_turned, 1)
            dve.tensor_copy(gcol[:, 0:8], score[:, 0:8]).then_inc(gains_ready, 1)

            def mean_x(t):
                n = rows(t)
                dve.wait_ge(x_squared, t + 1)
                dve.tensor_scalar(sq_x[0:n, t:t + 1], ss_x[0:n, t:t + 1], 1.0 / D, EPS, ALU.mult, ALU.add
                                  ).then_inc(x_mean, 1)

            def keep_x(j):
                dve.wait_ge(x_turned, j + 1)
                dve.tensor_copy(hT[:, j], x_bank(j)[:, 0:T]).then_inc(x_kept[0], 1)

            for t in range(QB - 1):
                mean_x(t)
            for k in range(KB):
                if k % 2 == 0 and k + 2 < KB:
                    keep_x(k + 2)
                dve.wait_ge(g_hi, k + 1)
                dve.scalar_tensor_tensor(out=act_lo[:, k], in0=hT[:, k] if k else x_bank(0)[:, 0:T], scalar=gcol[:, G_PRE + k:G_PRE + k + 1],
                                         in1=act_hi[:, k].bitcast(F32), op0=ALU.mult, op1=ALU.subtract
                                             ).then_inc(g_split, 1)
                if k == 0:
                    keep_x(0)
                if k == 2:
                    dve.wait_ge(rel_loaded, 16)
                    dve.tensor_copy(band_sb[:, 0:P], band_sb[:, P:P + 1].broadcast_to([2 * NA, P])
                                    ).then_inc(band_made, 1)
                if k == RING:
                    mean_x(QB - 1)
            dve.wait_ge(rows_turned, 2)
            done(dve.tensor_copy(gcol[:, 8:41], turn[:, 8:41]))
            settle()
            dve.tensor_scalar(gcol[:, G_SUBL:G_SUBL + 1], gcol[:, G_SUB:G_SUB + 1], 1.0 - LAM0, None,
                              ALU.mult).then_inc(gains_ready, 1)
            dve.wait_ge(x_row_ready, 1)
            done(dve.tensor_copy(x_row[:, :], score[:, 0:T]))
            settle()
            def projected(u, n, gates=False, pieces=None):
                b = (u * 3 + (PJ_IN + n)).mod(2)
                par = u.mod(2)
                at_least(dve, w_used, u * 6 + (pieces or 2 * n + 2))
                dst = (vT, kT, qT)[n][par][:, :]
                if n < 2 or gates:
                    dve.tensor_tensor(halves(dst), acc[b], halves(x_row[:, :]), ALU.mult).then_inc(proj_free[b], 1)
                else:
                    dve.scalar_tensor_tensor(out=halves(dst), in0=acc[b], scalar=0.125, in1=halves(x_row[:, :]),
                                             op0=ALU.mult, op1=ALU.mult).then_inc(proj_free[b], 1)
                    at_least(dve, proj_free[b], (u * 3 + (PJ_IN + n - b)).over(2) + 1)
                    dve.tensor_copy(q_pad[par][0:64, 0:SMP], dst[0:64, SEQ:T])
                    dve.tensor_copy(q_pad[par][64:P, SMP:2 * SMP], dst[64:P, SEQ:T]).then_inc(q_padded, 1)

            for n in range(2):
                projected(Count(0), n, pieces=3 + n)
            dve.wait_ge(lam_loaded, 16)
            done(dve.tensor_tensor(lam_pr[:, 0], lam_in[:, 0], lam_in[:, 1], ALU.mult))
            done(dve.tensor_tensor(lam_pr[:, 1], lam_in[:, 2], lam_in[:, 3], ALU.mult))
            settle()
            dve.tensor_reduce(lam_s[:, 0:2], lam_pr[:, :, :], AX.X, ALU.add).then_inc(lam_ready, 1)
            dve.wait_ge(dist_made, 1)
            done(dve.tensor_copy(dist[:, :], dist_i[:, :]))
            settle()
            done(dve.scalar_tensor_tensor(out=tab_b[0][:, :], in0=dist[:, :], scalar=-1.0, in1=dist[:, :],
                                          op0=ALU.mult, op1=ALU.max))
            settle()
            done(dve.memset(tab_b[0][0:SMP, TW - SMP:TW], -2e2 * MASK))
            settle()
            done(dve.tensor_scalar(tab_b[0][:, :], tab_b[0][:, :], -0.5, None, ALU.mult))
            dve.wait_ge(lam_exped, 1)
            done(dve.tensor_tensor(lam_s[:, 0:1], lam_s[:, 3:4], lam_s[:, 2:3], ALU.subtract))
            settle()
            done(dve.tensor_scalar(neg_lam[:, :], lam_s[:, 0:1], -LAM0, None, ALU.add))
            projected(Count(0), 2)

            def unit(u, kind, par, prev):
                steps = A_STEPS if kind == "A" else B_STEPS
                turns = turn_base(u, kind)

                def bias(i, m):
                    n, b = keys(i), i % 2
                    at_least_alone(dve, scored, u * JOBS + (2 * i + m + 1))
                    parts = [(slice(0, P), m, TW - n)] if i < QB - 1 else [(slice(0, SMP), 0, 0), (slice(SMP, P), 1, SMP)]
                    for rs, head, first in parts:
                        tab = tab_a[par][rs, head, first:first + n] if kind == "A" else tab_b[par][rs, first:first + n]
                        last = dve.tensor_tensor_reduce(prob[b][m][rs, 0:n], score[rs, 512 * m:512 * m + n], tab,
                                                        -1.0, 3e38, ALU.add, ALU.min, neg_max[rs, b, m:m + 1])
                    last.then_inc(biased, 1)

                def sample_outputs():
                    o = o_tm[par][0:SMP, QB - 1]
                    at_least(dve, exped, (u + 1) * JOBS)
                    at_least(dve, out_free, u * QB + (QB - 2))
                    done(dve.reciprocal(r_sum[:, 0, 0:1], sums[:, 0, 0:1]))
                    settle()
                    at_least(dve, av_done, (u + 1) * QB)
                    r0, r1 = r_sum[0:SMP, 0, 0:1], r_sum[SMP:P, 0, 0:1]
                    if kind == "A":
                        dve.tensor_scalar(o[:, 0:64], outp[0:SMP, 0:64], r0, None, ALU.mult)
                        dve.tensor_scalar(o[:, 64:P], outp[SMP:P, 64:P], r1, None, ALU.mult).then_inc(out_free, 1)
                    else:
                        done(dve.tensor_scalar(o_second[:, :], outp[SMP:P, 0:P], r1, None, ALU.mult))
                        done(dve.tensor_scalar(o, outp[0:SMP, 0:P], r0, None, ALU.mult))
                        settle()
                        dve.scalar_tensor_tensor(out=o, in0=o_second[:, :], scalar=neg_lam[0:SMP, :], in1=o,
                                                 op0=ALU.mult, op1=ALU.add).then_inc(out_free, 1)

                for name, arg, t in walk(steps, prev is not None):
                    if name == "k" and arg % 8 == 7:
                        projected(u + 1, arg // 8, u.const == NU - 1)
                    elif name == "S":
                        if arg == 0:
                            at_least(dve, tab_ready, u + int(kind == "A"))
                        for m in range(2 if arg < QB - 1 else 1):
                            bias(arg, m)
                    elif name == "Tail":
                        at_least(dve, turned, turns + (t + 1))
                        dve.tensor_copy(v_tm[0:SMP, QB - 1], turn[0:SMP, 0:P])
                        if prev is None:
                            dve.tensor_copy(k_tm[0:SMP, QB - 1], turn[0:SMP, P:2 * P]).then_inc(turn_free, 1)
                        else:
                            dve.tensor_copy(k_tm[0:SMP, QB - 1], turn[0:SMP, P:2 * P]).then_inc(tail_copied, 1)
                            at_least(dve, o_hi, u * 2)
                            out_lo(u + (-1), prev, turn[:, 2 * P:2 * P + SMP], slice(SEQ, T))
                    elif name == "OT":
                        if prev == "B":
                            normalise(u + (-1), 1 - par)
                        at_least(dve, o_hi, u * 2 + (-1))
                        out_lo(u + (-1), prev, turn[:, 0:SEQ], slice(0, SEQ))
                    elif name == "C":
                        i, b, np_ = arg, arg % 2, rows(arg)
                        at_least(dve, out_free, u * QB + max(i - 1, 0))
                        at_least(dve, exped, u * JOBS + (2 * i + 2))
                        done(dve.reciprocal(r_sum[0:np_, b], sums[0:np_, b]))
                        settle()
                        done(dve.scalar_tensor_tensor(out=c_map[0:np_, b:b + 1], in0=sums[0:np_, b, 0:1],
                                                      scalar=r_sum[0:np_, b, 1:2], in1=neg_lam[0:np_, :],
                                                      op0=ALU.mult, op1=ALU.mult))
                        settle()
                        n = keys(i)
                        dve.scalar_tensor_tensor(out=prob[b][0][0:np_, 0:n], in0=prob[b][1][0:np_, 0:n],
                                                 scalar=c_map[0:np_, b:b + 1], in1=prob[b][0][0:np_, 0:n],
                                                 op0=ALU.mult, op1=ALU.add).then_inc(combined, 1)
                    elif name == "AV":
                        i, b, np_ = arg, arg % 2, rows(arg)
                        if i == QB - 1:
                            sample_outputs()
                        elif kind == "A":
                            at_least(dve, exped, u * JOBS + (2 * i + 2))
                            done(dve.reciprocal(r_sum[0:np_, b], sums[0:np_, b]))
                            settle()
                            at_least(dve, av_done, u * QB + (i + 1))
                            for m in range(2):
                                last = dve.tensor_scalar(o_tm[par][0:np_, i, 64 * m:64 * m + 64], outp[0:np_, 64 * m:64 * m + 64],
                                                         r_sum[0:np_, b, m:m + 1], None, ALU.mult)
                            last.then_inc(out_free, 1)
                        else:
                            at_least(dve, av_done, u * QB + (i + 1))
                            dve.tensor_scalar(o_tm[par][0:np_, i], outp[0:np_, 0:P], r_sum[0:np_, b, 0:1], None,
                                              ALU.mult).then_inc(out_free, 1)
                if kind == "B":
                    at_least(dve, o_squared, (u + (1 - NA)) * QB)
                    dve.tensor_scalar(o_ms[:, par], o_ms[:, par], 1.0 / P, EPS, ALU.mult, ALU.add).then_inc(o_summed, 1)

            def normalise(u, par):
                at_least(dve, o_rooted, u + (1 - NA))
                dve.tensor_tensor(o_tm[par][:, :, :], o_tm[par][:, :, :], o_r[:, :].unsqueeze(2).broadcast_to([P, QB, P]),
                                  ALU.mult).then_inc(o_normed, 1)

            def out_lo(u, kind, src, cols):
                hi, lo = (oa_hi, oa_lo) if kind == "A" else (mid_hi, mid_lo)
                hi, lo = out_block(hi, u, kind, cols).bitcast(F32), out_block(lo, u, kind, cols)
                if kind == "A":
                    dve.tensor_tensor(lo, src, hi, ALU.subtract).then_inc(turn_free, 1)
                else:
                    dve.scalar_tensor_tensor(out=lo, in0=src, scalar=gcol[:, G_SUBL:G_SUBL + 1], in1=hi,
                                             op0=ALU.mult, op1=ALU.subtract).then_inc(turn_free, 1)

            for u in range(NA):
                unit(Count(u), "A", u % 2, "A" if u else None)
            unit(Count(NA), "B", 0, "A")
            unit(Count(NA + 1), "B", 1, "B")
            enter, leave = loop((NB - 4) // 2, 2 * (2 * (QB - 1) + 3))
            with dve.Fori(0, (NB - 4) // 2) as it:
                enter(it)
                for v in range(2):
                    unit(Count(NA + 2 + v, [(it, 2)]), "B", v, "B")
                leave(it)
            unit(Count(NU - 2), "B", 0, "B")
            unit(Count(NU - 1), "B", 1, "B")
            def gate(n, p):
                at_least(dve, w_used, p + 2)
                b = (n + PJ_GATE).mod(2)
                dve.tensor_tensor(halves(block_of(wide, n)), acc[b], halves(x_row[:, :]), ALU.mult
                                  ).then_inc(proj_free[b], 1)

            normalise(Count(NU - 1), 1)
            dve.wait_ge(av_done, NU * QB)
            gate(Count(3), Count(PC_GATE + 6))
            gate(Count(4), Count(PC_GATE + 8))
            dve.wait_ge(o_hi, 2 * NU - 1)
            out_lo(Count(NU - 1), "B", turn[:, 0:SEQ], slice(0, SEQ))
            gate(Count(5), Count(PC_GATE + 10))
            dve.wait_ge(o_hi, 2 * NU)
            out_lo(Count(NU - 1), "B", turn[:, 2 * P:2 * P + SMP], slice(SEQ, T))
            dve.wait_ge(kv_stored, 64 * NU)
            with dve.Fori(0, KB - 3) as it:
                for j in range(2):
                    gate(Count(6 + j, [(it, 2)]), Count(PC_GATE + 12 + 2 * j, [(it, 4)]))
            for k in range(2):
                dve.wait_ge(p_hi, k + 1)
                dve.tensor_tensor(pT_lo[:, k], pair[k][:, 0:T], pT_hi[:, k].bitcast(F32), ALU.subtract
                                  ).then_inc(p_split, 1)
            dve.memset(sq_sum[:, T:QB * P], 0.0).then_inc(sq_cleared, 1)

            dve.wait_ge(gated, 2 * KB)
            with dve.Fori(0, KB // RING) as it:
                for j in range(RING):
                    at_least(dve, w_used, Count(PC_BRA + j + 1, [(it, RING)]))
                    b = (PJ_BRA + j) % 2
                    w = block_of(wide, Count(j, [(it, RING)]))
                    dve.tensor_tensor(halves(w), acc[b], halves(w), ALU.mult).then_inc(proj_free[b], 1)
            with dve.Fori(0, KB // 2) as it:
                for j in range(2):
                    n = Count(j, [(it, 2)])
                    at_least(dve, w_used, Count(PC_BRB + 2 * j + 2, [(it, RING)]))
                    b = (PJ_BRB + j) % 2
                    wa, wb = block_of(wide, n), block_of(wide, n + KB)
                    dve.tensor_tensor(halves(wb), acc[b], halves(wb), ALU.mult).then_inc(proj_free[b], 1)
                    at_least(dve, proj_free[b], Count((PJ_BRB + j) // 2 + 1, [(it, 1)]))
                    dve.tensor_tensor(wa, wa, wb, ALU.add).then_inc(br_mixed, 1)
                    at_least(dve, m_hi, n + 1)
                    dve.tensor_tensor(block_of(act_lo, n), wa, block_of(act_hi, n).bitcast(F32), ALU.subtract
                                      ).then_inc(m_split, 1)

            def add_square(n):
                dve.wait_ge(squared, n + 1)
                if n % KB == 0:
                    dve.tensor_copy(sq_sum[:, 0:T], sq[n % 2][:, :]).then_inc(sq_added, 1)
                else:
                    dve.wait_ge(sq_added, n)
                    dve.tensor_tensor(sq_sum[:, 0:T], sq_sum[:, 0:T], sq[n % 2][:, :], ALU.add).then_inc(sq_added, 1)

            def row_of_norm(n):
                dve.wait_ge(sum_turned, n + 1)
                dve.tensor_scalar(ms_t[:, :], turn[:, 0:QB], 1.0 / D, EPS, ALU.mult, ALU.add).then_inc(ms_ready, 1)
                dve.wait_ge(row_ready, n + 1)

            def normed(x, k, g, row=score[:, 0:T]):
                return dve.scalar_tensor_tensor(out=x[:, k], in0=x[:, k], scalar=gcol[:, g + k:g + k + 1],
                                                in1=row, op0=ALU.mult, op1=ALU.mult)

            for m in range(KB):
                b = (PJ_OUT + m) % 2
                dve.wait_ge(w_used, PC_OUT + 2 * m + 2)
                dve.tensor_copy(halves(mixed[:, m]), acc[b]).then_inc(proj_free[b], 1)
                if m:
                    add_square(m - 1)
            add_square(KB - 1)

            def update(n, x, g):
                def rest(k):
                    dve.wait_ge(h_hi, n * KB + k + 1)
                    if n == 0:
                        dve.scalar_tensor_tensor(out=act_lo[:, k], in0=hT[:, k], scalar=gcol[:, G_FPRE + k:G_FPRE + k + 1],
                                                 in1=act_hi[:, k].bitcast(F32), op0=ALU.mult, op1=ALU.subtract
                                                     ).then_inc(h_split, 1)
                    else:
                        dve.tensor_tensor(act_lo[:, k], hT[:, k], act_hi[:, k].bitcast(F32), ALU.subtract
                                          ).then_inc(h_split, 1)

                for k in range(KB):
                    normed(x, k, g).then_inc(block_normed, 1)
                    if k in BY_VECTOR:
                        dve.wait_ge(block_normed, n * KB + k + 1)
                        dve.tensor_tensor(hT[:, k], hT[:, k], x[:, k], ALU.add).then_inc(h_added[1], 1)
                    if k >= 2:
                        rest(k - 2)
                rest(KB - 2)
                rest(KB - 1)

            row_of_norm(N_POST)
            update(0, mixed, G_POST)
            for k in range(KB):
                add_square(KB + k)
            row_of_norm(N_FPRE)
            dve.tensor_copy(r_row[:, :], score[:, 0:T]).then_inc(row_read, 1)
            dve.wait_ge(row_read, 1)
            dve.wait_ge(down_cleared, 1)

            def up(n, src, free, count):
                ins = dve.tensor_tensor(halves(up_t[:, :]), src, halves(r_row[:, :]), ALU.mult)
                if free is None:
                    done(ins)
                    settle()
                else:
                    ins.then_inc(free[0], 1)
                    at_least(dve, *free)
                dve.scalar_tensor_tensor(out=up_a[:, :], in0=up_t[:, :], scalar=0.0, in1=up_t[:, :],
                                         op0=ALU.max, op1=ALU.mult).then_inc(up_ready, 1)
                at_least(dve, up_hi, count)
                dve.tensor_tensor(block_of(mid_lo, n), up_a[:, :], block_of(mid_hi, n).bitcast(F32),
                                  ALU.subtract).then_inc(up_split, 1)

            def up_blocks(first, n, group):
                with dve.Fori(0, n // 2) as it:
                    for j in range(2):
                        b = (PJ_FF + j) % 2
                        at_least(dve, w_used, group * (4 * KB) + Count(PC_FF + 2 * (first + j) + 2, [(it, RING)]))
                        up(Count(first + j, [(it, 2)]), acc[b],
                           (proj_free[b], group * KB + Count((PJ_FF + first + j) // 2 + 1, [(it, 1)])),
                           group * KB + Count(first + j + 1, [(it, 2)]))

            def down_blocks(group):
                with dve.Fori(0, KB // 2) as it:
                    for j in range(2):
                        b = (PJ_FF + KB + j) % 2
                        at_least(dve, w_used, group * (4 * KB) + Count(PC_FF + 2 * KB + 2 * j + 2, [(it, RING)]))
                        d = block_of(wide, Count(j, [(it, 2)]))
                        dve.tensor_tensor(halves(d), acc[b], halves(d), ALU.add).then_inc(proj_free[b], 1)

            for j in range(RAW):
                dve.wait_ge(proj_free[(PJ_FF + j) % 2], (PJ_FF + j) // 2 + 1)
                up(Count(j), halves(up_raw[j]), None, Count(j + 1))
            up_blocks(RAW, KB - RAW, Count(0))
            down_blocks(Count(0))
            with dve.Fori(1, FG - 1) as g:
                up_blocks(0, KB, Count(0, [(g, 1)]))
                down_blocks(Count(0, [(g, 1)]))
            up_blocks(0, KB, Count(FG - 1))
            for k in range(KB):
                job = PJ_FF + (FG - 1) * 2 * KB + KB + k
                dve.wait_ge(w_used, PC_FF + (FG - 1) * 4 * KB + 2 * KB + 2 * k + 2)
                dve.tensor_tensor(halves(down_sum[:, k]), acc[job % 2], halves(down_sum[:, k]), ALU.add
                                  ).then_inc(proj_free[job % 2], 1)
                if k:
                    add_square(2 * KB + k - 1)
            add_square(3 * KB - 1)
            row_of_norm(N_FPOST)
            update(1, down_sum, G_FPOST)
            for k in range(KB):
                add_square(3 * KB + k)
            row_of_norm(N_PLE)
            done(dve.tensor_copy(r_row[:, :], score[:, 0:T]))
            settle()
            for m in range(KB):
                done(normed(ple, m, G_PLE, r_row[:, :]))
                dve.wait_ge(proj_free[(PJ_PG + m) % 2], (PJ_PG + m) // 2 + 1)
                settle()
                done(dve.tensor_tensor(y_f[m], y_f[m], ple[:, m], ALU.mult))
                settle()
                dve.tensor_tensor(y_f[m], y_f[m], hT[:, m], ALU.add).then_inc(y_ready, 1)

        @block.tensor
        def _(pe):
            def wait_projection(n):
                b = n.mod(2)
                at_least(pe, proj_free[b], (n + (-b)).over(2))

            def k_steps(n, p, hi, lo, blocks=KB, input_ready=None, apart=1):
                out = acc[n.mod(2)]
                for k in range(blocks):
                    if k == 0:
                        wait_projection(n)
                    if k % 4 == 0:
                        at_least(pe, lo_done, p + (apart * (k // 4) + 1))
                    if input_ready:
                        input_ready(k)
                    slot, at = (p + apart * (k // 4)).mod(RING), slice(P * (k % 4), P * (k % 4) + P)
                    for s, (w, x) in enumerate(((w_hi, hi), (w_lo, hi), (w_hi, lo))):
                        for h in range(2):
                            last = pe.matmul(out[:, h], w[:, slot, at], x[:, k, HALF * h:HALF * h + HALF],
                                             start=(k == 0 and s == 0), stop=(k == blocks - 1 and s == 2))
                    if k % 4 == 3:
                        last.then_inc(w_used, 1)
                    yield

            def project(*args, **kw):
                for _ in k_steps(*args, **kw):
                    pass

            def unit_steps(u):
                for n in range(3):
                    yield from k_steps(u * 3 + (PJ_IN + n), u * 6 + 2 * n, act_hi, act_lo)

            def two_tasks(n, p, ready, before, between=None):
                tasks = [k_steps(Count(n + j), Count(p + j), act_hi, act_lo, apart=2) for j in range(2)]
                for k in range(KB):
                    pe.wait_ge(ready, before + k + 1)
                    for task in tasks:
                        next(task)
                    if between:
                        between(k)

            def row_matmuls(r, valid):
                for t in range(QB):
                    n = valid(t)
                    last = pe.matmul(score[:, P * t:P * t + rows(t)], r[0:n, t:t + 1].broadcast_to([n, P]),
                                     ident[0:n, 0:rows(t)], start=True, stop=True)
                return last

            pe.wait_ge(consts, 1)
            pe.wait_ge(first_row_loaded, 16)
            pe.transpose(score[:, 0:8], gain_rows[0:8, :], ident[0:8, 0:8]).then_inc(rows_turned, 1)

            def turn_x(j, t):
                n = rows(t)
                last = pe.transpose(x_bank(j)[:, P * t:P * t + n], x_tm[0:n, t, P * j:P * j + P], ident[0:n, 0:n])
                if t == QB - 1:
                    last.then_inc(x_turned, 1)

            pe.wait_ge(gains_ready, 1)
            for t in range(QB):
                pe.wait_ge(x_loaded[t], 16)
                for j in range(X_EARLY):
                    turn_x(j, t)

            def in_between(k):
                for j in range(X_EARLY + k, X_EARLY + k + 1) if k < KB - X_EARLY else ():
                    pe.wait_ge(x_kept[j % 2], j // 2)
                    for t in range(QB):
                        turn_x(j, t)
                if k == KB - 3:
                    for b in range(2):
                        pe.wait_ge(x_kept[b], KB // 2)
                    pe.wait_ge(rows_loaded, 16 * 5)
                    pe.transpose(turn[:, 0:41], gain_rows[:, :], ident[0:41, 0:41]).then_inc(rows_turned, 1)
                    pe.wait_ge(x_rooted, QB)
                    row_matmuls(r_x, rows).then_inc(x_row_ready, 1)

            for b in range(2):
                pe.wait_ge(x_kept[b], 1)
            two_tasks(PJ_IN, 0, g_split, 0, between=in_between)
            project(Count(PJ_IN + 2), Count(4), act_hi, act_lo)
            pe.wait_ge(gains_ready, 2)

            def unit(u, kind, par, prev):
                steps = A_STEPS if kind == "A" else B_STEPS
                turns = turn_base(u, kind)
                projected = unit_steps(u + 1)

                def scores(i, m):
                    n, h = keys(i), slice(64 * m, 64 * m + 64)
                    at_least_alone(pe, biased, u * JOBS + (2 * i + m - 1 if i else 0))
                    pe.matmul(score[:, 512 * m:512 * m + n], qT[par][h, P * i:P * i + P], kT[par][h, 0:n],
                              start=True, stop=True).then_inc(scored, 1)

                def sample_scores():
                    at_least(pe, q_padded, u + 1)
                    at_least_alone(pe, biased, u * JOBS + (JOBS - 1))
                    pe.matmul(score[:, 0:SEQ], q_pad[par][:, :], ckT[:, :], start=True, stop=True)
                    pe.matmul(score[:, SEQ:T], q_pad[par][:, :], kT[par][:, SEQ:T], start=True, stop=True
                              ).then_inc(scored, 1)

                for name, arg, t in walk(steps, prev is not None):
                    if name == "k":
                        next(projected)
                        continue
                    if t is not None:
                        at_least_alone(pe, turn_free, turns + t)
                    if name == "S":
                        if arg == 0:
                            for n in (1, 2):
                                job = u * 3 + (PJ_IN + n)
                                b = job.mod(2)
                                at_least(pe, proj_free[b], (job + (-b)).over(2) + 1)
                        if arg == QB - 1:
                            sample_scores()
                        else:
                            scores(arg, 0)
                            scores(arg, 1)
                    elif name in ("V4", "K4"):
                        src = vT[par] if name == "V4" else kT[par]
                        for j in range(QB - 1):
                            last = pe.transpose(turn[:, P * j:P * j + P], src[:, P * j:P * j + P], ident[:, :])
                        last.then_inc(turned, 1)
                    elif name == "CK":
                        at_least(pe, ck_loaded, (u + 1) * 16)
                        for j in range(QB - 1):
                            last = pe.transpose(turn[:, P * j:P * j + P], ck[:, P * j:P * j + P], ident[:, :])
                        last.then_inc(turned, 1)
                    elif name == "Tail":
                        last = pe.transpose(turn[0:SMP, 0:P], vT[par][:, SEQ:T], ident[:, :])
                        last = pe.transpose(turn[0:SMP, P:2 * P], kT[par][:, SEQ:T], ident[:, :])
                        if prev is not None:
                            last = out_tail(1 - par)
                        last.then_inc(turned, 1)
                    elif name == "OT":
                        outputs_ready(u + (-1), prev)
                        out_main(1 - par)
                    elif name == "T":
                        i, m = arg
                        if i == QB - 1:
                            at_least_alone(pe, exped, (u + 1) * JOBS)
                        elif kind == "A":
                            at_least_alone(pe, exped, u * JOBS + (2 * i + m + 1))
                        else:
                            at_least_alone(pe, combined, (u + (-NA)) * (QB - 1) + (i + 1))
                        if arg == (QB - 1, 1):
                            last = pe.transpose(turn[0:SMP, 0:P], prob[0][0][:, SEQ:T], ident[:, :])
                        else:
                            for j in range(min(i + 1, QB - 1)):
                                last = pe.transpose(turn[:, P * j:P * j + P], prob[i % 2][0 if i == QB - 1 else m][:, P * j:P * j + P],
                                                    ident[:, :])
                        last.then_inc(turned, 1)
                    elif name == "AV":
                        i = arg
                        np_ = rows(i)
                        last_turn = max(tt for nn, aa, tt in walk(steps, prev is not None)
                                        if nn == "T" and aa[0] == i)
                        at_least(pe, turn_free, turns + (last_turn + 1))
                        at_least(pe, out_free, u * QB + i)
                        if i == QB - 1:
                            at_least(pe, cv_loaded, (u + 1) * 16)
                        if i == QB - 1:
                            for j in range(QB):
                                p_t, v = ((probT[0][:, P * j:P * j + P], cv[:, P * j:P * j + P]) if j < QB - 1 else
                                          (probT[1][0:SMP, 0:P], v_tm[0:SMP, j]))
                                last = pe.matmul(outp[:, 0:P], p_t, v, start=(j == 0), stop=(j == QB - 1))
                        else:
                            for m in range(2 if kind == "A" else 1):
                                c = slice(64 * m, 64 * m + 64) if kind == "A" else slice(0, P)
                                for j in range(i + 1):
                                    last = pe.matmul(outp[:, c], probT[m][:, P * j:P * j + P], v_tm[:, j, c],
                                                     start=(j == 0), stop=(j == i))
                        last.then_inc(av_done, 1)

            def outputs_ready(u, kind):
                if kind == "A":
                    at_least(pe, out_free, (u + 1) * QB)
                else:
                    at_least(pe, o_normed, u + (1 - NA))

            def out_main(b):
                for j in range(QB - 1):
                    last = pe.transpose(turn[:, P * j:P * j + P], o_tm[b][:, j], ident[:, :])
                last.then_inc(turned, 1)

            def out_tail(b):
                return pe.transpose(turn[:, 2 * P:2 * P + SMP], o_tm[b][0:SMP, QB - 1], ident[0:SMP, 0:SMP])

            for u in range(NA):
                unit(Count(u), "A", u % 2, "A" if u else None)
            unit(Count(NA), "B", 0, "A")
            unit(Count(NA + 1), "B", 1, "B")
            with pe.Fori(0, (NB - 4) // 2) as it:
                for v in range(2):
                    unit(Count(NA + 2 + v, [(it, 2)]), "B", v, "B")
            unit(Count(NU - 2), "B", 0, "B")
            unit(Count(NU - 1), "B", 1, "B")

            for n in range(3, 5):
                project(Count(PJ_GATE + n), Count(PC_GATE + 2 * n), act_hi, act_lo)
            outputs_ready(Count(NU - 1), "B")
            pe.wait_ge(turn_free, TURN_END)
            out_main(1)
            project(Count(PJ_GATE + 5), Count(PC_GATE + 10), act_hi, act_lo)
            pe.wait_ge(turn_free, TURN_END + 1)
            out_tail(1).then_inc(turned, 1)
            with pe.Fori(0, KB - 3) as it:
                for j in range(2):
                    project(Count(PJ_GATE + 6 + j, [(it, 2)]), Count(PC_GATE + 12 + 2 * j, [(it, RING)]), act_hi, act_lo)
            pe.wait_ge(p_loaded, 32)
            pe.wait_ge(turn_free, TURN_END + 2)
            for k in range(2):
                for t in range(QB):
                    n = rows(t)
                    last = pe.transpose(pair[k][:, P * t:P * t + n], p_tm[0:n, t, P * k:P * k + P], ident[0:n, 0:n])
                last.then_inc(p_turned, 1)
            with pe.Fori(0, KB // RING) as it:
                for j in range(RING):
                    project(Count(PJ_BRA + j, [(it, RING)]), Count(PC_BRA + j, [(it, RING)]), oa_hi, oa_lo, blocks=NA)
            with pe.Fori(0, KB // 2) as it:
                for j in range(2):
                    project(Count(PJ_BRB + j, [(it, 2)]), Count(PC_BRB + 2 * j, [(it, RING)]), mid_hi, mid_lo)
            with pe.Fori(0, KB // 2) as it:
                for j in range(2):
                    project(Count(PJ_OUT + j, [(it, 2)]), Count(PC_OUT + 2 * j, [(it, RING)]), act_hi, act_lo,
                            input_ready=lambda k: pe.wait_ge(m_split, k + 1))

            def project_ple(half, i):
                if half == i == 0:
                    pe.wait_ge(p_split, 2)
                n, p = PJ_PLE[half] + i, Count(PC_PLE[half] + i // 2)
                wait_projection(Count(n))
                at_least(pe, lo_done, p + 1)
                for k in range(2):
                    at = slice(2 * P * k + P * (i % 2), 2 * P * k + P * (i % 2) + P)
                    for s, (w, x) in enumerate(((w_hi, pT_hi), (w_lo, pT_hi), (w_hi, pT_lo))):
                        for h in range(2):
                            last = pe.matmul(acc[n % 2][:, h], w[:, p.mod(RING), at], x[:, k, HALF * h:HALF * h + HALF],
                                             start=(k == 0 and s == 0), stop=(k == 1 and s == 2))
                last.then_inc(w_used if i % 2 else ple_first, 1)

            def norm_sums(n):
                if n == 0:
                    pe.wait_ge(sq_cleared, 1)
                pe.wait_ge(sq_added, KB * (n + 1))
                for t in range(QB):
                    last = pe.matmul(turn[:, t:t + 1], sq_sum[:, P * t:P * t + P], ones[:, 0:1], start=True, stop=True)
                last.then_inc(sum_turned, 1)

            def norm_row(n):
                pe.wait_ge(r_ready, n + 1)
                row_matmuls(r_t, lambda t: P).then_inc(row_ready, 1)

            def behind_norm(half, n, pj, pc):
                project_ple(half, 0)
                norm_sums(n)
                project_ple(half, 1)
                norm_row(n)
                project_ple(half, 2)
                project_ple(half, 3)
                two_tasks(pj, pc, h_split, half * KB)

            def late_norm(n, pj, pc):
                project(Count(pj + 2), Count(pc + 4), act_hi, act_lo)
                steps = k_steps(Count(pj + 3), Count(pc + 6), act_hi, act_lo)
                for _ in range(KB // 2):
                    next(steps)
                norm_sums(n)
                for _ in steps:
                    pass
                norm_row(n)

            def up_blocks(first, n, group):
                with pe.Fori(0, n // 2) as it:
                    for j in range(2):
                        project(group * (2 * KB) + Count(PJ_FF + first + j, [(it, 2)]),
                                group * (4 * KB) + Count(PC_FF + 2 * (first + j), [(it, RING)]), act_hi, act_lo)

            def down_blocks(group):
                with pe.Fori(0, KB // 2) as it:
                    for j in range(2):
                        project(group * (2 * KB) + Count(PJ_FF + KB + j, [(it, 2)]),
                                group * (4 * KB) + Count(PC_FF + 2 * KB + 2 * j, [(it, RING)]), mid_hi, mid_lo,
                                input_ready=lambda k: at_least(pe, up_split, group * KB + (k + 1)))

            behind_norm(0, N_POST, PJ_FF, PC_FF)
            late_norm(N_FPRE, PJ_FF, PC_FF)
            up_blocks(4, KB - 4, Count(0))
            down_blocks(Count(0))
            with pe.Fori(1, FG) as g:
                up_blocks(0, KB, Count(0, [(g, 1)]))
                down_blocks(Count(0, [(g, 1)]))
            behind_norm(1, N_FPOST, PJ_PG, PC_PG)
            late_norm(N_PLE, PJ_PG, PC_PG)

            def turn_y(m):
                pe.wait_ge(y_ready, m + 1)
                if m >= 2:
                    pe.wait_ge(y_copied, m - 1)
                for t in range(QB):
                    n = rows(t)
                    last = pe.transpose(pair[m % 2][0:n, P * t:P * t + P], y_f[m][:, P * t:P * t + n], ident[:, :])
                last.then_inc(y_turned, 1)

            for m in range(4, KB):
                project(Count(PJ_PG + m), Count(PC_PG + 2 * m), act_hi, act_lo)
                for i in Y_AFTER[m]:
                    turn_y(i)


def kernel(**inputs):
    import numpy as np
    import concourse.bacc as bacc
    from concourse.bass_utils import run_bass_kernel_spmd

    names = ["x_prompt", "x_sample", "cache_a_k", "cache_a_v", "cache_b_k", "cache_b_v", "p_prompt", "p_sample",
             "w_in", "rel_bias", "diff_lambda", "diff_subln", "w_gate", "w_branch_a", "w_branch_b", "w_out",
             "g_mix_pre", "g_mix_post", "g_ffn_pre", "g_ffn_post", "w_up", "w_down", "w_ple", "g_ple", "w_ple_gate"]
    arrays = {n: np.ascontiguousarray(inputs[n]) for n in names}
    arrays["rel_bias"] = np.ascontiguousarray(arrays["rel_bias"][:, :, ::-1])
    d, bsz, s, m = 1, 1, arrays["x_prompt"].shape[1], arrays["x_sample"].shape[1]
    ha, hd = arrays["cache_a_k"].shape[3:]
    hb = arrays["cache_b_k"].shape[3]
    keep = min(8 * 64, s)
    shapes = [arrays["x_prompt"].shape, arrays["x_sample"].shape,
              (d, bsz, keep, ha, hd), (d, bsz, keep, ha, hd), (d, bsz, s, hb, 2, hd), (d, bsz, s, hb, 2 * hd),
              (d, bsz, m, ha, hd), (d, bsz, m, ha, hd), (d, bsz, m, hb, 2, hd), (d, bsz, m, hb, 2 * hd)]
    nc = bacc.Bacc("TRN2", target_bir_lowering=False, num_devices=1)
    ins = [nc.dram_tensor(n, arrays[n].shape, mybir.dt.from_np(arrays[n].dtype), kind="ExternalInput").ap() for n in names]
    outs = [nc.dram_tensor(f"out_{i}", sh, F32, kind="ExternalOutput").ap() for i, sh in enumerate(shapes)]
    encoder_layer(nc, *ins, *outs)
    r = run_bass_kernel_spmd(nc, [arrays], core_ids=[0])
    return tuple(r.results[0][f"out_{i}"] for i in range(len(shapes)))
```
